# Optimizing a Trainium2 kernel written in Bass

```python
import jax, jax.numpy as jnp
from jax import lax
import numpy as np

D_MODEL = 1024
BATCH = 1
SEQ = 2048
DEPTH = 1
DEC_BATCH = 8
DEC_SEQ = 4
PAST_LEN = 2048
PAGE_SIZE = 128

PLE_DIM = 256
N_HEADS_SB = 8
HEAD_DIM_SB = 64
D_SB = N_HEADS_SB * HEAD_DIM_SB
N_GROUPS_MLP = 8
GROUP_DIM_MLP = 64
D_MLP = N_GROUPS_MLP * GROUP_DIM_MLP
D_MIX = D_SB + D_MLP
D_IN = 3 * D_SB + 2 * D_MLP
CHUNK = 128
Q_BLOCK = 128
D_FF = 2816
CONV_W = 3
EPS = 1e-6
SB_BIAS_INIT = -7.0

kernel_name = "hymba_stickbreak_chunkmlp_convffn_ple_step"

def rmsnorm(x, g):
    xf = x.astype(jnp.float32)
    xf = xf * lax.rsqrt(jnp.mean(xf * xf, axis=-1, keepdims=True) + EPS)
    return (xf * g.astype(jnp.float32)).astype(x.dtype)

def split_projection(hn, w_in):
    z = hn @ w_in
    q, k, v, u, vm = jnp.split(z, [D_SB, 2 * D_SB, 3 * D_SB, 3 * D_SB + D_MLP], axis=-1)
    heads = lambda t: t.reshape(t.shape[:-1] + (N_HEADS_SB, HEAD_DIM_SB))
    return heads(q), heads(k), heads(v), jax.nn.gelu(u), jax.nn.gelu(vm)

def stick_breaking(q, k, v, sb_bias, q_pos, k_pos):
    z = jnp.einsum('bqhd,bkhd->bhqk', q.astype(jnp.float32), k.astype(jnp.float32)) * (HEAD_DIM_SB ** -0.5)
    z = z + sb_bias.astype(jnp.float32)[None, :, None, None]
    mask = k_pos[None, :] < q_pos[:, None]
    log_1mb = jnp.where(mask, jax.nn.log_sigmoid(-z), 0.0)
    suffix = lax.cumsum(log_1mb, axis=3, reverse=True) - log_1mb
    a = jnp.where(mask, jnp.exp(jax.nn.log_sigmoid(z) + suffix), 0.0)
    o = jnp.einsum('bhqk,bkhd->bqhd', a, v.astype(jnp.float32))
    return o.astype(v.dtype)

def sb_prompt(q, k, v, sb_bias):
    b, s, h, d = q.shape
    nb = s // Q_BLOCK
    qb = jnp.moveaxis(q.reshape(b, nb, Q_BLOCK, h, d), 1, 0)
    k_pos = jnp.arange(s, dtype=jnp.int32)

    def block(args):
        q_blk, i = args
        q_pos = i * Q_BLOCK + jnp.arange(Q_BLOCK, dtype=jnp.int32)
        return stick_breaking(q_blk, k, v, sb_bias, q_pos, k_pos)

    ob = lax.map(block, (qb, jnp.arange(nb, dtype=jnp.int32)))
    return jnp.moveaxis(ob, 0, 1).reshape(b, s, h * d)

def causal_spatial_weights(w_s):
    return w_s * jnp.tril(jnp.ones((CHUNK, CHUNK), w_s.dtype))

def chunk_mlp_prompt(u, vm, w_s, b_s):
    b, s, _ = vm.shape
    vc = vm.reshape(b, s // CHUNK, CHUNK, N_GROUPS_MLP, GROUP_DIM_MLP)
    mixed = jnp.einsum('gts,bcsgd->bctgd', causal_spatial_weights(w_s), vc)
    mixed = mixed + jnp.swapaxes(b_s, 0, 1)[:, :, None]
    return u * mixed.reshape(b, s, D_MLP)

def chunk_mlp_sample(u, vm, w_s, b_s):
    b, t, _ = vm.shape
    vc = vm.reshape(b, t, N_GROUPS_MLP, GROUP_DIM_MLP)
    w = causal_spatial_weights(w_s)[:, :t, :t]
    mixed = jnp.einsum('gts,bsgd->btgd', w, vc) + jnp.swapaxes(b_s[:, :t], 0, 1)[:, :, None]
    return u * mixed.reshape(b, t, D_MLP)

def mix_merge(o_sb, o_mlp, gn_sb, gn_mlp, w_out):
    return jnp.concatenate([rmsnorm(o_sb, gn_sb), rmsnorm(o_mlp, gn_mlp)], axis=-1) @ w_out

def conv_ffn(hn, prefix, w_up, conv_w, conv_b, w_down):
    gate, up = jnp.split(hn @ w_up, 2, axis=-1)
    t = gate.shape[1]
    gp = jnp.concatenate([prefix.astype(gate.dtype), gate], axis=1)
    conv = conv_b
    for j in range(CONV_W):
        conv = conv + conv_w[j] * gp[:, j:j + t]
    y = (jax.nn.gelu(conv) * up) @ w_down
    return y, gp[:, gp.shape[1] - (CONV_W - 1):]

def per_layer_embedding(h, p_i, g, w_gate, w_proj):
    gate = jax.nn.sigmoid(rmsnorm(h, g) @ w_gate)
    return h + gate * (p_i @ w_proj)

def setup_inputs(seed: int = 0) -> dict:
    key = jax.random.key(seed)
    ks = jax.random.split(key, 28)
    f32 = jnp.float32
    nrm = lambda k, shape, scale: jax.random.normal(k, shape, f32) * scale
    n_pages = PAST_LEN // PAGE_SIZE
    n_used = DEC_BATCH * n_pages
    n_phys = n_used + n_used // 4
    page_table = jax.random.permutation(ks[0], n_phys)[:n_used].reshape(DEC_BATCH, n_pages).astype(jnp.int32)
    return {
        "x_prompt": nrm(ks[1], (BATCH, SEQ, D_MODEL), 1.0),
        "x_sample": nrm(ks[2], (DEC_BATCH, DEC_SEQ, D_MODEL), 1.0),
        "cache_k": nrm(ks[3], (DEPTH, n_phys, PAGE_SIZE, N_HEADS_SB, HEAD_DIM_SB), 1.0),
        "cache_v": nrm(ks[4], (DEPTH, n_phys, PAGE_SIZE, N_HEADS_SB, HEAD_DIM_SB), 1.0),
        "state_conv": nrm(ks[5], (DEPTH, DEC_BATCH, CONV_W - 1, D_FF), 1.0),
        "page_table": page_table,
        "p_prompt": nrm(ks[6], (DEPTH, BATCH, SEQ, PLE_DIM), 1.0),
        "p_sample": nrm(ks[7], (DEPTH, DEC_BATCH, DEC_SEQ, PLE_DIM), 1.0),
        "norm_mix_g": 1.0 + nrm(ks[8], (DEPTH, D_MODEL), 0.1),
        "w_in": nrm(ks[9], (DEPTH, D_MODEL, D_IN), D_MODEL ** -0.5),
        "sb_bias": SB_BIAS_INIT + nrm(ks[24], (DEPTH, N_HEADS_SB), 0.5),
        "gn_sb": 1.0 + nrm(ks[10], (DEPTH, D_SB), 0.1),
        "gn_mlp": 1.0 + nrm(ks[11], (DEPTH, D_MLP), 0.1),
        "w_spatial": nrm(ks[12], (DEPTH, N_GROUPS_MLP, CHUNK, CHUNK), CHUNK ** -0.5),
        "b_spatial": 1.0 + nrm(ks[13], (DEPTH, N_GROUPS_MLP, CHUNK), 0.1),
        "w_out": nrm(ks[14], (DEPTH, D_MIX, D_MODEL), D_MIX ** -0.5),
        "norm_ffn_g": 1.0 + nrm(ks[15], (DEPTH, D_MODEL), 0.1),
        "w_up": nrm(ks[16], (DEPTH, D_MODEL, 2 * D_FF), D_MODEL ** -0.5),
        "conv_w": nrm(ks[17], (DEPTH, CONV_W, D_FF), CONV_W ** -0.5),
        "conv_b": nrm(ks[18], (DEPTH, D_FF), 0.02),
        "w_down": nrm(ks[19], (DEPTH, D_FF, D_MODEL), D_FF ** -0.5),
        "norm_ple_g": 1.0 + nrm(ks[20], (DEPTH, D_MODEL), 0.1),
        "w_ple_gate": nrm(ks[21], (DEPTH, D_MODEL, D_MODEL), D_MODEL ** -0.5),
        "w_ple_proj": nrm(ks[22], (DEPTH, PLE_DIM, D_MODEL), PLE_DIM ** -0.5),
        "final_norm_g": 1.0 + nrm(ks[23], (D_MODEL,), 0.1),
    }

def reference(x_prompt, x_sample, cache_k, cache_v, state_conv, page_table, p_prompt, p_sample,
              norm_mix_g, w_in, sb_bias, gn_sb, gn_mlp, w_spatial, b_spatial, w_out,
              norm_ffn_g, w_up, conv_w, conv_b, w_down,
              norm_ple_g, w_ple_gate, w_ple_proj, final_norm_g):
    n_pages = page_table.shape[1]
    past = n_pages * PAGE_SIZE
    bp = x_prompt.shape[0]
    dec_b, dec_t = x_sample.shape[0], x_sample.shape[1]
    q_pos_s = past + jnp.arange(dec_t, dtype=jnp.int32)
    k_pos_s = jnp.arange(past + dec_t, dtype=jnp.int32)
    hp, hs = x_prompt, x_sample
    kp_l, vp_l, ks_l, vs_l, cp_l, cs_l, ms_l = [], [], [], [], [], [], []
    for i in range(DEPTH):
        q, k, v, u, vm = split_projection(rmsnorm(hp, norm_mix_g[i]), w_in[i])
        o_sb = sb_prompt(q, k, v, sb_bias[i])
        o_mlp = chunk_mlp_prompt(u, vm, w_spatial[i], b_spatial[i])
        hp = hp + mix_merge(o_sb, o_mlp, gn_sb[i], gn_mlp[i], w_out[i])
        zero_prefix = jnp.zeros((bp, CONV_W - 1, D_FF), hp.dtype)
        y, conv_p = conv_ffn(rmsnorm(hp, norm_ffn_g[i]), zero_prefix, w_up[i], conv_w[i], conv_b[i], w_down[i])
        hp = hp + y
        hp = per_layer_embedding(hp, p_prompt[i], norm_ple_g[i], w_ple_gate[i], w_ple_proj[i])
        kp_l.append(k); vp_l.append(v); cp_l.append(conv_p)

        q, k, v, u, vm = split_projection(rmsnorm(hs, norm_mix_g[i]), w_in[i])
        k_past = cache_k[i][page_table].reshape(dec_b, past, N_HEADS_SB, HEAD_DIM_SB)
        v_past = cache_v[i][page_table].reshape(dec_b, past, N_HEADS_SB, HEAD_DIM_SB)
        k_all = jnp.concatenate([k_past, k.astype(k_past.dtype)], axis=1)
        v_all = jnp.concatenate([v_past, v.astype(v_past.dtype)], axis=1)
        o_sb = stick_breaking(q, k_all, v_all, sb_bias[i], q_pos_s, k_pos_s).reshape(dec_b, dec_t, D_SB)
        o_mlp = chunk_mlp_sample(u, vm, w_spatial[i], b_spatial[i])
        hs = hs + mix_merge(o_sb.astype(hs.dtype), o_mlp, gn_sb[i], gn_mlp[i], w_out[i])
        y, conv_s = conv_ffn(rmsnorm(hs, norm_ffn_g[i]), state_conv[i], w_up[i], conv_w[i], conv_b[i], w_down[i])
        hs = hs + y
        hs = per_layer_embedding(hs, p_sample[i], norm_ple_g[i], w_ple_gate[i], w_ple_proj[i])
        ks_l.append(k); vs_l.append(v); cs_l.append(conv_s); ms_l.append(vm)

    y_prompt = rmsnorm(hp, final_norm_g)
    y_sample = rmsnorm(hs, final_norm_g)
    k_prompt = jnp.stack(kp_l)
    v_prompt = jnp.stack(vp_l)
    k_sample = jnp.stack(ks_l)
    v_sample = jnp.stack(vs_l)
    conv_prompt = jnp.stack(cp_l)
    conv_sample = jnp.stack(cs_l)
    mlp_v_sample = jnp.stack(ms_l)
    return (y_prompt, y_sample, k_prompt, v_prompt, k_sample, v_sample, conv_prompt, conv_sample, mlp_v_sample)


_drawn_inputs = setup_inputs


def setup_inputs(seed=0):
    import zlib

    import numpy as np

    out = dict(_drawn_inputs(seed))
    spreads = {}
    factors = {'conv_b': 7.062, 'norm_ple_g': 4.627}
    for name, (base, spread) in spreads.items():
        noise = np.random.default_rng([zlib.crc32(name.encode()), seed]).standard_normal(out[name].shape)
        drawn = base * np.exp(spread * noise) if base else spread * noise
        out[name] = __import__('jax').numpy.asarray(drawn.astype(out[name].dtype))
    for name, factor in factors.items():
        out[name] = (out[name] * factor).astype(out[name].dtype)
    return out
```

```python
from contextlib import ExitStack

import concourse.bass as bass
from concourse import mybir

F32 = mybir.dt.float32
F32R = mybir.dt.float32r
I32 = mybir.dt.int32
ALU = mybir.AluOpType
ACT = mybir.ActivationFunctionType
AX = mybir.AxisListType

P = 128
BANK = 512
EPS = 1e-6
CHUNK_COLS = 512


class Alloc:

    def __init__(self, nc, ctx, phase):
        self.nc, self.ctx, self.phase, self.sems = nc, ctx, phase, []

    def sb(self, name, shape, dt=F32):
        return self.ctx.enter_context(self.nc.sbuf_tensor(f"{self.phase}_{name}", shape, dt))

    def bank(self, name, shape=(P, BANK)):
        return self.ctx.enter_context(self.nc.psum_tensor(f"{self.phase}_{name}", list(shape), F32))

    def sem(self, name):
        self.sems.append(self.nc.alloc_semaphore(name=f"{self.phase}_{name}"))
        return self.sems[-1]

    def free_sems(self):
        with self.nc.Block() as block:

            @block.gpsimd
            def _(pool):
                self.nc.clear_and_free_semaphores(self.sems)


def f32(ap):
    return ap.bitcast(F32)


def wait_apart(eng, sem, value):
    eng.wait_ge(sem, 1)
    eng.wait_ge(sem, value)


def split_product(nc, out, stat_hi, stat_lo, mov_hi, mov_lo, first, last):
    nc.tensor.matmul(out, stat_hi, mov_hi, start=first, stop=False)
    nc.tensor.matmul(out, stat_hi, mov_lo, start=False, stop=False)
    return nc.tensor.matmul(out, stat_lo, mov_hi, start=False, stop=last)


def constants(nc, keep, T):
    with ExitStack() as ctx:
        m = Alloc(nc, ctx, "const")
        rows = m.sb("rows", [P, P])
        ps = m.bank("ps")
        made, loaded, turned, copied = m.sem("made"), m.sem("loaded"), m.sem("turned"), m.sem("copied")
        with nc.Block() as block:

            @block.sync
            def _(sp):
                at = 0
                for name in ("norm_mix_g", "gn_sb", "gn_mlp", "norm_ffn_g", "norm_ple_g", "final_norm_g", "conv_w", "conv_b"):
                    v = T[name]
                    v = v if name == "final_norm_g" else v[0]
                    v = v.rearrange("j (k p) -> (j k) p", p=P) if name == "conv_w" else v.rearrange("(k p) -> k p", p=P)
                    n = v.shape[0]
                    sp.dma_start(rows[at:at + n, :], v).then_inc(loaded, 16)
                    at += n
                assert at == P
                sp.dma_start(keep["page_table"][0:1, :], T["page_table"].rearrange("b n -> (b n)").rearrange("(a n) -> a n", a=1)).then_inc(loaded, 16)
                sp.dma_start(keep["sb_bias"][:, :], T["sb_bias"][0:1, :].to_broadcast([P, 8])).then_inc(loaded, 16)
                sp.wait_ge(loaded, 16 * 10)

            @block.gpsimd
            def _(pool):
                nc.gpsimd.memset(keep["ident"][:, :], 1.0).then_inc(made, 1)
                pool.wait_ge(made, 1)
                nc.gpsimd.affine_select(out=keep["ident"][:, :], in_=keep["ident"][:, :], pattern=[[-1, P]],
                                        compare_op=ALU.is_equal, fill=0.0, base=0, channel_multiplier=1).then_inc(made, 1)
                nc.gpsimd.memset(keep["mean1024"][:, :], 1.0 / 1024)
                nc.gpsimd.memset(keep["mean512"][:, :], 1.0 / 512)
                nc.gpsimd.memset(keep["eps"][:, :], EPS)

            @block.tensor
            def _(pe):
                pe.wait_ge(loaded, 16 * 10)
                pe.wait_ge(made, 2)
                nc.tensor.transpose(ps[:, 0:P], rows[:, :], keep["ident"][:, :]).then_inc(turned, 1)

            @block.vector
            def _(dve):
                dve.wait_ge(turned, 1)
                nc.vector.tensor_copy(keep["cols"][:, :], ps[:, 0:P]).then_inc(copied, 1)


G_MIX, G_OUT, G_FFN, G_PLE, G_FIN, CONV_W0, CONV_B0 = 0, 8, 16, 24, 32, 40, 106


def project_mlp(nc, keep, T, D):
    NT = 17
    with ExitStack() as ctx:
        m = Alloc(nc, ctx, "pa")
        w_hi = m.sb("w_hi", [P, 8, 3 * BANK], F32R)
        w_lo = m.sb("w_lo", [P, 8, 3 * BANK], F32R)
        w_raw = [m.sb(f"w_raw{n}", [P, 4, BANK]) for n in range(2)]
        x_raw = [m.sb(f"x_raw{n}", [P, 1024]) for n in range(2)]
        p_raw = [m.sb(f"p_raw{n}", [P, 256]) for n in range(2)]
        xT = [m.sb(f"xT{n}", [P, 8, P]) for n in range(2)]
        x_hi = [m.sb(f"x_hi{n}", [P, 8, P], F32R) for n in range(2)]
        x_lo = [m.sb(f"x_lo{n}", [P, 8, P], F32R) for n in range(2)]
        pT = [m.sb(f"pT{n}", [P, 2, P]) for n in range(2)]
        vm = [m.sb(f"vm{n}", [P, BANK]) for n in range(2)]
        u = [m.sb(f"u{n}", [P, BANK]) for n in range(2)]
        v = [m.sb(f"v{n}", [P, BANK]) for n in range(2)]
        o = [m.sb(f"o{n}", [P, BANK]) for n in range(2)]
        oT = [m.sb(f"oT{n}", [P, 4, P]) for n in range(2)]
        ws = m.sb("ws", [P, 8, P])
        wsT = m.sb("wsT", [P, 8, P])
        wsT32 = m.sb("wsT32", [32, 8, 32])
        bs_raw = m.sb("bs_raw", [8, P])
        bs = m.sb("bs", [P, 8])
        bs32 = m.sb("bs32", [32, 8])
        x_sq = [m.sb(f"x_sq{n}", [P, 2]) for n in range(2)]
        x_ms = [m.sb(f"x_ms{n}", [P, 1]) for n in range(2)]
        x_rms = [m.sb(f"x_rms{n}", [P, 1]) for n in range(2)]
        x_rs = [m.sb(f"x_rs{n}", [P, 1]) for n in range(2)]
        o_sq = [m.sb(f"o_sq{n}", [P, 1]) for n in range(2)]
        o_rms = [m.sb(f"o_rms{n}", [P, 1]) for n in range(2)]
        o_rs = [m.sb(f"o_rs{n}", [P, 1]) for n in range(2)]
        ps_acc = [m.bank(f"ps_acc{n}") for n in range(2)]
        ps_x = m.bank("ps_x", (P, 2 * BANK))
        ps_p = m.bank("ps_p")
        ps_o = m.bank("ps_o")
        ps_mix = m.bank("ps_mix")
        ps_junk = m.bank("ps_junk")

        w_loaded = [m.sem(f"w_loaded{n}") for n in range(2)]
        w_hi_done, w_lo_done = m.sem("w_hi_done"), m.sem("w_lo_done")
        s_loaded, s_masked, s_turned, s_copied, s_zeroed, s_small = (
            m.sem(n) for n in ("s_loaded", "s_masked", "s_turned", "s_copied", "s_zeroed", "s_small"))
        x_loaded = [m.sem(f"x_loaded{n}") for n in range(2)]
        p_loaded = [m.sem(f"p_loaded{n}") for n in range(2)]
        x_turned, p_turned, acc_ready, mixed_ready, o_turned = (
            m.sem(n) for n in ("x_turned", "p_turned", "acc_ready", "mixed_ready", "o_turned"))
        sq_done, rms_done, xT_ready, vm_ready, u_ready, v_ready, osq_done = (
            m.sem(n) for n in ("sq_done", "rms_done", "xT_ready", "vm_ready", "u_ready", "v_ready", "osq_done"))
        hi_ready, lo_ready, pT_ready, ms_done, rs_ready, gated, o_rs_done, o_ready, oT_ready = (
            m.sem(n) for n in ("hi_ready", "lo_ready", "pT_ready", "ms_done", "rs_ready", "gated", "o_rs_done", "o_ready", "oT_ready"))
        xT_stored = [m.sem(f"xT_stored{n}") for n in range(2)]
        pT_stored = [m.sem(f"pT_stored{n}") for n in range(2)]
        oT_stored = [m.sem(f"oT_stored{n}") for n in range(2)]
        v_stored = [m.sem(f"v_stored{n}") for n in range(2)]
        vm_stored = m.sem("vm_stored")

        x_src, p_src = T["x_prompt"][0], T["p_prompt"][0, 0]
        xs_src, ps_src = T["x_sample"].rearrange("b t d -> (b t) d"), T["p_sample"][0].rearrange("b t d -> (b t) d")
        XT, PT, MIXT = (D[n].rearrange("(k p) t -> p k t", p=P) for n in ("XT", "PT", "MIXT"))
        v_out = T["v_prompt"][0, 0].rearrange("t h d -> t (h d)")
        vs_out = T["v_sample"][0].rearrange("b t h d -> (b t) (h d)")
        w_in = T["w_in"][0].rearrange("(k p) n -> p k n", p=P)
        COLS = (2048, 1536, 1024)

        with nc.Block() as block:

            @block.sync
            def _(sp):
                def load(at, s):
                    rows = P if at is not None else 32
                    a = x_src[bass.ds(at, P), :] if at is not None else xs_src
                    b = p_src[bass.ds(at, P), :] if at is not None else ps_src
                    sp.dma_start(x_raw[s][0:rows, :], a).then_inc(x_loaded[s], 16)
                    sp.dma_start(p_raw[s][0:rows, :], b).then_inc(p_loaded[s], 16)

                def store_turned(count, at, s, rows=P):
                    at = bass.ds(at, rows)
                    wait_apart(sp, xT_ready, count)
                    sp.dma_start(XT[:, :, at], xT[s][:, :, 0:rows]).then_inc(xT_stored[s], 16)
                    sp.wait_ge(pT_ready, count)
                    sp.dma_start(PT[:, :, at], pT[s][:, :, 0:rows]).then_inc(pT_stored[s], 16)

                def store_o(count, at, s, rows=P):
                    sp.wait_ge(oT_ready, count)
                    sp.dma_start(MIXT[:, 4:8, bass.ds(at, rows)], oT[s][:, :, 0:rows]).then_inc(oT_stored[s], 16)

                load(0, 0)
                for c in range(3):
                    for half in range(2):
                        n = 2 * c + half
                        if n >= 2:
                            sp.wait_ge(w_lo_done, 4 * (n - 1))
                        sp.dma_start(w_raw[n % 2][:, :, :],
                                     w_in[:, 4 * half:4 * half + 4, COLS[c]:COLS[c] + BANK]).then_inc(w_loaded[n % 2], 16)
                    if c == 0:
                        sp.dma_start(ws[:, :, :], T["w_spatial"][0].rearrange("g t s -> t g s")).then_inc(s_loaded, 16)
                        sp.dma_start(bs_raw[:, :], T["b_spatial"][0]).then_inc(s_loaded, 16)
                        load(P, 1)
                store_turned(1, 0, 0)
                sp.wait_ge(s_copied, 3)
                sp.wait_ge(s_zeroed, 1)
                for b in range(8):
                    sp.dma_start(wsT32[4 * b:4 * b + 4, :, 4 * b:4 * b + 4], wsT[0:4, :, 0:4]).then_inc(s_small, 16)
                    sp.dma_start(bs32[4 * b:4 * b + 4, :], bs[0:4, :]).then_inc(s_small, 16)
                with sp.Fori(0, 7) as i:
                    for s in range(2):
                        t = 2 * i + s
                        at, at1, at2 = t * P, (t + 1) * P, (t + 2) * P
                        one, two, squares = sp.snap(t + 1), sp.snap(t + 2), sp.snap(2 * t + 2)
                        sp.wait_ge(x_turned, one)
                        sp.wait_ge(p_turned, one)
                        sp.wait_ge(sq_done, squares)
                        load(at2, s)
                        store_turned(two, at1, 1 - s)
                        store_o(one, at, s)
                sp.wait_ge(x_turned, 15)
                sp.wait_ge(p_turned, 15)
                sp.wait_ge(sq_done, 30)
                load(None, 0)
                store_turned(16, 15 * P, 1)
                store_o(15, 14 * P, 0)
                store_turned(17, 16 * P, 0, 32)
                store_o(16, 15 * P, 1)
                sp.wait_ge(vm_ready, 17)
                sp.dma_start(T["mlp_v_sample"][0].rearrange("b t d -> (b t) d"), vm[0][0:32, :]).then_inc(vm_stored, 16)
                store_o(17, 16 * P, 0, 32)
                sp.wait_ge(vm_stored, 16)
                for sems in (xT_stored, pT_stored, oT_stored):
                    sp.wait_ge(sems[0], 16 * 9)
                    sp.wait_ge(sems[1], 16 * 8)
                sp.wait_ge(s_small, 16 * 16)

            @block.gpsimd
            def _(pool):
                nc.gpsimd.memset(wsT32[:, :, :], 0.0).then_inc(s_zeroed, 1)
                pool.wait_ge(s_loaded, 32)
                nc.gpsimd.affine_select(out=ws[:, :, :], in_=ws[:, :, :], pattern=[[0, 8], [-1, P]], compare_op=ALU.is_ge,
                                        fill=0.0, base=0, channel_multiplier=1).then_inc(s_masked, 1)

            @block.tensor
            def _(pe):
                def turn_x(s, loads):
                    pe.wait_ge(x_loaded[s], 16 * loads)
                    for k in range(8):
                        last = nc.tensor.transpose(ps_x[:, k * P:(k + 1) * P], x_raw[s][:, k * P:(k + 1) * P], keep["ident"][:, :])
                    last.then_inc(x_turned, 1)
                    pe.wait_ge(p_loaded[s], 16 * loads)
                    for k in range(2):
                        last = nc.tensor.transpose(ps_p[:, k * P:(k + 1) * P], p_raw[s][:, k * P:(k + 1) * P], keep["ident"][:, :])
                    last.then_inc(p_turned, 1)

                def project(t, s, c, tile0=False):
                    for k in range(8):
                        if tile0 and k % 4 == 0:
                            pe.wait_ge(w_lo_done, 8 * c + k + 4)
                        last = split_product(nc, ps_acc[(3 * s + c) % 2][:, :], x_hi[s][:, k, :], x_lo[s][:, k, :],
                                             w_hi[:, k, c * BANK:(c + 1) * BANK], w_lo[:, k, c * BANK:(c + 1) * BANK],
                                             k == 0, k == 7)
                    last.then_inc(acc_ready, 1)

                def tile(t, s, next_loads, rows=P, first=False):
                    pe.wait_ge(lo_ready, t + 1)
                    pe.wait_ge(u_ready, t + 1)
                    project(t, s, 0, first)
                    if next_loads is not None:
                        pe.wait_ge(xT_ready, t + 1)
                        pe.wait_ge(pT_ready, t + 1)
                        turn_x(1 - s, next_loads)
                    if first:
                        pe.wait_ge(s_copied, 3)
                    pe.wait_ge(v_ready, t + 1)
                    project(t, s, 1, first)
                    pe.wait_ge(vm_ready, t + 1)
                    if not first:
                        pe.wait_ge(gated, 2 * t)
                    w = wsT if rows == P else wsT32
                    if rows != P:
                        pe.wait_ge(s_small, 16 * 16)
                    for g in range(8):
                        last = nc.tensor.matmul(ps_mix[0:rows, g * 64:g * 64 + 64], w[0:rows, g, 0:rows],
                                                vm[s][0:rows, g * 64:g * 64 + 64], start=True, stop=True)
                    last.then_inc(mixed_ready, 1)
                    project(t, s, 2, first)
                    pe.wait_ge(o_ready, t + 1)
                    if not first:
                        pe.wait_ge(oT_ready, t + 0)
                    for k in range(4):
                        last = nc.tensor.transpose(ps_o[:, k * P:k * P + rows], o[s][0:rows, k * P:(k + 1) * P],
                                                   keep["ident"][0:rows, 0:rows])
                    last.then_inc(o_turned, 1)

                turn_x(0, 1)
                pe.wait_ge(s_masked, 1)
                for half in range(2):
                    for g in range(4):
                        last = nc.tensor.transpose((ps_mix, ps_o)[half][:, g * P:(g + 1) * P], ws[:, 4 * half + g, :], keep["ident"][:, :])
                    last.then_inc(s_turned, 1)
                nc.tensor.transpose(ps_acc[1][:, 0:8], bs_raw[:, :], keep["ident"][0:8, 0:8]).then_inc(s_turned, 1)
                tile(0, 0, 1, first=True)
                tile(1, 1, 2)
                with pe.Fori(1, 7) as i:
                    tile(2 * i, 0, i + 1)
                    tile(2 * i + 1, 1, i + 2)
                tile(14, 0, 8)
                tile(15, 1, 9)
                tile(16, 0, None, 32)

            @block.scalar
            def _(act):
                def prepare(t, s, loads, first=False):
                    act.wait_ge(x_loaded[s], 16 * loads)
                    for half in range(2):
                        if not first or half:
                            act.wait_ge(sq_done, 2 * t + half)
                        nc.scalar.activation(ps_junk[:, :], x_raw[s][:, half * BANK:(half + 1) * BANK], ACT.Square,
                                             accum_out=x_sq[s][:, half:half + 1]).then_inc(sq_done, 1)
                    act.wait_ge(x_turned, t + 1)
                    if not (isinstance(loads, int) and loads == 1):
                        act.wait_ge(xT_stored[s], 16 * (loads - 1))
                    nc.scalar.activation(xT[s][:, :, :].rearrange("p k t -> p (k t)"), ps_x[:, :], ACT.Copy).then_inc(xT_ready, 1)

                def root_x(t, s):
                    act.wait_ge(ms_done, t + 1)
                    nc.scalar.activation(x_rms[s][:, :], x_ms[s][:, :], ACT.Sqrt, bias=keep["eps"][:, :], scale=1.0 / 1024)\
                        .then_inc(rms_done, 1)

                def tile(t, s, next_loads, v_stores, rows=P):
                    scale = x_rs[s][:, :]
                    at = t * P if isinstance(t, int) else act.snap(t * P)
                    act.wait_ge(rs_ready, t + 1)
                    act.wait_ge(acc_ready, 3 * t + 1)
                    nc.scalar.activation(vm[s][:, :], ps_acc[(3 * s) % 2][:, :], ACT.Gelu_apprx_tanh, scale=scale).then_inc(vm_ready, 1)
                    if next_loads is not None:
                        prepare(t + 1, 1 - s, next_loads)
                    act.wait_ge(acc_ready, 3 * t + 2)
                    nc.scalar.activation(u[s][:, :], ps_acc[(3 * s + 1) % 2][:, :], ACT.Gelu_apprx_tanh, scale=scale).then_inc(u_ready, 1)
                    act.wait_ge(gated, 2 * t + 2)
                    nc.scalar.activation(ps_junk[0:rows, :], o[s][0:rows, :], ACT.Square, accum_out=o_sq[s][0:rows, :]).then_inc(osq_done, 1)
                    act.wait_ge(osq_done, t + 1)
                    nc.scalar.activation(o_rms[s][0:rows, :], o_sq[s][0:rows, :], ACT.Sqrt, bias=keep["eps"][0:rows, :],
                                         scale=1.0 / 512).then_inc(rms_done, 1)
                    if next_loads is not None:
                        root_x(t + 1, 1 - s)
                    act.wait_ge(acc_ready, 3 * t + 3)
                    if v_stores is not None:
                        act.wait_ge(v_stored[s], 16 * v_stores)
                    nc.scalar.activation(v[s][:, :], ps_acc[(3 * s + 2) % 2][:, :], ACT.Copy, scale=scale).then_inc(v_ready, 1)
                    act.wait_ge(v_ready, t + 2)
                    dst = v_out[bass.ds(at, P), :] if rows == P else vs_out
                    act.dma_start(dst, v[s][0:rows, :]).then_inc(v_stored[s], 16)

                act.sem_inc(u_ready, 1)
                act.sem_inc(v_ready, 1)
                prepare(0, 0, 1, first=True)
                root_x(0, 0)
                for c in range(3):
                    for k in range(8):
                        n = 2 * c + k // 4
                        if k % 4 == 0:
                            act.wait_ge(w_loaded[n % 2], 16 * (n // 2 + 1))
                        nc.scalar.activation(w_hi[:, k, c * BANK:(c + 1) * BANK], w_raw[n % 2][:, k % 4, :], ACT.Copy,
                                             scale=keep["cols"][:, G_MIX + k:G_MIX + k + 1]).then_inc(w_hi_done, 1)
                tile(0, 0, 1, None)
                tile(1, 1, 2, None)
                with act.Fori(1, 7) as i:
                    tile(2 * i, 0, i + 1, i)
                    tile(2 * i + 1, 1, i + 2, i)
                tile(14, 0, 8, 7)
                tile(15, 1, 9, 7)
                tile(16, 0, None, 8, 32)
                act.wait_ge(v_stored[0], 16 * 9)
                act.wait_ge(v_stored[1], 16 * 8)

            @block.vector
            def _(dve):
                def mean_square(t, s):
                    dve.wait_ge(sq_done, 2 * t + 2)
                    nc.vector.tensor_tensor(x_ms[s][:, :], x_sq[s][:, 0:1], x_sq[s][:, 1:2], ALU.add).then_inc(ms_done, 1)

                def invert_x(t, s):
                    nc.vector.reciprocal(x_rs[s][:, :], x_rms[s][:, :]).then_inc(rs_ready, 1)
                    dve.wait_ge(rs_ready, t + 1)
                    nc.vector.tensor_scalar(keep["rs"][:, bass.ds(t, 1)], x_rs[s][:, :], 1.0, None, ALU.mult)

                def split_x(t, s):
                    dve.wait_ge(xT_ready, t + 1)
                    nc.vector.tensor_copy(x_hi[s][:, :, :], xT[s][:, :, :]).then_inc(hi_ready, 1)
                    dve.wait_ge(hi_ready, t + 1)
                    nc.vector.tensor_tensor(x_lo[s][:, :, :], xT[s][:, :, :], f32(x_hi[s][:, :, :]), ALU.subtract).then_inc(lo_ready, 1)

                def copy_p(t, s, stores):
                    dve.wait_ge(p_turned, t + 1)
                    if stores is not None:
                        dve.wait_ge(pT_stored[s], 16 * stores)
                    nc.vector.tensor_copy(pT[s][:, :, :].rearrange("p k t -> p (k t)"), ps_p[:, 0:2 * P]).then_inc(pT_ready, 1)

                def tile(t, s, nxt, stores, stores_next, rows=P):
                    if nxt:
                        mean_square(t + 1, 1 - s)
                        split_x(t + 1, 1 - s)
                        copy_p(t + 1, 1 - s, stores_next)
                    b = bs if rows == P else bs32
                    dve.wait_ge(mixed_ready, t + 1)
                    nc.vector.tensor_tensor(
                        o[s][0:rows, :].rearrange("p (g d) -> p g d", g=8), ps_mix[0:rows, :].rearrange("p (g d) -> p g d", g=8),
                        b[0:rows, :].unsqueeze(2).to_broadcast([rows, 8, 64]), ALU.add).then_inc(gated, 1)
                    dve.wait_ge(gated, 2 * t + 1)
                    dve.wait_ge(u_ready, t + 2)
                    nc.vector.tensor_tensor(o[s][0:rows, :], o[s][0:rows, :], u[s][0:rows, :], ALU.mult).then_inc(gated, 1)
                    dve.wait_ge(rms_done, 2 * t + 2)
                    nc.vector.reciprocal(o_rs[s][0:rows, :], o_rms[s][0:rows, :]).then_inc(o_rs_done, 1)
                    dve.wait_ge(o_rs_done, t + 1)
                    nc.vector.tensor_scalar(o[s][0:rows, :], o[s][0:rows, :], o_rs[s][0:rows, :], None, ALU.mult).then_inc(o_ready, 1)
                    if nxt:
                        dve.wait_ge(rms_done, 2 * t + 3)
                        invert_x(t + 1, 1 - s)
                    dve.wait_ge(o_turned, t + 1)
                    if stores is not None:
                        dve.wait_ge(oT_stored[s], 16 * stores)
                    if rows == P:
                        nc.vector.tensor_copy(oT[s][:, :, :].rearrange("p k t -> p (k t)"), ps_o[:, :]).then_inc(oT_ready, 1)
                    else:
                        nc.vector.tensor_copy(oT[s][:, :, 0:rows], ps_o[:, :].rearrange("p (k t) -> p k t", k=4)[:, :, 0:rows])\
                            .then_inc(oT_ready, 1)

                mean_square(0, 0)
                split_x(0, 0)
                copy_p(0, 0, None)
                dve.wait_ge(rms_done, 1)
                invert_x(0, 0)
                for c in range(3):
                    for k in range(8):
                        n = 2 * c + k // 4
                        dve.wait_ge(w_hi_done, 8 * c + k + 1)
                        nc.vector.scalar_tensor_tensor(
                            w_lo[:, k, c * BANK:(c + 1) * BANK], w_raw[n % 2][:, k % 4, :], keep["cols"][:, G_MIX + k:G_MIX + k + 1],
                            f32(w_hi[:, k, c * BANK:(c + 1) * BANK]), ALU.mult, ALU.subtract).then_inc(w_lo_done, 1)
                    if c == 0:
                        dve.wait_ge(s_turned, 3)
                        nc.vector.tensor_copy(wsT[:, 0:4, :].rearrange("p g t -> p (g t)"), ps_mix[:, :]).then_inc(s_copied, 1)
                        nc.vector.tensor_copy(wsT[:, 4:8, :].rearrange("p g t -> p (g t)"), ps_o[:, :]).then_inc(s_copied, 1)
                        nc.vector.tensor_copy(bs[:, :], ps_acc[1][:, 0:8]).then_inc(s_copied, 1)
                tile(0, 0, True, None, None)
                tile(1, 1, True, None, 1)
                with dve.Fori(1, 7) as i:
                    tile(2 * i, 0, True, i, i)
                    tile(2 * i + 1, 1, True, i, i + 1)
                tile(14, 0, True, 7, 7)
                tile(15, 1, True, 7, 8)
                tile(16, 0, False, 8, None, 32)
        m.free_sems()


def project_qk(nc, keep, T, D):
    with ExitStack() as ctx:
        m = Alloc(nc, ctx, "pb")
        w_hi = m.sb("w_hi", [P, 8, 2 * BANK], F32R)
        w_lo = m.sb("w_lo", [P, 8, 2 * BANK], F32R)
        w_raw = [m.sb(f"w_raw{n}", [P, 4, BANK]) for n in range(4)]
        xT = [m.sb(f"xT{n}", [P, 8, P]) for n in range(2)]
        x_hi = [m.sb(f"x_hi{n}", [P, 8, P], F32R) for n in range(2)]
        x_lo = [m.sb(f"x_lo{n}", [P, 8, P], F32R) for n in range(2)]
        x_rs = [m.sb(f"x_rs{n}", [P, 2]) for n in range(2)]
        k = [m.sb(f"k{n}", [P, BANK]) for n in range(2)]
        q = [m.sb(f"q{n}", [P, BANK]) for n in range(2)]
        kT = [m.sb(f"kT{n}", [P, 4, P]) for n in range(2)]
        qT = [m.sb(f"qT{n}", [P, 4, P]) for n in range(2)]
        ps_k, ps_q, ps_kT, ps_qT = (m.bank(n) for n in ("ps_k", "ps_q", "ps_kT", "ps_qT"))

        w_loaded = [m.sem(f"w_loaded{n}") for n in range(4)]
        w_hi_done, w_lo_done, rs_done, hi_ready, lo_ready, k_proj, q_proj, k_ready, q_ready, k_turned, q_turned, kT_ready, qT_ready = (
            m.sem(n) for n in ("w_hi_done", "w_lo_done", "rs_done", "hi_ready", "lo_ready", "k_proj", "q_proj", "k_ready", "q_ready",
                               "k_turned", "q_turned", "kT_ready", "qT_ready"))
        x_loaded, k_stored, kT_stored, qT_stored = (
            [m.sem(f"{n}{s}") for s in range(2)] for n in ("x_loaded", "k_stored", "kT_stored", "qT_stored"))

        XT = D["XT"].rearrange("(k p) t -> p k t", p=P)
        KT, QT = (D[n].rearrange("(k p) t -> p k t", p=P) for n in ("KT", "QT"))
        k_out = T["k_prompt"][0, 0].rearrange("t h d -> t (h d)")
        ks_out = T["k_sample"][0].rearrange("b t h d -> (b t) (h d)")
        w_in = T["w_in"][0].rearrange("(k p) n -> p k n", p=P)
        COLS = (BANK, 0)

        with nc.Block() as block:

            @block.sync
            def _(sp):
                def load(at, s):
                    sp.dma_start(xT[s][:, :, :], XT[:, :, bass.ds(at, P)]).then_inc(x_loaded[s], 16)

                def store(count, at, s, which):
                    ready, src, dst, stored = (kT_ready, kT, KT, kT_stored) if which == "k" else (qT_ready, qT, QT, qT_stored)
                    wait_apart(sp, ready, count)
                    sp.dma_start(dst[:, :, bass.ds(at, P)], src[s][:, :, :]).then_inc(stored[s], 16)

                sp.dma_start(xT[0][:, :, 0:32], XT[:, :, 2048:2080]).then_inc(x_loaded[0], 16)
                sp.dma_start(xT[0][:, :, 32:P], XT[:, :, 0:P - 32]).then_inc(x_loaded[0], 16)
                for n in range(4):
                    c, half = n // 2, n % 2
                    sp.dma_start(w_raw[n][:, :, :], w_in[:, 4 * half:4 * half + 4, COLS[c]:COLS[c] + BANK]).then_inc(w_loaded[n], 16)
                load(0, 1)
                sp.wait_ge(lo_ready, 1)
                load(P, 0)
                with sp.Fori(0, 7) as i:
                    for e in range(2):
                        n, s = 2 * i + 1 + e, 1 - e
                        nxt, at2 = sp.snap(n + 1), sp.snap((n + 1) * P)
                        wait_apart(sp, lo_ready, nxt)
                        load(at2, s)
                        store(nxt, (n - 1) * P, s, "k")
                        store(nxt, (n - 1) * P, s, "q")
                for n in (15, 16):
                    store(n + 1, (n - 1) * P, n % 2, "k")
                    store(n + 1, (n - 1) * P, n % 2, "q")
                for sems in (kT_stored, qT_stored):
                    for s in range(2):
                        sp.wait_ge(sems[s], 16 * 8)

            @block.tensor
            def _(pe):
                def project(out, s, c, first, ready):
                    for kt in range(8):
                        if first and kt % 4 == 0:
                            pe.wait_ge(w_lo_done, 8 * c + kt + 4)
                        last = split_product(nc, out[:, :], x_hi[s][:, kt, :], x_lo[s][:, kt, :],
                                             w_hi[:, kt, c * BANK:(c + 1) * BANK], w_lo[:, kt, c * BANK:(c + 1) * BANK],
                                             kt == 0, kt == 7)
                    last.then_inc(ready, 1)

                def turn(out, src, signal):
                    for kt in range(4):
                        last = nc.tensor.transpose(out[:, kt * P:(kt + 1) * P], src[:, kt * P:(kt + 1) * P], keep["ident"][:, :])
                    last.then_inc(signal, 1)

                def turn_q(n, s):
                    pe.wait_ge(q_ready, n + 1)
                    if not (isinstance(n, int) and n == 0):
                        pe.wait_ge(qT_ready, n)
                    turn(ps_qT, q[s], q_turned)

                def tile(n, s, first=False):
                    pe.wait_ge(lo_ready, n + 1)
                    if not first:
                        pe.wait_ge(k_ready, n)
                    project(ps_k, s, 0, first, k_proj)
                    if not first:
                        turn_q(n - 1, 1 - s)
                    project(ps_q, s, 1, first, q_proj)
                    pe.wait_ge(k_ready, n + 1)
                    if not first:
                        pe.wait_ge(kT_ready, n)
                    turn(ps_kT, k[s], k_turned)

                tile(0, 0, True)
                tile(1, 1)
                tile(2, 0)
                with pe.Fori(1, 8) as i:
                    tile(2 * i + 1, 1)
                    tile(2 * i + 2, 0)
                turn_q(16, 0)

            @block.scalar
            def _(act):
                def tile(n, s, stores, rows=P):
                    at = None if rows != P else (n - 1) * P if isinstance(n, int) else act.snap((n - 1) * P)
                    act.wait_ge(rs_done, n + 1)
                    act.wait_ge(k_proj, n + 1)
                    if stores is not None:
                        act.wait_ge(k_stored[s], 16 * stores)
                    nc.scalar.activation(k[s][:, :], ps_k[:, :], ACT.Copy, scale=x_rs[s][:, 0:1]).then_inc(k_ready, 1)
                    act.wait_ge(k_ready, n + 1)
                    act.dma_start(ks_out if rows != P else k_out[bass.ds(at, P), :], k[s][0:rows, :]).then_inc(k_stored[s], 16)
                    act.wait_ge(q_proj, n + 1)
                    nc.scalar.activation(q[s][:, :], ps_q[:, :], ACT.Copy, scale=x_rs[s][:, 1:2]).then_inc(q_ready, 1)

                for c in range(2):
                    for kt in range(8):
                        n = 2 * c + kt // 4
                        if kt % 4 == 0:
                            act.wait_ge(w_loaded[n], 16)
                        nc.scalar.activation(w_hi[:, kt, c * BANK:(c + 1) * BANK], w_raw[n][:, kt % 4, :], ACT.Copy,
                                             scale=keep["cols"][:, G_MIX + kt:G_MIX + kt + 1]).then_inc(w_hi_done, 1)
                tile(0, 0, None, 32)
                tile(1, 1, None)
                tile(2, 0, 1)
                with act.Fori(1, 8) as i:
                    tile(2 * i + 1, 1, i)
                    tile(2 * i + 2, 0, i + 1)
                act.wait_ge(k_stored[0], 16 * 9)
                act.wait_ge(k_stored[1], 16 * 8)

            @block.vector
            def _(dve):
                def prepare(n, s, loads, rs_at):
                    dve.wait_ge(x_loaded[s], 16 * loads)
                    nc.vector.tensor_copy(x_hi[s][:, :, :], xT[s][:, :, :]).then_inc(hi_ready, 1)
                    dve.wait_ge(hi_ready, n + 1)
                    nc.vector.tensor_tensor(x_lo[s][:, :, :], xT[s][:, :, :], f32(x_hi[s][:, :, :]), ALU.subtract).then_inc(lo_ready, 1)
                    rs = keep["rs"][:, bass.ds(rs_at, 1)]
                    if not (isinstance(n, int) and n < 2):
                        dve.wait_ge(q_ready, n - 1)
                    nc.vector.tensor_scalar(x_rs[s][:, 0:1], rs, 1.0, None, ALU.mult)
                    nc.vector.tensor_scalar(x_rs[s][:, 1:2], rs, 0.125, None, ALU.mult).then_inc(rs_done, 1)

                def turned(n, s, which, stores):
                    signal, ready, src, dst, stored, own = (
                        (k_turned, kT_ready, ps_kT, kT, kT_stored, keep["kT_s"]) if which == "k" else
                        (q_turned, qT_ready, ps_qT, qT, qT_stored, keep["qT_s"]))
                    dve.wait_ge(signal, n + 1)
                    if isinstance(n, int) and n == 0:
                        nc.vector.tensor_copy(own[:, :, :], src[:, :].rearrange("p (k t) -> p k t", k=4)[:, :, 0:32]).then_inc(ready, 1)
                        return
                    if stores is not None:
                        dve.wait_ge(stored[s], 16 * stores)
                    nc.vector.tensor_copy(dst[s][:, :, :].rearrange("p k t -> p (k t)"), src[:, :]).then_inc(ready, 1)

                prepare(0, 0, 2, 16)
                for c in range(2):
                    for kt in range(8):
                        n = 2 * c + kt // 4
                        dve.wait_ge(w_hi_done, 8 * c + kt + 1)
                        nc.vector.scalar_tensor_tensor(
                            w_lo[:, kt, c * BANK:(c + 1) * BANK], w_raw[n][:, kt % 4, :], keep["cols"][:, G_MIX + kt:G_MIX + kt + 1],
                            f32(w_hi[:, kt, c * BANK:(c + 1) * BANK]), ALU.mult, ALU.subtract).then_inc(w_lo_done, 1)
                def step(j, odd, stored=True):
                    n = 2 * j + odd
                    before = j - 1 if stored else None
                    prepare(n + 1, 1 - odd, j + 3 if odd else j + 1, n)
                    turned(n - 1, 1 - odd, "q", before)
                    turned(n, odd, "k", (j if odd else before) if stored or j == 1 and odd else None)

                prepare(1, 1, 1, 0)
                turned(0, 0, "k", None)
                prepare(2, 0, 3, 1)
                turned(0, 0, "q", None)
                turned(1, 1, "k", None)
                step(1, 0, False)
                step(1, 1, False)
                with dve.Fori(2, 8) as j:
                    step(j, 0)
                    step(j, 1)
                turned(15, 1, "q", 7)
                turned(16, 0, "k", 7)
                turned(16, 0, "q", 7)


def attend_prompt(nc, keep, T, D):
    HEADS, NQ, LAG = 8, 16, 3
    PER = 2 * NQ
    granules = [1 + (s % NQ) // 8 for s in range(PER)]
    groups = [1 + (s % NQ) // 4 for s in range(PER)]
    NG, NR = sum(granules), sum(groups)

    def before(counts, total, s):
        return sum(counts[:s]) if s >= 0 else sum(counts[:s + PER]) - total

    with ExitStack() as ctx:
        m = Alloc(nc, ctx, "at")
        k_raw, q_raw = m.sb("k_raw", [P, 2048]), m.sb("q_raw", [P, 2048])
        v_raw = m.sb("v_raw", [P, NQ, 64])
        k_hi, k_lo, q2 = ([m.sb(f"{n}{s}", [P, 2048], F32R) for s in range(2)] for n in ("k_hi", "k_lo", "q2"))
        v2 = [m.sb(f"v2{s}", [P, NQ, P], F32R) for s in range(2)]
        beta = [m.sb(f"beta{s}", [P, 2048]) for s in range(4)]
        rest = [m.sb(f"rest{s}", [P, 2048]) for s in range(4)]
        aT = [m.sb(f"aT{s}", [P, 4, 2 * P], F32R) for s in range(4)]
        o2 = [m.sb(f"o2{s}", [P, BANK]) for s in range(2)]
        bias = [m.sb(f"bias{s}", [P, 1]) for s in range(2)]
        o_part = m.sb("o_part", [P, P])
        oT = [m.sb(f"oT{s}", [64, BANK]) for s in range(2)]
        sq = m.sb("sq", [64, BANK])
        ssum = m.sb("ssum", [64, 2048])
        far = m.sb("far", [P, P])
        far_r, ident_r = m.sb("far_r", [P, P], F32R), m.sb("ident_r", [P, P], F32R)
        fold = m.sb("fold", [P, 64])
        ps_z = [m.bank(f"ps_z{s}", (P, 1024)) for s in range(2)]
        ps_t = [m.bank(f"ps_t{s}") for s in range(2)]
        ps_o, ps_f = m.bank("ps_o"), m.bank("ps_f")

        loaded, head_split, z_ready, b_done, rest_done, product_done, a_done = (
            m.sem(n) for n in ("loaded", "head_split", "z_ready", "b_done", "rest_done", "product_done", "a_done"))
        a_turned, ahi_done, alo_done, o_ready, o_read, folded, oT_done, osq_done, sum_done = (
            m.sem(n) for n in ("a_turned", "ahi_done", "alo_done", "o_ready", "o_read", "folded", "oT_done", "osq_done", "sum_done"))
        o_part_done = m.sem("o_part_done")
        oT_stored = [m.sem(f"oT_stored{s}") for s in range(2)]
        made, cast, mean_ready, rms_done, rs_done, rs_stored = (
            m.sem(n) for n in ("made", "cast", "mean_ready", "rms_done", "rs_done", "rs_stored"))

        v_src = T["v_prompt"][0, 0].rearrange("(kt p) h d -> p kt h d", p=P)

        def iterations(eng, tick, drain=True):
            for s in range(PER):
                tick(0, s)
            with eng.Fori(1, HEADS // 2 - 1) as it:
                for s in range(PER):
                    tick(it, s)
            for s in range(PER):
                tick(HEADS // 2 - 1, s)
            for s in range(LAG):
                tick(HEADS // 2, s)

        def has(it, s):
            if isinstance(it, int):
                return 0 <= PER * it + s < PER * HEADS // 2
            return True

        with nc.Block() as block:

            @block.sync
            def _(sp):
                def load(h):
                    rows = bass.ds(64 * h, 64)
                    for raw, src in ((k_raw, D["KT"]), (q_raw, D["QT"])):
                        for half in range(2):
                            sp.dma_start(raw[64 * half:64 * half + 64, :], src[rows, :]).then_inc(loaded, 16)
                    sp.dma_start(v_raw[:, :, :].unsqueeze(2), v_src[:, :, bass.ds(h, 1), :]).then_inc(loaded, 16)

                def store(h, quad):
                    n = 4 * h + quad + 1
                    wait_apart(sp, oT_done, n if isinstance(n, int) else sp.snap(n))
                    sp.dma_start(D["MIXT"][bass.ds(64 * h, 64), quad * BANK:(quad + 1) * BANK], oT[quad % 2][:, :])\
                        .then_inc(oT_stored[quad % 2], 16)

                load(0)
                sp.wait_ge(head_split, 7)
                load(1)
                with sp.Fori(0, HEADS - 2) as h:
                    for quad in range(4):
                        store(h, quad)
                    wait_apart(sp, head_split, sp.snap(7 * h + 14))
                    load(h + 2)
                for h in (HEADS - 2, HEADS - 1):
                    for quad in range(4):
                        store(h, quad)
                sp.wait_ge(oT_stored[0], 16 * 16)
                sp.wait_ge(oT_stored[1], 16 * 16)
                sp.wait_ge(rs_done, 4)
                sp.dma_start(D["RSB"][:, 0:2048], beta[0][:, :]).then_inc(rs_stored, 16)
                sp.wait_ge(rs_stored, 16)

            @block.gpsimd
            def _(pool):
                nc.gpsimd.memset(far[:, :], 0.0).then_inc(made, 1)
                nc.gpsimd.memset(fold[:, :], 0.0).then_inc(made, 1)
                nc.gpsimd.memset(ssum[:, :], 0.0).then_inc(made, 1)
                pool.wait_ge(made, 3)
                nc.gpsimd.affine_select(out=far[:, :], in_=far[:, :], pattern=[[-1, P]], compare_op=ALU.is_gt,
                                        fill=-float(2 ** 100), base=0, channel_multiplier=1).then_inc(made, 1)
                pool.wait_ge(made, 4)
                nc.gpsimd.affine_select(out=fold[0:64, :], in_=fold[0:64, :], pattern=[[-1, 64]], compare_op=ALU.not_equal,
                                        fill=1.0, base=0, channel_multiplier=1).then_inc(made, 1)
                pool.wait_ge(made, 5)
                nc.gpsimd.affine_select(out=fold[64:P, :], in_=fold[64:P, :], pattern=[[-1, 64]], compare_op=ALU.not_equal,
                                        fill=1.0, base=0, channel_multiplier=1).then_inc(made, 1)

                def tick(it, t):
                    s = t - 2
                    if not has(it, s):
                        return
                    n = P * (s % NQ + 1)
                    pool.wait_ge(product_done, PER * it + s + 1)
                    nc.gpsimd.tensor_tensor(beta[s % 4][:, 0:n - 1], beta[s % 4][:, 0:n - 1], rest[s % 4][:, 1:n], ALU.mult)\
                        .then_inc(a_done, 1)

                iterations(pool, tick)

            @block.tensor
            def _(pe):
                def logits(it, s):
                    i, hs = s % NQ, s // NQ
                    n = P * (i + 1)
                    if i == 0:
                        pe.wait_ge(head_split, 14 * it + 7 * hs + 7)
                    for g in range(granules[s]):
                        at = NG * it + before(granules, NG, s) + g
                        z = ps_z[(before(granules, NG, s) + g) % 2]
                        pe.wait_ge(b_done, at + 1)
                        width = min(n - 1024 * g, 1024)
                        for c in range(0, width, BANK):
                            w = max(min(BANK, width - c), 2 * P)
                            k0 = 1024 * g + c
                            diagonal = k0 <= n - P < k0 + w
                            q = q2[hs][:, i * P:(i + 1) * P]
                            nc.tensor.matmul(z[:, c:c + w], q, k_hi[hs][:, k0:k0 + w], start=True, stop=False)
                            last = nc.tensor.matmul(z[:, c:c + w], q, k_lo[hs][:, k0:k0 + w], start=False, stop=not diagonal)
                            if diagonal:
                                d = n - P - 1024 * g
                                last = nc.tensor.matmul(z[:, d:d + P], ident_r[:, :], far_r[:, :], start=False, stop=True)
                        last.then_inc(z_ready, 1)

                def turn(it, s, r):
                    at = NR * it + before(groups, NR, s) + r
                    slot = before(groups, NR, s) + r
                    pe.wait_ge(alo_done, at + 1)
                    for kt in range(4 * r, min(4 * r + 4, s % NQ + 1)):
                        last = nc.tensor.transpose(ps_t[slot % 2][:, kt % 4 * P:kt % 4 * P + P], beta[s % 4][:, kt * P:(kt + 1) * P],
                                                   keep["ident"][:, :])
                    last.then_inc(a_turned, 1)

                def weigh(it, s, r):
                    at = NR * it + before(groups, NR, s) + r
                    slot = before(groups, NR, s) + r
                    pe.wait_ge(alo_done, at + 3)
                    if r == 0:
                        pe.wait_ge(o_read, PER * it + s + 1)
                    i, hs = s % NQ, s // NQ % 2
                    for kt in range(4 * r, min(4 * r + 4, i + 1)):
                        last = nc.tensor.matmul(ps_o[:, 0:2 * P], v2[hs][:, kt, :], aT[slot % 4][:, kt % 4, :],
                                                start=kt == 0, stop=kt == i)
                    if r == groups[s] - 1:
                        last.then_inc(o_ready, 1)

                def add_halves(it, s):
                    quad = s // 4
                    pe.wait_ge(o_read, PER * it + s + 2)
                    pe.wait_ge(osq_done, 8 * it + quad + 1)
                    nc.tensor.matmul(ps_f[0:64, :], fold[:, :], o2[quad % 2][:, :], start=True, stop=True).then_inc(folded, 1)

                def tick(it, t):
                    s = t - LAG
                    if has(it, s):
                        pe.wait_ge(a_done, PER * it + s + 1)
                        turn(it, s, 0)
                        for r in range(1, groups[s]):
                            turn(it, s, r)
                            weigh(it, s, r - 1)
                    if has(it, t):
                        logits(it, t)
                    if has(it, s):
                        weigh(it, s, groups[s] - 1)
                    if has(it, s - 1) and s % 4 == 0:
                        add_halves(it, s - 1)

                pe.sem_inc(o_read, 1)
                pe.wait_ge(cast, 2)
                iterations(pe, tick)
                add_halves(HEADS // 2, -1)
                for c in range(4):
                    if c == 0:
                        pe.wait_ge(sum_done, 33)
                    if c >= 2:
                        pe.wait_ge(rms_done, c - 1)
                    nc.tensor.matmul(ps_t[c % 2][:, :], keep["mean512"][0:64, :], ssum[:, c * BANK:(c + 1) * BANK], start=True, stop=True)\
                        .then_inc(mean_ready, 1)

            @block.scalar
            def _(act):
                def tick(it, t):
                    if has(it, t - 1):
                        s = t - 1
                        n = P * (s % NQ + 1)
                        act.wait_ge(b_done, NG * it + before(granules, NG, s) + granules[s] + 2)
                        nc.scalar.activation(rest[s % 4][:, 0:n], beta[s % 4][:, 0:n], ACT.Identity, scale=-1.0, bias=1.0).then_inc(rest_done, 1)
                    if has(it, t - LAG):
                        s = t - LAG
                        for r in range(groups[s]):
                            at = NR * it + before(groups, NR, s) + r
                            slot = before(groups, NR, s) + r
                            w = min(4, s % NQ + 1 - 4 * r)
                            act.wait_ge(a_turned, at + 1)
                            nc.scalar.activation(aT[slot % 4][:, 0:w, 0:P], ps_t[slot % 2][:, 0:w * P].rearrange("p (k t) -> p k t", k=w),
                                                 ACT.Copy).then_inc(ahi_done, 1)
                    if has(it, t):
                        n = P * (t % NQ + 1)
                        for g in range(granules[t]):
                            at = before(granules, NG, t) + g
                            w = min(n - 1024 * g, 1024)
                            act.wait_ge(z_ready, NG * it + at + 1)
                            nc.scalar.activation(beta[t % 4][:, 1024 * g:1024 * g + w], ps_z[at % 2][:, 0:w], ACT.Sigmoid,
                                                 bias=bias[t // NQ][:, :]).then_inc(b_done, 1)
                    s = t - LAG - 1
                    if has(it, s) and s % 4 == 3:
                        fold_out(it, s // 4)

                def fold_out(it, quad):
                    act.wait_ge(folded, 8 * it + quad + 1)
                    act.wait_ge(oT_stored[quad % 2], 64 * it + 16 * (quad // 2) + 16)
                    nc.scalar.activation(oT[quad % 2][:, :], ps_f[0:64, :], ACT.Copy).then_inc(oT_done, 1)
                    act.wait_ge(sum_done, 8 * it + quad + 1)
                    nc.scalar.activation(sq[:, :], ps_f[0:64, :], ACT.Square).then_inc(osq_done, 1)

                act.sem_inc(b_done, 2)
                act.sem_inc(oT_stored[0], 16)
                act.sem_inc(oT_stored[1], 16)
                act.sem_inc(osq_done, 1)
                iterations(act, tick)
                fold_out(HEADS // 2, -1)
                for c in range(4):
                    act.wait_ge(mean_ready, c + 1)
                    nc.scalar.activation(beta[0][:, c * BANK:(c + 1) * BANK], ps_t[c % 2][:, :], ACT.Sqrt, bias=keep["eps"][:, :])\
                        .then_inc(rms_done, 1)

            @block.vector
            def _(dve):
                def split_head(h, slot):
                    dve.wait_ge(loaded, 80 * h + 80)
                    at = 7 * h
                    nc.vector.tensor_copy(k_hi[slot][:, :], k_raw[:, :]).then_inc(head_split, 1)
                    nc.vector.tensor_copy(q2[slot][:, :], q_raw[:, :]).then_inc(head_split, 1)
                    nc.vector.tensor_copy(v2[slot][:, :, 0:64], v_raw[:, :, :]).then_inc(head_split, 1)
                    nc.vector.tensor_scalar(bias[slot][:, :], keep["sb_bias"][:, bass.ds(h, 1)], 1.0, None, ALU.mult).then_inc(head_split, 1)
                    dve.wait_ge(head_split, at + 4)
                    nc.vector.tensor_tensor(k_lo[slot][:, :], k_raw[:, :], f32(k_hi[slot][:, :]), ALU.subtract).then_inc(head_split, 1)
                    nc.vector.tensor_tensor(q2[slot][64:P, :], q_raw[64:P, :], f32(q2[slot][64:P, :]), ALU.subtract).then_inc(head_split, 1)
                    nc.vector.tensor_tensor(v2[slot][:, :, 64:P], v_raw[:, :, :], f32(v2[slot][:, :, 0:64]), ALU.subtract).then_inc(head_split, 1)

                def tick(it, t):
                    if has(it, t - 1):
                        s = t - 1
                        n = P * (s % NQ + 1)
                        r = rest[s % 4][:, 0:n][:, ::-1]
                        dve.wait_ge(rest_done, PER * it + s + 1)
                        nc.vector.tensor_tensor_scan(r, r, r, 1.0, ALU.mult, ALU.min).then_inc(product_done, 1)
                    s = t - LAG
                    if has(it, s):
                        for g in range(groups[s]):
                            at = NR * it + before(groups, NR, s) + g
                            slot = before(groups, NR, s) + g
                            w = min(4, s % NQ + 1 - 4 * g)
                            dve.wait_ge(ahi_done, at + 1)
                            nc.vector.tensor_tensor(aT[slot % 4][:, 0:w, P:2 * P], ps_t[slot % 2][:, 0:w * P].rearrange("p (k t) -> p k t", k=w),
                                                    f32(aT[slot % 4][:, 0:w, 0:P]), ALU.subtract).then_inc(alo_done, 1)
                    if s % NQ == 8 and has(it, s) and not (isinstance(it, int) and 2 * it + s // NQ + 1 >= HEADS):
                        split_head(2 * it + s // NQ + 1, 1 - s // NQ)
                    if has(it, s):
                        quad = s // 4
                        dve.wait_ge(o_ready, PER * it + s + 1)
                        nc.vector.tensor_copy(o_part[:, :], ps_o[:, P:2 * P]).then_inc(o_part_done, 1)
                        dve.wait_ge(o_part_done, PER * it + s + 1)
                        nc.vector.tensor_tensor(o2[quad % 2][:, s % 4 * P:(s % 4 + 1) * P], ps_o[:, 0:P], o_part[:, :], ALU.add).then_inc(o_read, 1)
                    if has(it, s - 2) and (s - 2) % 4 == 3:
                        add_square(it, (s - 2) // 4)

                def add_square(it, quad):
                    dve.wait_ge(osq_done, 8 * it + quad + 2)
                    cols = slice(quad % 4 * BANK, (quad % 4 + 1) * BANK)
                    nc.vector.tensor_tensor(ssum[:, cols], ssum[:, cols], sq[:, :], ALU.add).then_inc(sum_done, 1)

                dve.sem_inc(alo_done, 2)
                dve.sem_inc(sum_done, 1)
                dve.wait_ge(made, 6)
                nc.vector.tensor_copy(far_r[:, :], far[:, :]).then_inc(cast, 1)
                nc.vector.tensor_copy(ident_r[:, :], keep["ident"][:, :]).then_inc(cast, 1)
                split_head(0, 0)
                iterations(dve, tick)
                add_square(HEADS // 2, -1)
                for c in range(4):
                    dve.wait_ge(rms_done, c + 1)
                    nc.vector.reciprocal(beta[0][:, c * BANK:(c + 1) * BANK], beta[0][:, c * BANK:(c + 1) * BANK]).then_inc(rs_done, 1)


def attend_sample(nc, keep, T, D):
    GROUPS, PB, STEPS, RING = 2, 4, 16, 8
    KEYS = 2048
    with ExitStack() as ctx:
        m = Alloc(nc, ctx, "as")
        pages = [m.sb(f"pages{s}", [P, 4, BANK]) for s in range(RING)]
        kT4 = [m.sb(f"kT4{s}", [P, 4, BANK]) for s in range(2)]
        q_block = m.sb("q_block", [P, 4, PB, 32])
        k_new = m.sb("k_new", [P, 4, 4 * PB])
        v_new = m.sb("v_new", [4, PB, BANK])
        beta, rest = m.sb("beta", [P, KEYS + 4]), m.sb("rest", [P, KEYS + 4])
        aT = m.sb("aT", [P, 16, P])
        aT_new = m.sb("aT_new", [4, P])
        own = m.sb("own", [P, BANK])
        row_head, row_bias, biases = m.sb("row_head", [P, 8]), m.sb("row_bias", [P, 1]), m.sb("biases", [P, 8])
        row_query, before = m.sb("row_query", [P, 4]), m.sb("before", [P, 4])
        merge = m.sb("merge", [P, 4 * PB])
        mixT, sq = m.sb("mixT", [P, 4, 32]), m.sb("sq", [P, 4, 32])
        rms = m.sb("rms", [P, 32])
        ps_z = [m.bank(f"ps_z{j}") for j in range(4)]
        ps_t = [m.bank(f"ps_t{s}") for s in range(2)]
        ps_new, ps_o = m.bank("ps_new"), m.bank("ps_o")

        masks, blocks, v_loaded, turned, kT_even, kT_odd, z_done, new_done, b_done, b_new_done, new_masked, rest_done = (
            m.sem(n) for n in ("masks", "blocks", "v_loaded", "turned", "kT_even", "kT_odd", "z_done", "new_done", "b_done",
                               "b_new_done", "new_masked", "rest_done"))
        product_done, a_done, a_turned, aT_even, aT_odd, page_used, o_ready, own_done, mix_ready, mix_done = (
            m.sem(n) for n in ("product_done", "a_done", "a_turned", "aT_even", "aT_odd", "page_used", "o_ready", "own_done",
                               "mix_ready", "mix_done"))
        sq_done, mean_ready, rms_done, rs_done, stored = (m.sem(n) for n in ("sq_done", "mean_ready", "rms_done", "rs_done", "stored"))
        page_loaded = [m.sem(f"page_loaded{s}") for s in range(RING)]
        N_MASKS = 10

        caches = [T[n][0].rearrange("n p h d -> p n (h d)") for n in ("cache_k", "cache_v")]
        v_src = T["v_sample"][0].rearrange("b t h d -> t b (h d)")

        with nc.Block() as block:

            @block.sync
            def _(sp):
                with sp.Fori(0, GROUPS) as g:
                    for part in range(2):
                        if part == 1:
                            wait_apart(sp, o_ready, sp.snap(g + 1))
                            sp.dma_start(v_new[:, :, :], v_src[:, bass.ds(PB * g, PB), :]).then_inc(v_loaded, 16)
                        with sp.Fori(0, STEPS // RING) as turn:
                            for slot in range(RING):
                                first = sp.snap(16 * PB * g + 4 * (RING // PB) * turn + 16 * (slot % PB) + 4 * (slot // PB))
                                free = sp.snap(2 * STEPS * g + STEPS * part + RING * turn + slot + 1)
                                with sp.Fori(0, 4) as p:
                                    wait_apart(sp, page_used, free)
                                    page = sp.value_load(keep["page_table"][0:1, bass.ds(first + p, 1)], min_val=0, max_val=159)
                                    sp.dma_start(pages[slot][:, bass.ds(p, 1), :], caches[part][:, bass.ds(page, 1), :])\
                                        .then_inc(page_loaded[slot], 16)
                sp.wait_ge(mix_done, GROUPS + 1)
                sp.dma_start(D["MIXT"][0:512, 2048:2080].rearrange("(k p) t -> p k t", p=P), mixT[:, :, :]).then_inc(stored, 16)
                sp.wait_ge(rs_done, 1)
                sp.dma_start(D["RSB"][:, 2048:2080], rms[:, :]).then_inc(stored, 16)
                sp.wait_ge(stored, 32)

            @block.tensor
            def _(pe):
                def logits(g, k):
                    j, bi = k // PB, k % PB
                    pe.wait_ge(kT_even, 2 * STEPS * g + 2 * k + 3)
                    pe.wait_ge(kT_odd, 2 * STEPS * g + 2 * k + 3)
                    for hp in range(4):
                        last = nc.tensor.matmul(ps_z[j][32 * bi:32 * bi + 32, :], q_block[:, hp, bi, :], kT4[k % 2][:, hp, :],
                                                start=hp == 0, stop=hp == 3, tile_position=(0, 32 * bi))
                    last.then_inc(z_done, 1)

                pe.sem_inc(page_used, RING)
                pe.sem_inc(o_ready, 1)
                pe.sem_inc(z_done, 2)
                pe.wait_ge(masks, N_MASKS)
                with pe.Fori(0, GROUPS) as g:
                    pe.wait_ge(blocks, 9 * g + 9)
                    for k in range(STEPS):
                        pe.wait_ge(page_loaded[k % RING], 256 * g + 64 * (k // RING) + 64)
                        for p in range(4):
                            pe.wait_ge((kT_even, kT_odd)[p % 2], 2 * STEPS * g + 2 * k + p // 2 + 1)
                            for hp in range(4):
                                last = nc.tensor.transpose(ps_t[p % 2][:, hp * P:(hp + 1) * P], pages[k % RING][:, p, hp * P:(hp + 1) * P],
                                                           keep["ident"][:, :])
                            last.then_inc(turned, 1)
                        pe.wait_ge(turned, 4 * STEPS * g + 4 * k + 4)
                        pe.sem_inc(page_used, 1)
                        if k:
                            logits(g, k - 1)
                    logits(g, STEPS - 1)
                    pe.wait_ge(mix_done, g + 1)
                    for bi in range(PB):
                        for hp in range(4):
                            last = nc.tensor.matmul(ps_new[32 * bi:32 * bi + 32, 0:4], q_block[:, hp, bi, :], k_new[:, hp, 4 * bi:4 * bi + 4],
                                                    start=hp == 0, stop=hp == 3, tile_position=(0, 32 * bi))
                    last.then_inc(new_done, 1)
                    pe.wait_ge(a_done, g + 1)
                    for r in range(4):
                        if r >= 2:
                            pe.wait_ge((aT_even, aT_odd)[r % 2], (3, 2)[r % 2] * g + 1)
                        for kt in range(4):
                            last = nc.tensor.transpose(ps_t[r % 2][:, kt * P:(kt + 1) * P], beta[:, (4 * r + kt) * P:(4 * r + kt + 1) * P],
                                                       keep["ident"][:, :])
                        last.then_inc(a_turned, 1)
                    pe.wait_ge(aT_even, 3 * g + 2)
                    nc.tensor.transpose(ps_t[0][0:4, 0:P], beta[:, KEYS:KEYS + 4], keep["ident"][:, :]).then_inc(a_turned, 1)
                    for k in range(STEPS):
                        j, bi = k // PB, k % PB
                        if k == 3 * PB:
                            pe.wait_ge(v_loaded, 16 * g + 16)
                            pe.wait_ge(aT_even, 3 * g + 3)
                        if bi == 0:
                            pe.wait_ge((aT_even, aT_odd)[j % 2], (3, 2)[j % 2] * g + j // 2 + 1)
                        pe.wait_ge(page_loaded[k % RING], 256 * g + 128 + 64 * (k // RING) + 64)
                        for p in range(4):
                            last = nc.tensor.matmul(ps_o[32 * bi:32 * bi + 32, :], aT[:, 4 * j + p, 32 * bi:32 * bi + 32], pages[k % RING][:, p, :],
                                                    start=k < PB and p == 0, stop=False, tile_position=(0, 32 * bi))
                        last.then_inc(page_used, 1)
                    for bi in range(PB):
                        last = nc.tensor.matmul(ps_o[32 * bi:32 * bi + 32, :], aT_new[:, 32 * bi:32 * bi + 32], v_new[:, bi, :],
                                                start=False, stop=True, tile_position=(0, 32 * bi))
                    last.then_inc(o_ready, 1)
                    pe.wait_ge(own_done, g + 1)
                    for c in range(4):
                        last = nc.tensor.matmul(ps_new[:, 64 + 16 * c:80 + 16 * c], own[:, c * P:(c + 1) * P], merge[:, :], start=True, stop=True)
                    last.then_inc(mix_ready, 1)
                pe.wait_ge(sq_done, 1)
                for c in range(4):
                    last = nc.tensor.matmul(ps_new[:, 0:32], keep["mean512"][:, :], sq[:, c, :], start=c == 0, stop=c == 3)
                last.then_inc(mean_ready, 1)

            @block.scalar
            def _(act):
                def sigmoid(g, j):
                    cols = slice(j * BANK, (j + 1) * BANK)
                    act.wait_ge(z_done, STEPS * g + PB * (j + 1) + 2)
                    nc.scalar.activation(beta[:, cols], ps_z[j][:, :], ACT.Sigmoid, bias=row_bias[:, :]).then_inc(b_done, 1)
                    act.wait_ge(b_done, 4 * g + j + 1)
                    if j < 3:
                        nc.scalar.activation(rest[:, cols], beta[:, cols], ACT.Identity, scale=-1.0, bias=1.0).then_inc(rest_done, 1)

                act.sem_inc(kT_odd, 1)
                act.wait_ge(masks, N_MASKS)
                with act.Fori(0, GROUPS) as g:
                    for k in range(STEPS):
                        for p in (1, 3):
                            act.wait_ge(turned, 4 * STEPS * g + 4 * k + p + 1)
                            if p == 1:
                                act.wait_ge(z_done, STEPS * g + k + 1)
                            nc.scalar.activation(kT4[k % 2][:, :, p * P:(p + 1) * P], ps_t[1][:, :].rearrange("p (h t) -> p h t", h=4),
                                                 ACT.Copy).then_inc(kT_odd, 1)
                        if k % PB == 0 and k:
                            sigmoid(g, k // PB - 1)
                    sigmoid(g, 3)
                    act.wait_ge(new_done, g + 1)
                    nc.scalar.activation(beta[:, KEYS:KEYS + 4], ps_new[:, 0:4], ACT.Sigmoid, bias=row_bias[:, :]).then_inc(b_new_done, 1)
                    act.wait_ge(new_masked, g + 1)
                    nc.scalar.activation(rest[:, 1536:KEYS + 4], beta[:, 1536:KEYS + 4], ACT.Identity, scale=-1.0, bias=1.0).then_inc(rest_done, 1)
                    for r in (1, 3):
                        act.wait_ge(a_turned, 5 * g + r + 1)
                        nc.scalar.activation(aT[:, 4 * r:4 * r + 4, :], ps_t[1][:, :].rearrange("p (k t) -> p k t", k=4), ACT.Copy)\
                            .then_inc(aT_odd, 1)
                act.wait_ge(mean_ready, 1)
                nc.scalar.activation(rms[:, :], ps_new[:, 0:32], ACT.Sqrt, bias=keep["eps"][:, :]).then_inc(rms_done, 1)

            @block.gpsimd
            def _(pool):
                nc.gpsimd.memset(q_block[:, :, :, :], 0.0).then_inc(masks, 1)

            @block.vector
            def _(dve):
                ident = keep["ident"]
                nc.vector.tensor_reduce(row_head[:, :], ident[:, :].rearrange("p (b h q) -> p h b q", b=PB, h=8), AX.XY, ALU.add).then_inc(masks, 1)
                nc.vector.tensor_reduce(row_query[:, :], ident[:, :].rearrange("p (b h q) -> p q b h", b=PB, h=8), AX.XY, ALU.add).then_inc(masks, 1)
                nc.vector.tensor_reduce(merge[:, :].rearrange("p (b q) -> p b q", b=PB), ident[:, :].rearrange("p (b h q) -> p b q h", b=PB, h=8),
                                        AX.X, ALU.add).then_inc(masks, 1)
                nc.vector.memset(before[:, :], 0.0).then_inc(masks, 1)
                dve.wait_ge(masks, 5)
                for t in range(3):
                    nc.vector.tensor_reduce(before[:, t:t + 1], row_query[:, t + 1:4], AX.X, ALU.add).then_inc(masks, 1)
                nc.vector.tensor_tensor(biases[:, :], row_head[:, :], keep["sb_bias"][:, :], ALU.mult).then_inc(masks, 1)
                dve.wait_ge(masks, 9)
                nc.vector.tensor_reduce(row_bias[:, :], biases[:, :], AX.X, ALU.add).then_inc(masks, 1)
                dve.sem_inc(kT_even, 1)
                dve.sem_inc(mix_done, 1)
                dve.wait_ge(masks, N_MASKS)
                with dve.Fori(0, GROUPS) as g:
                    cols = bass.ds(4 * PB * g, 4 * PB)
                    for h in range(8):
                        rows, hp = slice(64 * (h % 2), 64 * (h % 2) + 64), h // 2
                        nc.vector.tensor_scalar(q_block[rows, hp, :, 4 * h:4 * h + 4], keep["qT_s"][rows, hp, cols].rearrange("p (b q) -> p b q", b=PB),
                                                1.0, None, ALU.mult).then_inc(blocks, 1)
                    nc.vector.tensor_scalar(k_new[:, :, :], keep["kT_s"][:, :, cols], 1.0, None, ALU.mult).then_inc(blocks, 1)
                    for k in range(STEPS):
                        for p in (0, 2):
                            dve.wait_ge(turned, 4 * STEPS * g + 4 * k + p + 1)
                            if p == 0:
                                dve.wait_ge(z_done, STEPS * g + k + 1)
                            nc.vector.tensor_copy(kT4[k % 2][:, :, p * P:(p + 1) * P], ps_t[0][:, :].rearrange("p (h t) -> p h t", h=4))\
                                .then_inc(kT_even, 1)
                    dve.wait_ge(b_new_done, g + 1)
                    nc.vector.tensor_tensor(beta[:, KEYS:KEYS + 4], beta[:, KEYS:KEYS + 4], before[:, :], ALU.mult).then_inc(new_masked, 1)
                    dve.wait_ge(rest_done, 4 * g + 4)
                    r = rest[:, :][:, ::-1]
                    nc.vector.tensor_tensor_scan(r, r, r, 1.0, ALU.mult, ALU.min).then_inc(product_done, 1)
                    dve.wait_ge(product_done, g + 1)
                    nc.vector.tensor_tensor(beta[:, 0:KEYS + 3], beta[:, 0:KEYS + 3], rest[:, 1:KEYS + 4], ALU.mult).then_inc(a_done, 1)
                    for r in (0, 2):
                        dve.wait_ge(a_turned, 5 * g + r + 1)
                        nc.vector.tensor_copy(aT[:, 4 * r:4 * r + 4, :], ps_t[0][:, :].rearrange("p (k t) -> p k t", k=4)).then_inc(aT_even, 1)
                    dve.wait_ge(a_turned, 5 * g + 5)
                    nc.vector.tensor_copy(aT_new[:, :], ps_t[0][0:4, 0:P]).then_inc(aT_even, 1)
                    dve.wait_ge(o_ready, g + 2)
                    nc.vector.tensor_tensor(own[:, :].rearrange("p (h d) -> p h d", h=8), ps_o[:, :].rearrange("p (h d) -> p h d", h=8),
                                            row_head[:, :].unsqueeze(2).to_broadcast([P, 8, 64]), ALU.mult).then_inc(own_done, 1)
                    dve.wait_ge(mix_ready, g + 1)
                    nc.vector.tensor_scalar(mixT[:, :, cols], ps_new[:, 64:128].rearrange("p (c t) -> p c t", c=4), 1.0, None, ALU.mult)\
                        .then_inc(mix_done, 1)
                dve.wait_ge(mix_done, GROUPS + 1)
                nc.vector.tensor_tensor(sq[:, :, :], mixT[:, :, :], mixT[:, :, :], ALU.mult).then_inc(sq_done, 1)
                dve.wait_ge(rms_done, 1)
                nc.vector.reciprocal(rms[:, :], rms[:, :]).then_inc(rs_done, 1)


def finish_tokens(nc, keep, T, D):
    NB, TB, NJ = 5, 416, 22
    SLABS, UNITS = 88, 76
    O_AT, U_AT, D_AT, P_AT = 0, 8, 52, 76
    OU, UU, DU, PU = 0, 8, 52, 60
    MIX_ORDER = (4, 5, 6, 7, 0, 1, 2, 3)
    with ExitStack() as ctx:
        m = Alloc(nc, ctx, "pf")
        h = m.sb("h", [P, 8, TB])
        mix = m.sb("mix", [P, 8, TB])
        x_hi, x_lo = (m.sb(n, [P, 8, TB], F32R) for n in ("x_hi", "x_lo"))
        f_hi, f_lo = (m.sb(n, [P, NJ, TB], F32R) for n in ("f_hi", "f_lo"))
        raw = [m.sb(f"raw{n}", [P, 1024]) for n in range(4)]
        w_hi = [m.sb(f"w_hi{n}", [P, 1024], F32R) for n in range(4)]
        w_lo = [m.sb(f"w_lo{n}", [P, 1024], F32R) for n in range(4)]
        p_raw = m.sb("p_raw", [P, 2, TB])
        rs_sb = m.sb("rs_sb", [P, TB])
        ssum, sq, rs = (m.sb(n, [P, TB]) for n in ("ssum", "sq", "rs"))
        gate = m.sb("gate", [P, TB + 2])
        gate_s = m.sb("gate_s", [P, 8, 6])
        c = [m.sb(f"c{n}", [P, BANK]) for n in range(2)]
        u = [m.sb(f"u{n}", [P, BANK]) for n in range(2)]
        carry = m.sb("carry", [P, NJ, 2])
        state = m.sb("state", [P, NJ, 16])
        last_rows = m.sb("last_rows", [P, NJ, 18])
        acc = [m.bank(f"acc{n}") for n in range(4)]
        ps_sum = m.bank("ps_sum")
        ps_t = [m.bank(f"ps_t{n}") for n in range(2)]
        state_raw = h[0:16, :, :].rearrange("p k t -> p (k t)")[:, 0:NJ * P]
        out_rows = mix[0:18, :, :].rearrange("p k t -> p (k t)")[:, 0:NJ * P]
        y = [c[0], c[1], u[0], u[1]]

        raw_loaded = [m.sem(f"raw_loaded{n}") for n in range(4)]
        hi_split, lo_split, slab_done, acc_free = (m.sem(n) for n in ("hi_split", "lo_split", "slab_done", "acc_free"))
        h_loaded, mix_loaded, p_loaded, rs_loaded, st_loaded, st_turned, st_ready, carry_zero = (
            m.sem(n) for n in ("h_loaded", "mix_loaded", "p_loaded", "rs_loaded", "st_loaded", "st_turned", "st_ready", "carry_zero"))
        mix_scaled, mix_hi, mix_lo = (m.sem(n) for n in ("mix_scaled", "mix_hi", "mix_lo"))
        sq_done, s_added, xhi_done, xlo_done, sum_ready, rms_done, rs_done = (
            m.sem(n) for n in ("sq_done", "s_added", "xhi_done", "xlo_done", "sum_ready", "rms_done", "rs_done"))
        conv_step, gelu_done, f_ready, fhi_done, flo_done = (
            m.sem(n) for n in ("conv_step", "gelu_done", "f_ready", "fhi_done", "flo_done"))
        p_hi, p_lo, sig_done, h_ready, y_ready, y_turned, y_copied = (
            m.sem(n) for n in ("p_hi", "p_lo", "sig_done", "h_ready", "y_ready", "y_turned", "y_copied"))
        y_stored = [m.sem(f"y_stored{n}") for n in range(4)]
        rows_turned, rows_copied, rows_stored = m.sem("rows_turned"), m.sem("rows_copied"), m.sem("rows_stored")

        w_out, w_up, w_down, w_gate, w_proj = (
            T[n][0].rearrange("(k p) n -> p k n", p=P) for n in ("w_out", "w_up", "w_down", "w_ple_gate", "w_ple_proj"))
        XT, PT, MIXT = (D[n].rearrange("(k p) t -> p k t", p=P) for n in ("XT", "PT", "MIXT"))

        def col(n, count=1):
            return keep["cols"][:, bass.ds(n, count)]

        STEPS, STEPS_LAST = 5, 11

        with nc.Block() as block:

            @block.sync
            def _(sp):
                def slab(q4, k, src, shape=None):
                    g = 4 * q4 + k + 1
                    if not isinstance(g, int):
                        g = sp.snap(g)
                    wait_apart(sp, lo_split, g)
                    n = src.shape[1] * src.shape[2]
                    sp.dma_start(raw[k % 4][:, 0:n].rearrange("p (k n) -> p k n", k=src.shape[1]), src)\
                        .then_inc(raw_loaded[k % 4], 16)

                def load_mix(at):
                    sp.dma_start(mix[:, :, :], MIXT[:, :, bass.ds(at, TB)]).then_inc(mix_loaded, 16)
                    sp.dma_start(rs_sb[:, :], D["RSB"][:, bass.ds(at, TB)]).then_inc(rs_loaded, 16)

                def block_loads(b, last):
                    q4 = b * (SLABS // 4)
                    for k in range(4):
                        slab(q4, O_AT + k, w_out[:, :, k * P:(k + 1) * P])
                    at = b * TB if isinstance(b, int) else sp.snap(b * TB)
                    turned = 8 * b + 1 if isinstance(b, int) else sp.snap(8 * b + 1)
                    sp.wait_ge(st_turned, 1)
                    wait_apart(sp, y_turned, turned)
                    sp.dma_start(h[:, :, :], XT[:, :, bass.ds(at, TB)]).then_inc(h_loaded, 16)
                    sp.dma_start(p_raw[:, :, :], PT[:, :, bass.ds(at, TB)]).then_inc(p_loaded, 16)
                    for k in range(4, 8):
                        slab(q4, O_AT + k, w_out[:, :, k * P:(k + 1) * P])
                    if not last:
                        used = sp.snap(8 * b + 8)
                        nxt = sp.snap(b * TB + TB)
                        wait_apart(sp, mix_lo, used)
                        load_mix(nxt)
                    with sp.Fori(0, NJ // 2) as jj:
                        for e in range(2):
                            for part in range(2):
                                n = sp.snap(part * NJ * P + (2 * jj + e) * P)
                                slab(q4 + jj, U_AT + 2 * e + part, w_up[:, :, bass.ds(n, P)])
                    for mt in range(8):
                        for r in range(3):
                            kt = (8 * r, min(8 * r + 8, NJ))
                            slab(q4, D_AT + 3 * mt + r, w_down[:, kt[0]:kt[1], mt * P:(mt + 1) * P])
                    for q in range(4):
                        for e in range(2):
                            slab(q4, P_AT + 3 * q + e, w_gate[:, :, (2 * q + e) * P:(2 * q + e + 1) * P])
                        slab(q4, P_AT + 3 * q + 2, w_proj[:, :, 2 * q * P:2 * (q + 1) * P])

                load_mix(0)
                sp.dma_start(state_raw, T["state_conv"][0].rearrange("b w f -> (b w) f")).then_inc(st_loaded, 16)
                with sp.Fori(0, NB - 1) as b:
                    block_loads(b, False)
                block_loads(NB - 1, True)
                sp.wait_ge(rows_copied, 6)
                sp.dma_start(T["conv_prompt"][0, 0], out_rows[0:2, :]).then_inc(rows_stored, 16)
                sp.dma_start(T["conv_sample"][0].rearrange("b w f -> (b w) f"), out_rows[2:18, :]).then_inc(rows_stored, 16)
                sp.wait_ge(rows_stored, 32)

            @block.gpsimd
            def _(pool):
                pool.sem_inc(lo_split, 4)
                nc.gpsimd.memset(carry[:, :, :], 0.0).then_inc(carry_zero, 1)
                with pool.Fori(0, NB * SLABS // 4) as q4:
                    for k in range(4):
                        pool.wait_ge(hi_split, 4 * q4 + k + 1)
                        nc.gpsimd.tensor_tensor(w_lo[k][:, :], raw[k][:, :], f32(w_hi[k][:, :]), ALU.subtract).then_inc(lo_split, 1)

            @block.tensor
            def _(pe):
                def tile_of(w, k, width=P):
                    return w[:, k * width:(k + 1) * width]

                def take(q4, k, units):
                    pe.wait_ge(lo_split, 4 * q4 + k + 5)
                    pe.wait_ge(acc_free, units)

                def mean_square(value):
                    pe.wait_ge(s_added, value)
                    nc.tensor.matmul(ps_sum[:, 0:TB], ones[0][:, :], ssum[:, :], start=True, stop=True).then_inc(sum_ready, 1)

                ones = [keep["mean1024"]]

                def product(q4, k, unit, mov_hi, mov_lo, order=range(8), ready=None):
                    for i, kt in enumerate(order):
                        if ready:
                            pe.wait_ge(ready[0], ready[1] + i + 1)
                        last = split_product(nc, acc[unit % 4][:, 0:TB], tile_of(w_hi[k % 4], kt), tile_of(w_lo[k % 4], kt),
                                             mov_hi[:, kt, :], mov_lo[:, kt, :], i == 0, i == 7)
                    last.then_inc(slab_done, 1)

                def block_products(b, last):
                    q4, u0 = b * (SLABS // 4), b * UNITS
                    for mt in range(8):
                        take(q4, O_AT + mt, u0 + OU + mt + 1)
                        product(q4, O_AT + mt, OU + mt, f_hi, f_lo, MIX_ORDER, (mix_lo, 8 * b) if mt == 0 else None)

                    def up_pair(q4, u, first=False):
                        for n in range(4):
                            take(q4, U_AT + n, u + UU + n + 1)
                            product(q4, U_AT + n, UU + n, x_hi, x_lo, ready=(xlo_done, 16 * b) if first and n == 0 else None)
                            if first and n == 0:
                                mean_square(21 * b + 7)

                    up_pair(q4, u0, True)
                    with pe.Fori(1, NJ // 2) as jj:
                        up_pair(q4 + jj, u0 + 4 * jj)
                    for mt in range(8):
                        for r in range(3):
                            if r == 0:
                                take(q4, D_AT + 3 * mt, u0 + DU + mt + 1)
                            else:
                                pe.wait_ge(lo_split, 4 * q4 + D_AT + 3 * mt + r + 5)
                            if mt == 0:
                                pe.wait_ge(flo_done, NJ * b + (NJ - 1 if r < 2 else NJ))
                            for kt in range(8 * r, min(8 * r + 8, NJ)):
                                k = (D_AT + 3 * mt + r) % 4
                                done = split_product(nc, acc[(DU + mt) % 4][:, 0:TB], tile_of(w_hi[k], kt % 8), tile_of(w_lo[k], kt % 8),
                                                     f_hi[:, kt, :], f_lo[:, kt, :], kt == 0, kt == NJ - 1)
                            done.then_inc(slab_done, 1)
                    for q in range(4):
                        for e in range(2):
                            take(q4, P_AT + 3 * q + e, u0 + PU + 4 * q + e + 1)
                            product(q4, P_AT + 3 * q + e, PU + 4 * q + e, x_hi, x_lo, ready=(xlo_done, 16 * b + 8) if q + e == 0 else None)
                            if q + e == 0:
                                mean_square(21 * b + 14)
                        take(q4, P_AT + 3 * q + 2, u0 + PU + 4 * q + 4)
                        if q == 0:
                            pe.wait_ge(p_lo, b + 1)
                        k = (P_AT + 3 * q + 2) % 4
                        for e in range(2):
                            for kt in range(2):
                                at = kt * 2 * P + e * P
                                done = split_product(nc, acc[(PU + 4 * q + 2 + e) % 4][:, 0:TB], w_hi[k][:, at:at + P], w_lo[k][:, at:at + P],
                                                     f_hi[:, kt, :], f_lo[:, kt, :], kt == 0, kt == 1)
                        done.then_inc(slab_done, 1)
                    mean_square(21 * b + 21)
                    for tt in range(4):
                        w = P if tt < 3 else 32
                        for half in range(2):
                            n = 2 * tt + half
                            pe.wait_ge(y_ready, 8 * b + 4 * half + 4)
                            pe.wait_ge(y_copied, 8 * b + n + 1)
                            for k in range(4):
                                done = nc.tensor.transpose(ps_t[half][0:w, k * P:(k + 1) * P],
                                                           h[:, 4 * half + k, tt * P:tt * P + w], keep["ident"][:, :])
                            done.then_inc(y_turned, 1)

                pe.sem_inc(slab_done, 2)
                pe.sem_inc(y_turned, 1)
                pe.wait_ge(st_loaded, 16)
                for j in range(NJ):
                    done = nc.tensor.transpose(ps_t[0][:, 16 * j:16 * j + 16], state_raw[:, j * P:(j + 1) * P], keep["ident"][0:16, 0:16])
                done.then_inc(st_turned, 1)
                with pe.Fori(0, NB - 1) as b:
                    block_products(b, False)
                block_products(NB - 1, True)
                for n in range(6):
                    if n < 2:
                        pe.wait_ge(y_copied, 8 * NB + n + 1)
                    else:
                        pe.wait_ge(rows_copied, n - 1)
                    for j in range(4 * n, min(4 * n + 4, NJ)):
                        done = nc.tensor.transpose(ps_t[n % 2][0:18, (j % 4) * P:(j % 4 + 1) * P], last_rows[:, j, :], keep["ident"][:, :])
                    done.then_inc(rows_turned, 1)

            @block.scalar
            def _(act):
                def square(b, norm, mt, ready, value):
                    act.wait_ge(ready, value)
                    if mt >= 2:
                        act.wait_ge(s_added, 21 * b + 7 * norm + mt - 1)
                    nc.scalar.activation((ssum if mt == 0 else sq)[:, :], h[:, mt, :], ACT.Square).then_inc(sq_done, 1)

                def root(b, norm):
                    act.wait_ge(sum_ready, 3 * b + norm + 1)
                    nc.scalar.activation(rs[:, :], ps_sum[:, 0:TB], ACT.Sqrt, bias=keep["eps"][:, :]).then_inc(rms_done, 1)

                def residual(b, norm, mt, unit, gain):
                    square(b, norm, mt, acc_free, UNITS * b + unit + mt + 5)
                    nc.scalar.activation(x_hi[:, mt, :], h[:, mt, :], ACT.Copy, scale=col(gain + mt)).then_inc(xhi_done, 1)

                def block_acts(b, last):
                    act.wait_ge(mix_loaded, 16 * b + 16)
                    for i, kt in enumerate(MIX_ORDER):
                        if kt < 4:
                            act.wait_ge(mix_scaled, 4 * b + kt + 1)
                            nc.scalar.activation(f_hi[:, kt, :], mix[:, kt, :], ACT.Copy).then_inc(mix_hi, 1)
                        else:
                            nc.scalar.activation(f_hi[:, kt, :], mix[:, kt, :], ACT.Copy, scale=col(G_OUT + kt)).then_inc(mix_hi, 1)
                    for mt in range(8):
                        residual(b, 0, mt, OU, G_FFN)
                    root(b, 0)
                    steps = (STEPS * (NB - 1) * NJ) if last else STEPS * NJ * b
                    per = STEPS_LAST if last else STEPS

                    with act.Fori(0, NJ // 2) as jj:
                        for e in range(2):
                            j = 2 * jj + e
                            wait_apart(act, conv_step, steps + per * (j + 1))
                            nc.scalar.activation(c[e][:, 0:TB], c[e][:, 0:TB], ACT.Gelu_apprx_tanh, bias=col(CONV_B0 + j)).then_inc(gelu_done, 1)
                            wait_apart(act, f_ready, NJ * b + j + 1)
                            nc.scalar.activation(f_hi[:, bass.ds(j, 1), :], u[e][:, 0:TB].unsqueeze(1), ACT.Copy).then_inc(fhi_done, 1)
                    for mt in range(8):
                        residual(b, 1, mt, DU, G_PLE)
                    root(b, 1)
                    for q in range(4):
                        for e in range(2):
                            act.wait_ge(acc_free, UNITS * b + PU + 4 * q + e + 5)
                            nc.scalar.activation(c[e][:, 0:TB], c[e][:, 0:TB], ACT.Sigmoid).then_inc(sig_done, 1)
                        for e in range(2):
                            square(b, 2, 2 * q + e, h_ready, 8 * b + 2 * q + e + 1)
                    root(b, 2)
                    at = b * TB if isinstance(b, int) else act.snap(b * TB)
                    for tt in range(4):
                        w = P if tt < 3 else 32
                        for half in range(2):
                            n = 2 * tt + half
                            act.wait_ge(y_turned, 8 * b + n + 2)
                            act.wait_ge(y_stored[n % 4], 32 * b + 16 * (n // 4) + 16)
                            nc.scalar.activation(y[n % 4][0:w, :], ps_t[half][0:w, :], ACT.Copy).then_inc(y_copied, 1)
                            act.wait_ge(y_copied, 8 * b + n + 3)
                            cols = slice(half * BANK, (half + 1) * BANK)
                            dst = (T["y_sample"].rearrange("b t d -> (b t) d")[:, cols] if last and tt == 3 else
                                   T["y_prompt"][0][bass.ds(at + tt * P, w), cols])
                            act.dma_start(dst, y[n % 4][0:w, :]).then_inc(y_stored[n % 4], 16)

                for n in range(4):
                    act.sem_inc(y_stored[n], 16)
                act.sem_inc(y_copied, 2)
                with act.Fori(0, NB - 1) as b:
                    block_acts(b, False)
                block_acts(NB - 1, True)
                for n in range(6):
                    w = min(4, NJ - 4 * n) * P
                    act.wait_ge(rows_turned, n + 1)
                    nc.scalar.activation(out_rows[:, n * BANK:n * BANK + w], ps_t[n % 2][0:18, 0:w], ACT.Copy).then_inc(rows_copied, 1)
                for n in range(4):
                    act.wait_ge(y_stored[n], 32 * NB + 16)

            @block.vector
            def _(dve):
                def split(q4, k, start=False):
                    dve.wait_ge(raw_loaded[k % 4], 16 * (q4 + k // 4 + 1))
                    if not start:
                        dve.wait_ge(slab_done, 4 * q4 + k - 1)
                    nc.vector.tensor_copy(w_hi[k % 4][:, :], raw[k % 4][:, :]).then_inc(hi_split, 1)

                def done(q4, k):
                    dve.wait_ge(slab_done, 4 * q4 + k + 3)

                def mult(out, a, b):
                    return nc.vector.tensor_tensor(out, a, b, ALU.mult)

                def copy(out, a):
                    return nc.vector.tensor_scalar(out, a, 1.0, None, ALU.mult)

                def add_square(b, norm, mt):
                    if mt:
                        dve.wait_ge(sq_done, 24 * b + 8 * norm + mt + 1)
                        if mt >= 2:
                            dve.wait_ge(s_added, 21 * b + 7 * norm + mt - 1)
                        nc.vector.tensor_tensor(ssum[:, :], ssum[:, :], sq[:, :], ALU.add).then_inc(s_added, 1)

                def residual(b, norm, mt, unit, gain):
                    nc.vector.tensor_tensor(h[:, mt, :], acc[(unit + mt) % 4][:, 0:TB], h[:, mt, :], ALU.add).then_inc(acc_free, 1)
                    dve.wait_ge(xhi_done, 16 * b + 8 * norm + mt + 1)
                    nc.vector.scalar_tensor_tensor(x_lo[:, mt, :], h[:, mt, :], col(gain + mt), f32(x_hi[:, mt, :]),
                                                   ALU.mult, ALU.subtract).then_inc(xlo_done, 1)
                    add_square(b, norm, mt)

                def inverse(b, norm):
                    dve.wait_ge(rms_done, 3 * b + norm + 1)
                    nc.vector.reciprocal(rs[:, :], rs[:, :]).then_inc(rs_done, 1)
                    dve.wait_ge(rs_done, 3 * b + norm + 1)

                def block_steps(b, last):
                    q4 = b * (SLABS // 4)
                    dve.wait_ge(mix_loaded, 16 * b + 16)
                    dve.wait_ge(rs_loaded, 16 * b + 16)
                    for kt in range(4):
                        nc.vector.scalar_tensor_tensor(mix[:, kt, :], mix[:, kt, :], col(G_OUT + kt), rs_sb[:, :],
                                                       ALU.mult, ALU.mult).then_inc(mix_scaled, 1)
                        dve.wait_ge(mix_hi, 8 * b + kt + 1)
                        nc.vector.scalar_tensor_tensor(f_lo[:, 4 + kt, :], mix[:, 4 + kt, :], col(G_OUT + 4 + kt), f32(f_hi[:, 4 + kt, :]),
                                                       ALU.mult, ALU.subtract).then_inc(mix_lo, 1)
                    for kt in range(4):
                        dve.wait_ge(mix_hi, 8 * b + kt + 5)
                        nc.vector.tensor_tensor(f_lo[:, kt, :], mix[:, kt, :], f32(f_hi[:, kt, :]), ALU.subtract).then_inc(mix_lo, 1)
                    dve.wait_ge(h_loaded, 16 * b + 16)
                    for mt in range(8):
                        split(q4, O_AT + mt + 2)
                        done(q4, O_AT + mt)
                        residual(b, 0, mt, OU, G_FFN)

                    steps = (STEPS * (NB - 1) * NJ) if last else STEPS * NJ * b
                    per = STEPS_LAST if last else STEPS

                    def conv(out, src, width, base, start):
                        win = (lambda n: src[:, n:n + width]) if width != 4 else (lambda n: src[:, :, n:n + 4])
                        dve.wait_ge(conv_step, base + start)
                        nc.vector.tensor_scalar(out, win(0), col(CONV_W0 + jcol[0]), None, ALU.mult).then_inc(conv_step, 1)
                        for tap in (1, 2):
                            dve.wait_ge(conv_step, base + start + tap)
                            nc.vector.scalar_tensor_tensor(out, win(tap), col(CONV_W0 + NJ * tap + jcol[0]), out,
                                                           ALU.mult, ALU.add).then_inc(conv_step, 1)

                    jcol = [None]

                    def up_pair(q4, jj, first=False):
                        for e in range(2):
                            j = 2 * jj + e
                            jcol[0] = j
                            base = steps + per * j
                            split(q4, U_AT + 2 * e + 2)
                            if first and e == 0:
                                inverse(b, 0)
                                for n in range(4):
                                    dve.wait_ge(y_stored[n], 32 * b + 16)
                            done(q4, U_AT + 2 * e)
                            copy(gate[:, 0:2], carry[:, bass.ds(j, 1), :].rearrange("p a t -> p (a t)")).then_inc(conv_step, 1)
                            g_acc = acc[(UU + 2 * e) % 4]
                            if not last:
                                mult(gate[:, 2:TB + 2], g_acc[:, 0:TB], rs[:, :]).then_inc(acc_free, 1)
                                dve.wait_ge(acc_free, UNITS * b + UU + 2 * j + 5)
                                copy(carry[:, bass.ds(j, 1), :].rearrange("p a t -> p (a t)"), gate[:, TB:TB + 2])\
                                    .then_inc(conv_step, 1)
                                conv(c[e][:, 0:TB], gate, TB, base, 2)
                            else:
                                tp = TB - 32
                                copy(gate_s[:, :, 0:2], state[:, bass.ds(j, 1), :].rearrange("p a (b w) -> p (a b) w", w=2))\
                                    .then_inc(conv_step, 1)
                                mult(gate[:, 2:tp + 2], g_acc[:, 0:tp], rs[:, 0:tp]).then_inc(conv_step, 1)
                                mult(gate_s[:, :, 2:6], g_acc[:, tp:TB].rearrange("p (b t) -> p b t", b=8),
                                     rs[:, tp:TB].rearrange("p (b t) -> p b t", b=8)).then_inc(acc_free, 1)
                                dve.wait_ge(conv_step, base + 3)
                                dve.wait_ge(acc_free, UNITS * b + UU + 2 * j + 5)
                                copy(last_rows[:, bass.ds(j, 1), 0:2].rearrange("p a t -> p (a t)"), gate[:, tp:tp + 2])\
                                    .then_inc(conv_step, 1)
                                copy(last_rows[:, bass.ds(j, 1), 2:18].rearrange("p a (b w) -> p (a b) w", w=2),
                                                      gate_s[:, :, 4:6]).then_inc(conv_step, 1)
                                conv(c[e][:, 0:tp], gate, tp, base, 5)
                                conv(c[e][:, tp:TB].rearrange("p (b t) -> p b t", b=8), gate_s, 4, base, 8)
                            split(q4, U_AT + 2 * e + 3)
                            done(q4, U_AT + 2 * e + 1)
                            mult(u[e][:, 0:TB], acc[(UU + 2 * e + 1) % 4][:, 0:TB], rs[:, :]).then_inc(acc_free, 1)
                            dve.wait_ge(acc_free, UNITS * b + UU + 2 * j + 6)
                            dve.wait_ge(gelu_done, NJ * b + j + 1)
                            mult(u[e][:, 0:TB], u[e][:, 0:TB], c[e][:, 0:TB]).then_inc(f_ready, 1)
                            dve.wait_ge(fhi_done, NJ * b + j + 1)
                            nc.vector.tensor_tensor(f_lo[:, bass.ds(j, 1), :], u[e][:, 0:TB].unsqueeze(1), f32(f_hi[:, bass.ds(j, 1), :]),
                                                    ALU.subtract).then_inc(flo_done, 1)

                    up_pair(q4, 0, True)
                    with dve.Fori(1, NJ // 2) as jj:
                        up_pair(q4 + jj, jj)
                    for mt in range(8):
                        for r in range(3):
                            split(q4, D_AT + 3 * mt + r + 2)
                        done(q4, D_AT + 3 * mt + 2)
                        residual(b, 1, mt, DU, G_PLE)
                        if mt == 7:
                            dve.wait_ge(p_loaded, 16 * b + 16)
                            nc.vector.tensor_copy(f_hi[:, 0:2, :], p_raw[:, :, :]).then_inc(p_hi, 1)
                            dve.wait_ge(p_hi, b + 1)
                            nc.vector.tensor_tensor(f_lo[:, 0:2, :], p_raw[:, :, :], f32(f_hi[:, 0:2, :]), ALU.subtract).then_inc(p_lo, 1)
                    for q in range(4):
                        for e in range(2):
                            split(q4, P_AT + 3 * q + e + 2) if not (last and 3 * q + e + 2 >= 12) else None
                            if q + e == 0:
                                inverse(b, 1)
                            done(q4, P_AT + 3 * q + e)
                            mult(c[e][:, 0:TB], acc[(PU + 4 * q + e) % 4][:, 0:TB], rs[:, :]).then_inc(acc_free, 1)
                        if not (last and 3 * q + 4 >= 12):
                            split(q4, P_AT + 3 * q + 4)
                        done(q4, P_AT + 3 * q + 2)
                        for e in range(2):
                            mt = 2 * q + e
                            dve.wait_ge(sig_done, 8 * b + mt + 1)
                            mult(u[e][:, 0:TB], c[e][:, 0:TB], acc[(PU + 4 * q + 2 + e) % 4][:, 0:TB]).then_inc(acc_free, 1)
                            dve.wait_ge(acc_free, UNITS * b + PU + 4 * q + 2 + e + 5)
                            nc.vector.tensor_tensor(h[:, mt, :], h[:, mt, :], u[e][:, 0:TB], ALU.add).then_inc(h_ready, 1)
                            add_square(b, 2, mt)
                    inverse(b, 2)
                    for mt in range(8):
                        nc.vector.scalar_tensor_tensor(h[:, mt, :], h[:, mt, :], col(G_FIN + mt), rs[:, :], ALU.mult, ALU.mult)\
                            .then_inc(y_ready, 1)

                dve.sem_inc(acc_free, 4)
                dve.wait_ge(carry_zero, 1)
                dve.wait_ge(st_turned, 1)
                nc.vector.tensor_copy(state[:, :, :].rearrange("p j t -> p (j t)"), ps_t[0][:, 0:16 * NJ]).then_inc(st_ready, 1)
                for k in range(2):
                    split(0, k, True)
                with dve.Fori(0, NB - 1) as b:
                    block_steps(b, False)
                block_steps(NB - 1, True)


def program(nc, T, internal="Internal", phases=15):
    D = {n: nc.dram_tensor(n, s, F32, kind=internal).ap() for n, s in
         (("XT", (1024, 2080)), ("PT", (256, 2080)), ("MIXT", (1024, 2080)), ("QT", (512, 2048)), ("KT", (512, 2048)),
          ("RSB", (P, 2080)))}
    with ExitStack() as ctx:
        m = Alloc(nc, ctx, "keep")
        keep = {
            "ident": m.sb("ident", [P, P]), "mean1024": m.sb("mean1024", [P, P]), "mean512": m.sb("mean512", [P, P]),
            "eps": m.sb("eps", [P, 1]), "cols": m.sb("cols", [P, P]), "rs": m.sb("rs", [P, 17]),
            "page_table": m.sb("page_table", [1, P], I32), "sb_bias": m.sb("sb_bias", [P, 8]),
            "qT_s": m.sb("qT_s", [P, 4, 32]), "kT_s": m.sb("kT_s", [P, 4, 32]),
        }
        constants(nc, keep, T)
        if phases & 1:
            project_mlp(nc, keep, T, D)
            project_qk(nc, keep, T, D)
        if phases & 2:
            attend_prompt(nc, keep, T, D)
        if phases & 4:
            attend_sample(nc, keep, T, D)
        if phases & 8:
            finish_tokens(nc, keep, T, D)


_OUTS = (
    ("y_prompt", (1, 2048, 1024)), ("y_sample", (8, 4, 1024)),
    ("k_prompt", (1, 1, 2048, 8, 64)), ("v_prompt", (1, 1, 2048, 8, 64)),
    ("k_sample", (1, 8, 4, 8, 64)), ("v_sample", (1, 8, 4, 8, 64)),
    ("conv_prompt", (1, 1, 2, 2816)), ("conv_sample", (1, 8, 2, 2816)), ("mlp_v_sample", (1, 8, 4, 512)),
)


def kernel(**inputs):
    import numpy as np
    import concourse.bacc as bacc
    from concourse.bass_utils import run_bass_kernel_spmd

    nc = bacc.Bacc("TRN2", target_bir_lowering=False, num_devices=1)
    arrays, T = {}, {}
    for name, value in inputs.items():
        a = np.ascontiguousarray(value)
        arrays[f"in_{name}_dram"] = a
        T[name] = nc.dram_tensor(f"in_{name}_dram", a.shape, mybir.dt.from_np(a.dtype), kind="ExternalInput").ap()
    for name, shape in _OUTS:
        T[name] = nc.dram_tensor(f"out_{name}_dram", shape, F32, kind="ExternalOutput").ap()
    program(nc, T)
    got = run_bass_kernel_spmd(nc, [arrays], core_ids=[0]).results[0]
    return tuple(got[f"out_{name}_dram"] for name, _ in _OUTS)
```

```python
from contextlib import ExitStack

import concourse.bass as bass
from concourse import mybir

F32 = mybir.dt.float32
F32R = mybir.dt.float32r
I32 = mybir.dt.int32
ALU = mybir.AluOpType
ACT = mybir.ActivationFunctionType
AX = mybir.AxisListType

P = 128
BANK = 512
EPS = 1e-6
CHUNK_COLS = 512


class Alloc:

    def __init__(self, nc, ctx, phase):
        self.nc, self.ctx, self.phase, self.sems = nc, ctx, phase, []

    def sb(self, name, shape, dt=F32):
        return self.ctx.enter_context(self.nc.sbuf_tensor(f"{self.phase}_{name}", shape, dt))

    def bank(self, name, shape=(P, BANK)):
        return self.ctx.enter_context(self.nc.psum_tensor(f"{self.phase}_{name}", list(shape), F32))

    def sem(self, name):
        self.sems.append(self.nc.alloc_semaphore(name=f"{self.phase}_{name}"))
        return self.sems[-1]

    def free_sems(self):
        with self.nc.Block() as block:

            @block.gpsimd
            def _(pool):
                self.nc.clear_and_free_semaphores(self.sems)


def f32(ap):
    return ap.bitcast(F32)


def wait_apart(eng, sem, value):
    eng.wait_ge(sem, 1)
    eng.wait_ge(sem, value)


def split_product(nc, out, stat_hi, stat_lo, mov_hi, mov_lo, first, last):
    nc.tensor.matmul(out, stat_hi, mov_hi, start=first, stop=False)
    nc.tensor.matmul(out, stat_hi, mov_lo, start=False, stop=False)
    return nc.tensor.matmul(out, stat_lo, mov_hi, start=False, stop=last)


def constants(nc, keep, T):
    with ExitStack() as ctx:
        m = Alloc(nc, ctx, "const")
        rows = m.sb("rows", [P, P])
        ps = m.bank("ps")
        made, loaded, turned, copied = m.sem("made"), m.sem("loaded"), m.sem("turned"), m.sem("copied")
        with nc.Block() as block:

            @block.sync
            def _(sp):
                at = 0
                for name in ("norm_mix_g", "gn_sb", "gn_mlp", "norm_ffn_g", "norm_ple_g", "final_norm_g", "conv_w", "conv_b"):
                    v = T[name]
                    v = v if name == "final_norm_g" else v[0]
                    v = v.rearrange("j (k p) -> (j k) p", p=P) if name == "conv_w" else v.rearrange("(k p) -> k p", p=P)
                    n = v.shape[0]
                    sp.dma_start(rows[at:at + n, :], v).then_inc(loaded, 16)
                    at += n
                assert at == P
                sp.dma_start(keep["page_table"][0:1, :], T["page_table"].rearrange("b n -> (b n)").rearrange("(a n) -> a n", a=1)).then_inc(loaded, 16)
                sp.dma_start(keep["sb_bias"][:, :], T["sb_bias"][0:1, :].to_broadcast([P, 8])).then_inc(loaded, 16)
                sp.wait_ge(loaded, 16 * 10)

            @block.gpsimd
            def _(pool):
                nc.gpsimd.memset(keep["ident"][:, :], 1.0).then_inc(made, 1)
                pool.wait_ge(made, 1)
                nc.gpsimd.affine_select(out=keep["ident"][:, :], in_=keep["ident"][:, :], pattern=[[-1, P]],
                                        compare_op=ALU.is_equal, fill=0.0, base=0, channel_multiplier=1).then_inc(made, 1)
                nc.gpsimd.memset(keep["mean1024"][:, :], 1.0 / 1024)
                nc.gpsimd.memset(keep["mean512"][:, :], 1.0 / 512)
                nc.gpsimd.memset(keep["eps"][:, :], EPS)

            @block.tensor
            def _(pe):
                pe.wait_ge(loaded, 16 * 10)
                pe.wait_ge(made, 2)
                nc.tensor.transpose(ps[:, 0:P], rows[:, :], keep["ident"][:, :]).then_inc(turned, 1)

            @block.vector
            def _(dve):
                dve.wait_ge(turned, 1)
                nc.vector.tensor_copy(keep["cols"][:, :], ps[:, 0:P]).then_inc(copied, 1)


G_MIX, G_OUT, G_FFN, G_PLE, G_FIN, CONV_W0, CONV_B0 = 0, 8, 16, 24, 32, 40, 106


def project_mlp(nc, keep, T, D):
    NT = 17
    with ExitStack() as ctx:
        m = Alloc(nc, ctx, "pa")
        w_hi = m.sb("w_hi", [P, 8, 3 * BANK], F32R)
        w_lo = m.sb("w_lo", [P, 8, 3 * BANK], F32R)
        w_raw = [m.sb(f"w_raw{n}", [P, 4, BANK]) for n in range(2)]
        x_raw = [m.sb(f"x_raw{n}", [P, 1024]) for n in range(2)]
        p_raw = [m.sb(f"p_raw{n}", [P, 256]) for n in range(2)]
        xT = [m.sb(f"xT{n}", [P, 8, P]) for n in range(2)]
        x_hi = [m.sb(f"x_hi{n}", [P, 8, P], F32R) for n in range(2)]
        x_lo = [m.sb(f"x_lo{n}", [P, 8, P], F32R) for n in range(2)]
        pT = [m.sb(f"pT{n}", [P, 2, P]) for n in range(2)]
        vm = [m.sb(f"vm{n}", [P, BANK]) for n in range(2)]
        u = [m.sb(f"u{n}", [P, BANK]) for n in range(2)]
        v = [m.sb(f"v{n}", [P, BANK]) for n in range(2)]
        o = [m.sb(f"o{n}", [P, BANK]) for n in range(2)]
        oT = [m.sb(f"oT{n}", [P, 4, P]) for n in range(2)]
        ws = m.sb("ws", [P, 8, P])
        wsT = m.sb("wsT", [P, 8, P])
        wsT32 = m.sb("wsT32", [32, 8, 32])
        bs_raw = m.sb("bs_raw", [8, P])
        bs = m.sb("bs", [P, 8])
        bs32 = m.sb("bs32", [32, 8])
        x_sq = [m.sb(f"x_sq{n}", [P, 2]) for n in range(2)]
        x_ms = [m.sb(f"x_ms{n}", [P, 1]) for n in range(2)]
        x_rms = [m.sb(f"x_rms{n}", [P, 1]) for n in range(2)]
        x_rs = [m.sb(f"x_rs{n}", [P, 1]) for n in range(2)]
        o_sq = [m.sb(f"o_sq{n}", [P, 1]) for n in range(2)]
        o_rms = [m.sb(f"o_rms{n}", [P, 1]) for n in range(2)]
        o_rs = [m.sb(f"o_rs{n}", [P, 1]) for n in range(2)]
        ps_acc = [m.bank(f"ps_acc{n}") for n in range(2)]
        ps_x = m.bank("ps_x", (P, 2 * BANK))
        ps_p = m.bank("ps_p")
        ps_o = m.bank("ps_o")
        ps_mix = m.bank("ps_mix")
        ps_junk = m.bank("ps_junk")

        w_loaded = [m.sem(f"w_loaded{n}") for n in range(2)]
        w_hi_done, w_lo_done = m.sem("w_hi_done"), m.sem("w_lo_done")
        s_loaded, s_masked, s_turned, s_copied, s_zeroed, s_small = (
            m.sem(n) for n in ("s_loaded", "s_masked", "s_turned", "s_copied", "s_zeroed", "s_small"))
        x_loaded = [m.sem(f"x_loaded{n}") for n in range(2)]
        p_loaded = [m.sem(f"p_loaded{n}") for n in range(2)]
        x_turned, p_turned, acc_ready, mixed_ready, o_turned = (
            m.sem(n) for n in ("x_turned", "p_turned", "acc_ready", "mixed_ready", "o_turned"))
        sq_done, rms_done, xT_ready, vm_ready, u_ready, v_ready, osq_done = (
            m.sem(n) for n in ("sq_done", "rms_done", "xT_ready", "vm_ready", "u_ready", "v_ready", "osq_done"))
        hi_ready, lo_ready, pT_ready, ms_done, rs_ready, gated, o_rs_done, o_ready, oT_ready = (
            m.sem(n) for n in ("hi_ready", "lo_ready", "pT_ready", "ms_done", "rs_ready", "gated", "o_rs_done", "o_ready", "oT_ready"))
        xT_stored = [m.sem(f"xT_stored{n}") for n in range(2)]
        pT_stored = [m.sem(f"pT_stored{n}") for n in range(2)]
        oT_stored = [m.sem(f"oT_stored{n}") for n in range(2)]
        v_stored = [m.sem(f"v_stored{n}") for n in range(2)]
        vm_stored = m.sem("vm_stored")

        x_src, p_src = T["x_prompt"][0], T["p_prompt"][0, 0]
        xs_src, ps_src = T["x_sample"].rearrange("b t d -> (b t) d"), T["p_sample"][0].rearrange("b t d -> (b t) d")
        XT, PT, MIXT = (D[n].rearrange("(k p) t -> p k t", p=P) for n in ("XT", "PT", "MIXT"))
        v_out = T["v_prompt"][0, 0].rearrange("t h d -> t (h d)")
        vs_out = T["v_sample"][0].rearrange("b t h d -> (b t) (h d)")
        w_in = T["w_in"][0].rearrange("(k p) n -> p k n", p=P)
        COLS = (2048, 1536, 1024)

        with nc.Block() as block:

            @block.sync
            def _(sp):
                def load(at, s):
                    rows = P if at is not None else 32
                    a = x_src[bass.ds(at, P), :] if at is not None else xs_src
                    b = p_src[bass.ds(at, P), :] if at is not None else ps_src
                    sp.dma_start(x_raw[s][0:rows, :], a).then_inc(x_loaded[s], 16)
                    sp.dma_start(p_raw[s][0:rows, :], b).then_inc(p_loaded[s], 16)

                def store_turned(count, at, s, rows=P):
                    at = bass.ds(at, rows)
                    wait_apart(sp, xT_ready, count)
                    sp.dma_start(XT[:, :, at], xT[s][:, :, 0:rows]).then_inc(xT_stored[s], 16)
                    sp.wait_ge(pT_ready, count)
                    sp.dma_start(PT[:, :, at], pT[s][:, :, 0:rows]).then_inc(pT_stored[s], 16)

                def store_o(count, at, s, rows=P):
                    sp.wait_ge(oT_ready, count)
                    sp.dma_start(MIXT[:, 4:8, bass.ds(at, rows)], oT[s][:, :, 0:rows]).then_inc(oT_stored[s], 16)

                load(0, 0)
                for c in range(3):
                    for half in range(2):
                        n = 2 * c + half
                        if n >= 2:
                            sp.wait_ge(w_lo_done, 4 * (n - 1))
                        sp.dma_start(w_raw[n % 2][:, :, :],
                                     w_in[:, 4 * half:4 * half + 4, COLS[c]:COLS[c] + BANK]).then_inc(w_loaded[n % 2], 16)
                    if c == 0:
                        sp.dma_start(ws[:, :, :], T["w_spatial"][0].rearrange("g t s -> t g s")).then_inc(s_loaded, 16)
                        sp.dma_start(bs_raw[:, :], T["b_spatial"][0]).then_inc(s_loaded, 16)
                        load(P, 1)
                store_turned(1, 0, 0)
                sp.wait_ge(s_copied, 3)
                sp.wait_ge(s_zeroed, 1)
                for b in range(8):
                    sp.dma_start(wsT32[4 * b:4 * b + 4, :, 4 * b:4 * b + 4], wsT[0:4, :, 0:4]).then_inc(s_small, 16)
                    sp.dma_start(bs32[4 * b:4 * b + 4, :], bs[0:4, :]).then_inc(s_small, 16)
                with sp.Fori(0, 7) as i:
                    for s in range(2):
                        t = 2 * i + s
                        at, at1, at2 = t * P, (t + 1) * P, (t + 2) * P
                        one, two, squares = sp.snap(t + 1), sp.snap(t + 2), sp.snap(2 * t + 2)
                        sp.wait_ge(x_turned, one)
                        sp.wait_ge(p_turned, one)
                        sp.wait_ge(sq_done, squares)
                        load(at2, s)
                        store_turned(two, at1, 1 - s)
                        store_o(one, at, s)
                sp.wait_ge(x_turned, 15)
                sp.wait_ge(p_turned, 15)
                sp.wait_ge(sq_done, 30)
                load(None, 0)
                store_turned(16, 15 * P, 1)
                store_o(15, 14 * P, 0)
                store_turned(17, 16 * P, 0, 32)
                store_o(16, 15 * P, 1)
                sp.wait_ge(vm_ready, 17)
                sp.dma_start(T["mlp_v_sample"][0].rearrange("b t d -> (b t) d"), vm[0][0:32, :]).then_inc(vm_stored, 16)
                store_o(17, 16 * P, 0, 32)
                sp.wait_ge(vm_stored, 16)
                for sems in (xT_stored, pT_stored, oT_stored):
                    sp.wait_ge(sems[0], 16 * 9)
                    sp.wait_ge(sems[1], 16 * 8)
                sp.wait_ge(s_small, 16 * 16)

            @block.gpsimd
            def _(pool):
                nc.gpsimd.memset(wsT32[:, :, :], 0.0).then_inc(s_zeroed, 1)
                pool.wait_ge(s_loaded, 32)
                nc.gpsimd.affine_select(out=ws[:, :, :], in_=ws[:, :, :], pattern=[[0, 8], [-1, P]], compare_op=ALU.is_ge,
                                        fill=0.0, base=0, channel_multiplier=1).then_inc(s_masked, 1)

            @block.tensor
            def _(pe):
                def turn_x(s, loads):
                    pe.wait_ge(x_loaded[s], 16 * loads)
                    for k in range(8):
                        last = nc.tensor.transpose(ps_x[:, k * P:(k + 1) * P], x_raw[s][:, k * P:(k + 1) * P], keep["ident"][:, :])
                    last.then_inc(x_turned, 1)
                    pe.wait_ge(p_loaded[s], 16 * loads)
                    for k in range(2):
                        last = nc.tensor.transpose(ps_p[:, k * P:(k + 1) * P], p_raw[s][:, k * P:(k + 1) * P], keep["ident"][:, :])
                    last.then_inc(p_turned, 1)

                def project(t, s, c, tile0=False):
                    for k in range(8):
                        if tile0 and k % 4 == 0:
                            pe.wait_ge(w_lo_done, 8 * c + k + 4)
                        last = split_product(nc, ps_acc[(3 * s + c) % 2][:, :], x_hi[s][:, k, :], x_lo[s][:, k, :],
                                             w_hi[:, k, c * BANK:(c + 1) * BANK], w_lo[:, k, c * BANK:(c + 1) * BANK],
                                             k == 0, k == 7)
                    last.then_inc(acc_ready, 1)

                def tile(t, s, next_loads, rows=P, first=False):
                    pe.wait_ge(lo_ready, t + 1)
                    pe.wait_ge(u_ready, t + 1)
                    project(t, s, 0, first)
                    if next_loads is not None:
                        pe.wait_ge(xT_ready, t + 1)
                        pe.wait_ge(pT_ready, t + 1)
                        turn_x(1 - s, next_loads)
                    if first:
                        pe.wait_ge(s_copied, 3)
                    pe.wait_ge(v_ready, t + 1)
                    project(t, s, 1, first)
                    pe.wait_ge(vm_ready, t + 1)
                    if not first:
                        pe.wait_ge(gated, 2 * t)
                    w = wsT if rows == P else wsT32
                    if rows != P:
                        pe.wait_ge(s_small, 16 * 16)
                    for g in range(8):
                        last = nc.tensor.matmul(ps_mix[0:rows, g * 64:g * 64 + 64], w[0:rows, g, 0:rows],
                                                vm[s][0:rows, g * 64:g * 64 + 64], start=True, stop=True)
                    last.then_inc(mixed_ready, 1)
                    project(t, s, 2, first)
                    pe.wait_ge(o_ready, t + 1)
                    if not first:
                        pe.wait_ge(oT_ready, t)
                    for k in range(4):
                        last = nc.tensor.transpose(ps_o[:, k * P:k * P + rows], o[s][0:rows, k * P:(k + 1) * P],
                                                   keep["ident"][0:rows, 0:rows])
                    last.then_inc(o_turned, 1)

                turn_x(0, 1)
                pe.wait_ge(s_masked, 1)
                for half in range(2):
                    for g in range(4):
                        last = nc.tensor.transpose((ps_mix, ps_o)[half][:, g * P:(g + 1) * P], ws[:, 4 * half + g, :], keep["ident"][:, :])
                    last.then_inc(s_turned, 1)
                nc.tensor.transpose(ps_acc[1][:, 0:8], bs_raw[:, :], keep["ident"][0:8, 0:8]).then_inc(s_turned, 1)
                tile(0, 0, 1, first=True)
                tile(1, 1, 2)
                with pe.Fori(1, 7) as i:
                    tile(2 * i, 0, i + 1)
                    tile(2 * i + 1, 1, i + 2)
                tile(14, 0, 8)
                tile(15, 1, 9)
                tile(16, 0, None, 32)

            @block.scalar
            def _(act):
                def prepare(t, s, loads, first=False):
                    act.wait_ge(x_loaded[s], 16 * loads)
                    for half in range(2):
                        if not first or half:
                            act.wait_ge(sq_done, 2 * t + half)
                        nc.scalar.activation(ps_junk[:, :], x_raw[s][:, half * BANK:(half + 1) * BANK], ACT.Square,
                                             accum_out=x_sq[s][:, half:half + 1]).then_inc(sq_done, 1)
                    act.wait_ge(x_turned, t + 1)
                    if not (isinstance(loads, int) and loads == 1):
                        act.wait_ge(xT_stored[s], 16 * (loads - 1))
                    nc.scalar.activation(xT[s][:, :, :].rearrange("p k t -> p (k t)"), ps_x[:, :], ACT.Copy).then_inc(xT_ready, 1)

                def root_x(t, s):
                    act.wait_ge(ms_done, t + 1)
                    nc.scalar.activation(x_rms[s][:, :], x_ms[s][:, :], ACT.Sqrt, bias=keep["eps"][:, :], scale=1.0 / 1024)\
                        .then_inc(rms_done, 1)

                def tile(t, s, next_loads, v_stores, rows=P):
                    scale = x_rs[s][:, :]
                    at = t * P if isinstance(t, int) else act.snap(t * P)
                    act.wait_ge(rs_ready, t + 1)
                    act.wait_ge(acc_ready, 3 * t + 1)
                    nc.scalar.activation(vm[s][:, :], ps_acc[(3 * s) % 2][:, :], ACT.Gelu_apprx_tanh, scale=scale).then_inc(vm_ready, 1)
                    if next_loads is not None:
                        prepare(t + 1, 1 - s, next_loads)
                    act.wait_ge(acc_ready, 3 * t + 2)
                    nc.scalar.activation(u[s][:, :], ps_acc[(3 * s + 1) % 2][:, :], ACT.Gelu_apprx_tanh, scale=scale).then_inc(u_ready, 1)
                    act.wait_ge(gated, 2 * t + 2)
                    nc.scalar.activation(ps_junk[0:rows, :], o[s][0:rows, :], ACT.Square, accum_out=o_sq[s][0:rows, :]).then_inc(osq_done, 1)
                    act.wait_ge(osq_done, t + 1)
                    nc.scalar.activation(o_rms[s][0:rows, :], o_sq[s][0:rows, :], ACT.Sqrt, bias=keep["eps"][0:rows, :],
                                         scale=1.0 / 512).then_inc(rms_done, 1)
                    if next_loads is not None:
                        root_x(t + 1, 1 - s)
                    act.wait_ge(acc_ready, 3 * t + 3)
                    if v_stores is not None:
                        act.wait_ge(v_stored[s], 16 * v_stores)
                    nc.scalar.activation(v[s][:, :], ps_acc[(3 * s + 2) % 2][:, :], ACT.Copy, scale=scale).then_inc(v_ready, 1)
                    act.wait_ge(v_ready, t + 2)
                    dst = v_out[bass.ds(at, P), :] if rows == P else vs_out
                    act.dma_start(dst, v[s][0:rows, :]).then_inc(v_stored[s], 16)

                act.sem_inc(u_ready, 1)
                act.sem_inc(v_ready, 1)
                prepare(0, 0, 1, first=True)
                root_x(0, 0)
                for c in range(3):
                    for k in range(8):
                        n = 2 * c + k // 4
                        if k % 4 == 0:
                            act.wait_ge(w_loaded[n % 2], 16 * (n // 2 + 1))
                        nc.scalar.activation(w_hi[:, k, c * BANK:(c + 1) * BANK], w_raw[n % 2][:, k % 4, :], ACT.Copy,
                                             scale=keep["cols"][:, G_MIX + k:G_MIX + k + 1]).then_inc(w_hi_done, 1)
                tile(0, 0, 1, None)
                tile(1, 1, 2, None)
                with act.Fori(1, 7) as i:
                    tile(2 * i, 0, i + 1, i)
                    tile(2 * i + 1, 1, i + 2, i)
                tile(14, 0, 8, 7)
                tile(15, 1, 9, 7)
                tile(16, 0, None, 8, 32)
                act.wait_ge(v_stored[0], 16 * 9)
                act.wait_ge(v_stored[1], 16 * 8)

            @block.vector
            def _(dve):
                def mean_square(t, s):
                    dve.wait_ge(sq_done, 2 * t + 2)
                    nc.vector.tensor_tensor(x_ms[s][:, :], x_sq[s][:, 0:1], x_sq[s][:, 1:2], ALU.add).then_inc(ms_done, 1)

                def invert_x(t, s):
                    nc.vector.reciprocal(x_rs[s][:, :], x_rms[s][:, :]).then_inc(rs_ready, 1)
                    dve.wait_ge(rs_ready, t + 1)
                    nc.vector.tensor_scalar(keep["rs"][:, bass.ds(t, 1)], x_rs[s][:, :], 1.0, None, ALU.mult)

                def split_x(t, s):
                    dve.wait_ge(xT_ready, t + 1)
                    nc.vector.tensor_copy(x_hi[s][:, :, :], xT[s][:, :, :]).then_inc(hi_ready, 1)
                    dve.wait_ge(hi_ready, t + 1)
                    nc.vector.tensor_tensor(x_lo[s][:, :, :], xT[s][:, :, :], f32(x_hi[s][:, :, :]), ALU.subtract).then_inc(lo_ready, 1)

                def copy_p(t, s, stores):
                    dve.wait_ge(p_turned, t + 1)
                    if stores is not None:
                        dve.wait_ge(pT_stored[s], 16 * stores)
                    nc.vector.tensor_copy(pT[s][:, :, :].rearrange("p k t -> p (k t)"), ps_p[:, 0:2 * P]).then_inc(pT_ready, 1)

                def tile(t, s, nxt, stores, stores_next, rows=P):
                    if nxt:
                        mean_square(t + 1, 1 - s)
                        split_x(t + 1, 1 - s)
                        copy_p(t + 1, 1 - s, stores_next)
                    b = bs if rows == P else bs32
                    dve.wait_ge(mixed_ready, t + 1)
                    nc.vector.tensor_tensor(
                        o[s][0:rows, :].rearrange("p (g d) -> p g d", g=8), ps_mix[0:rows, :].rearrange("p (g d) -> p g d", g=8),
                        b[0:rows, :].unsqueeze(2).to_broadcast([rows, 8, 64]), ALU.add).then_inc(gated, 1)
                    dve.wait_ge(gated, 2 * t + 1)
                    dve.wait_ge(u_ready, t + 2)
                    nc.vector.tensor_tensor(o[s][0:rows, :], o[s][0:rows, :], u[s][0:rows, :], ALU.mult).then_inc(gated, 1)
                    dve.wait_ge(rms_done, 2 * t + 2)
                    nc.vector.reciprocal(o_rs[s][0:rows, :], o_rms[s][0:rows, :]).then_inc(o_rs_done, 1)
                    dve.wait_ge(o_rs_done, t + 1)
                    nc.vector.tensor_scalar(o[s][0:rows, :], o[s][0:rows, :], o_rs[s][0:rows, :], None, ALU.mult).then_inc(o_ready, 1)
                    if nxt:
                        dve.wait_ge(rms_done, 2 * t + 3)
                        invert_x(t + 1, 1 - s)
                    dve.wait_ge(o_turned, t + 1)
                    if stores is not None:
                        dve.wait_ge(oT_stored[s], 16 * stores)
                    if rows == P:
                        nc.vector.tensor_copy(oT[s][:, :, :].rearrange("p k t -> p (k t)"), ps_o[:, :]).then_inc(oT_ready, 1)
                    else:
                        nc.vector.tensor_copy(oT[s][:, :, 0:rows], ps_o[:, :].rearrange("p (k t) -> p k t", k=4)[:, :, 0:rows])\
                            .then_inc(oT_ready, 1)

                mean_square(0, 0)
                split_x(0, 0)
                copy_p(0, 0, None)
                dve.wait_ge(rms_done, 1)
                invert_x(0, 0)
                for c in range(3):
                    for k in range(8):
                        n = 2 * c + k // 4
                        dve.wait_ge(w_hi_done, 8 * c + k + 1)
                        nc.vector.scalar_tensor_tensor(
                            w_lo[:, k, c * BANK:(c + 1) * BANK], w_raw[n % 2][:, k % 4, :], keep["cols"][:, G_MIX + k:G_MIX + k + 1],
                            f32(w_hi[:, k, c * BANK:(c + 1) * BANK]), ALU.mult, ALU.subtract).then_inc(w_lo_done, 1)
                    if c == 0:
                        dve.wait_ge(s_turned, 3)
                        nc.vector.tensor_copy(wsT[:, 0:4, :].rearrange("p g t -> p (g t)"), ps_mix[:, :]).then_inc(s_copied, 1)
                        nc.vector.tensor_copy(wsT[:, 4:8, :].rearrange("p g t -> p (g t)"), ps_o[:, :]).then_inc(s_copied, 1)
                        nc.vector.tensor_copy(bs[:, :], ps_acc[1][:, 0:8]).then_inc(s_copied, 1)
                tile(0, 0, True, None, None)
                tile(1, 1, True, None, 1)
                with dve.Fori(1, 7) as i:
                    tile(2 * i, 0, True, i, i)
                    tile(2 * i + 1, 1, True, i, i + 1)
                tile(14, 0, True, 7, 7)
                tile(15, 1, True, 7, 8)
                tile(16, 0, False, 8, None, 32)
        m.free_sems()


def project_qk(nc, keep, T, D):
    with ExitStack() as ctx:
        m = Alloc(nc, ctx, "pb")
        w_hi = m.sb("w_hi", [P, 8, 2 * BANK], F32R)
        w_lo = m.sb("w_lo", [P, 8, 2 * BANK], F32R)
        w_raw = [m.sb(f"w_raw{n}", [P, 4, BANK]) for n in range(4)]
        xT = [m.sb(f"xT{n}", [P, 8, P]) for n in range(2)]
        x_hi = [m.sb(f"x_hi{n}", [P, 8, P], F32R) for n in range(2)]
        x_lo = [m.sb(f"x_lo{n}", [P, 8, P], F32R) for n in range(2)]
        x_rs = [m.sb(f"x_rs{n}", [P, 2]) for n in range(2)]
        k = [m.sb(f"k{n}", [P, BANK]) for n in range(2)]
        q = [m.sb(f"q{n}", [P, BANK]) for n in range(2)]
        kT = [m.sb(f"kT{n}", [P, 4, P]) for n in range(2)]
        qT = [m.sb(f"qT{n}", [P, 4, P]) for n in range(2)]
        ps_k, ps_q, ps_kT, ps_qT = (m.bank(n) for n in ("ps_k", "ps_q", "ps_kT", "ps_qT"))

        w_loaded = [m.sem(f"w_loaded{n}") for n in range(4)]
        w_hi_done, w_lo_done, rs_done, hi_ready, lo_ready, k_proj, q_proj, k_ready, q_ready, k_turned, q_turned, kT_ready, qT_ready = (
            m.sem(n) for n in ("w_hi_done", "w_lo_done", "rs_done", "hi_ready", "lo_ready", "k_proj", "q_proj", "k_ready", "q_ready",
                               "k_turned", "q_turned", "kT_ready", "qT_ready"))
        x_loaded, k_stored, kT_stored, qT_stored = (
            [m.sem(f"{n}{s}") for s in range(2)] for n in ("x_loaded", "k_stored", "kT_stored", "qT_stored"))

        XT = D["XT"].rearrange("(k p) t -> p k t", p=P)
        KT, QT = (D[n].rearrange("(k p) t -> p k t", p=P) for n in ("KT", "QT"))
        k_out = T["k_prompt"][0, 0].rearrange("t h d -> t (h d)")
        ks_out = T["k_sample"][0].rearrange("b t h d -> (b t) (h d)")
        w_in = T["w_in"][0].rearrange("(k p) n -> p k n", p=P)
        COLS = (BANK, 0)

        with nc.Block() as block:

            @block.sync
            def _(sp):
                def load(at, s):
                    sp.dma_start(xT[s][:, :, :], XT[:, :, bass.ds(at, P)]).then_inc(x_loaded[s], 16)

                def store(count, at, s, which):
                    ready, src, dst, stored = (kT_ready, kT, KT, kT_stored) if which == "k" else (qT_ready, qT, QT, qT_stored)
                    wait_apart(sp, ready, count)
                    sp.dma_start(dst[:, :, bass.ds(at, P)], src[s][:, :, :]).then_inc(stored[s], 16)

                sp.dma_start(xT[0][:, :, 0:32], XT[:, :, 2048:2080]).then_inc(x_loaded[0], 16)
                sp.dma_start(xT[0][:, :, 32:P], XT[:, :, 0:P - 32]).then_inc(x_loaded[0], 16)
                for n in range(4):
                    c, half = n // 2, n % 2
                    sp.dma_start(w_raw[n][:, :, :], w_in[:, 4 * half:4 * half + 4, COLS[c]:COLS[c] + BANK]).then_inc(w_loaded[n], 16)
                load(0, 1)
                sp.wait_ge(lo_ready, 1)
                load(P, 0)
                with sp.Fori(0, 7) as i:
                    for e in range(2):
                        n, s = 2 * i + 1 + e, 1 - e
                        nxt, at2 = sp.snap(n + 1), sp.snap((n + 1) * P)
                        wait_apart(sp, lo_ready, nxt)
                        load(at2, s)
                        store(nxt, (n - 1) * P, s, "k")
                        store(nxt, (n - 1) * P, s, "q")
                for n in (15, 16):
                    store(n + 1, (n - 1) * P, n % 2, "k")
                    store(n + 1, (n - 1) * P, n % 2, "q")
                for sems in (kT_stored, qT_stored):
                    for s in range(2):
                        sp.wait_ge(sems[s], 16 * 8)

            @block.tensor
            def _(pe):
                def project(out, s, c, first, ready):
                    for kt in range(8):
                        if first and kt % 4 == 0:
                            pe.wait_ge(w_lo_done, 8 * c + kt + 4)
                        last = split_product(nc, out[:, :], x_hi[s][:, kt, :], x_lo[s][:, kt, :],
                                             w_hi[:, kt, c * BANK:(c + 1) * BANK], w_lo[:, kt, c * BANK:(c + 1) * BANK],
                                             kt == 0, kt == 7)
                    last.then_inc(ready, 1)

                def turn(out, src, signal):
                    for kt in range(4):
                        last = nc.tensor.transpose(out[:, kt * P:(kt + 1) * P], src[:, kt * P:(kt + 1) * P], keep["ident"][:, :])
                    last.then_inc(signal, 1)

                def turn_q(n, s):
                    pe.wait_ge(q_ready, n + 1)
                    if not (isinstance(n, int) and n == 0):
                        pe.wait_ge(qT_ready, n)
                    turn(ps_qT, q[s], q_turned)

                def tile(n, s, first=False):
                    pe.wait_ge(lo_ready, n + 1)
                    if not first:
                        pe.wait_ge(k_ready, n)
                    project(ps_k, s, 0, first, k_proj)
                    if not first:
                        turn_q(n - 1, 1 - s)
                    project(ps_q, s, 1, first, q_proj)
                    pe.wait_ge(k_ready, n + 1)
                    if not first:
                        pe.wait_ge(kT_ready, n)
                    turn(ps_kT, k[s], k_turned)

                tile(0, 0, True)
                tile(1, 1)
                tile(2, 0)
                with pe.Fori(1, 8) as i:
                    tile(2 * i + 1, 1)
                    tile(2 * i + 2, 0)
                turn_q(16, 0)

            @block.scalar
            def _(act):
                def tile(n, s, stores, rows=P):
                    at = None if rows != P else (n - 1) * P if isinstance(n, int) else act.snap((n - 1) * P)
                    act.wait_ge(rs_done, n + 1)
                    act.wait_ge(k_proj, n + 1)
                    if stores is not None:
                        act.wait_ge(k_stored[s], 16 * stores)
                    nc.scalar.activation(k[s][:, :], ps_k[:, :], ACT.Copy, scale=x_rs[s][:, 0:1]).then_inc(k_ready, 1)
                    act.wait_ge(k_ready, n + 1)
                    act.dma_start(ks_out if rows != P else k_out[bass.ds(at, P), :], k[s][0:rows, :]).then_inc(k_stored[s], 16)
                    act.wait_ge(q_proj, n + 1)
                    nc.scalar.activation(q[s][:, :], ps_q[:, :], ACT.Copy, scale=x_rs[s][:, 1:2]).then_inc(q_ready, 1)

                for c in range(2):
                    for kt in range(8):
                        n = 2 * c + kt // 4
                        if kt % 4 == 0:
                            act.wait_ge(w_loaded[n], 16)
                        nc.scalar.activation(w_hi[:, kt, c * BANK:(c + 1) * BANK], w_raw[n][:, kt % 4, :], ACT.Copy,
                                             scale=keep["cols"][:, G_MIX + kt:G_MIX + kt + 1]).then_inc(w_hi_done, 1)
                tile(0, 0, None, 32)
                tile(1, 1, None)
                tile(2, 0, 1)
                with act.Fori(1, 8) as i:
                    tile(2 * i + 1, 1, i)
                    tile(2 * i + 2, 0, i + 1)
                act.wait_ge(k_stored[0], 16 * 9)
                act.wait_ge(k_stored[1], 16 * 8)

            @block.vector
            def _(dve):
                def prepare(n, s, loads, rs_at):
                    dve.wait_ge(x_loaded[s], 16 * loads)
                    nc.vector.tensor_copy(x_hi[s][:, :, :], xT[s][:, :, :]).then_inc(hi_ready, 1)
                    dve.wait_ge(hi_ready, n + 1)
                    nc.vector.tensor_tensor(x_lo[s][:, :, :], xT[s][:, :, :], f32(x_hi[s][:, :, :]), ALU.subtract).then_inc(lo_ready, 1)
                    rs = keep["rs"][:, bass.ds(rs_at, 1)]
                    if not (isinstance(n, int) and n < 2):
                        dve.wait_ge(q_ready, n - 1)
                    nc.vector.tensor_scalar(x_rs[s][:, 0:1], rs, 1.0, None, ALU.mult)
                    nc.vector.tensor_scalar(x_rs[s][:, 1:2], rs, 0.125, None, ALU.mult).then_inc(rs_done, 1)

                def turned(n, s, which, stores):
                    signal, ready, src, dst, stored, own = (
                        (k_turned, kT_ready, ps_kT, kT, kT_stored, keep["kT_s"]) if which == "k" else
                        (q_turned, qT_ready, ps_qT, qT, qT_stored, keep["qT_s"]))
                    dve.wait_ge(signal, n + 1)
                    if isinstance(n, int) and n == 0:
                        nc.vector.tensor_copy(own[:, :, :], src[:, :].rearrange("p (k t) -> p k t", k=4)[:, :, 0:32]).then_inc(ready, 1)
                        return
                    if stores is not None:
                        dve.wait_ge(stored[s], 16 * stores)
                    nc.vector.tensor_copy(dst[s][:, :, :].rearrange("p k t -> p (k t)"), src[:, :]).then_inc(ready, 1)

                prepare(0, 0, 2, 16)
                for c in range(2):
                    for kt in range(8):
                        n = 2 * c + kt // 4
                        dve.wait_ge(w_hi_done, 8 * c + kt + 1)
                        nc.vector.scalar_tensor_tensor(
                            w_lo[:, kt, c * BANK:(c + 1) * BANK], w_raw[n][:, kt % 4, :], keep["cols"][:, G_MIX + kt:G_MIX + kt + 1],
                            f32(w_hi[:, kt, c * BANK:(c + 1) * BANK]), ALU.mult, ALU.subtract).then_inc(w_lo_done, 1)
                def step(j, odd, stored=True):
                    n = 2 * j + odd
                    before = j - 1 if stored else None
                    prepare(n + 1, 1 - odd, j + 3 if odd else j + 1, n)
                    turned(n - 1, 1 - odd, "q", before)
                    turned(n, odd, "k", (j if odd else before) if stored or j == 1 and odd else None)

                prepare(1, 1, 1, 0)
                turned(0, 0, "k", None)
                prepare(2, 0, 3, 1)
                turned(0, 0, "q", None)
                turned(1, 1, "k", None)
                step(1, 0, False)
                step(1, 1, False)
                with dve.Fori(2, 8) as j:
                    step(j, 0)
                    step(j, 1)
                turned(15, 1, "q", 7)
                turned(16, 0, "k", 7)
                turned(16, 0, "q", 7)


def attend_prompt(nc, keep, T, D):
    HEADS, NQ, LAG = 8, 16, 4
    PER = 2 * NQ
    granules = [1 + (s % NQ) // 8 for s in range(PER)]
    groups = [1 + (s % NQ) // 4 for s in range(PER)]
    doubles = [n - 1 for n in granules]
    NG, NR, N2 = sum(granules), sum(groups), sum(doubles)

    def before(counts, total, s):
        return sum(counts[:s]) if s >= 0 else sum(counts[:s + PER]) - total

    with ExitStack() as ctx:
        m = Alloc(nc, ctx, "at")
        k_raw, q_raw = m.sb("k_raw", [P, 2048]), m.sb("q_raw", [P, 2048])
        v_raw = m.sb("v_raw", [P, NQ, 64])
        k_hi, k_lo, q2 = ([m.sb(f"{n}{s}", [P, 2048], F32R) for s in range(2)] for n in ("k_hi", "k_lo", "q2"))
        v2 = [m.sb(f"v2{s}", [P, NQ, P], F32R) for s in range(2)]
        beta = [m.sb(f"beta{s}", [P, 2048]) for s in range(4)]
        rest = [m.sb(f"rest{s}", [P, 2048]) for s in range(4)]
        aT = [m.sb(f"aT{s}", [P, 4, 2 * P], F32R) for s in range(4)]
        o2 = [m.sb(f"o2{s}", [P, BANK]) for s in range(2)]
        bias = [m.sb(f"bias{s}", [P, 1]) for s in range(2)]
        o_part = m.sb("o_part", [P, P])
        oT = [m.sb(f"oT{s}", [64, BANK]) for s in range(2)]
        sq = m.sb("sq", [64, BANK])
        ssum = m.sb("ssum", [64, 2048])
        far = m.sb("far", [P, P])
        far_r, ident_r = m.sb("far_r", [P, P], F32R), m.sb("ident_r", [P, P], F32R)
        fold = m.sb("fold", [P, 64])
        ps_z = [m.bank(f"ps_z{s}", (P, 1024)) for s in range(2)]
        ps_t = [m.bank(f"ps_t{s}") for s in range(2)]
        ps_o, ps_f = m.bank("ps_o"), m.bank("ps_f")

        loaded, head_high, head_low, z_ready, b_done, product_done, a_done = (
            m.sem(n) for n in ("loaded", "head_high", "head_low", "z_ready", "b_done", "product_done", "a_done"))
        rest_by_dve, rest_by_act, k_high, o_part_done = (m.sem(n) for n in ("rest_by_dve", "rest_by_act", "k_high", "o_part_done"))
        a_turned, ahi_done, alo_done, o_ready, o_read, folded, oT_done, osq_done, sum_done = (
            m.sem(n) for n in ("a_turned", "ahi_done", "alo_done", "o_ready", "o_read", "folded", "oT_done", "osq_done", "sum_done"))
        rest_zeroed = m.sem("rest_zeroed")
        oT_stored = [m.sem(f"oT_stored{s}") for s in range(2)]
        made, cast, mean_ready, rms_done, rs_done, rs_stored = (
            m.sem(n) for n in ("made", "cast", "mean_ready", "rms_done", "rs_done", "rs_stored"))

        v_src = T["v_prompt"][0, 0].rearrange("(kt p) h d -> p kt h d", p=P)

        def iterations(eng, tick, drain=True):
            for s in range(PER):
                tick(0, s)
            with eng.Fori(1, HEADS // 2 - 1) as it:
                for s in range(PER):
                    tick(it, s)
            for s in range(PER):
                tick(HEADS // 2 - 1, s)
            for s in range(LAG + 5):
                tick(HEADS // 2, s)

        def has(it, s):
            if isinstance(it, int):
                return 0 <= PER * it + s < PER * HEADS // 2
            return True

        def one_less(eng, op, signal, it, s, g):
            n = P * (s % NQ + 1)
            c0, c1 = (0, min(n, 1024) - 1) if g == 0 else (1023, n - 1)
            eng.wait_ge(b_done, NG * it + before(granules, NG, s) + g + 3)
            op(rest[s % 4][:, c0:c1], beta[s % 4][:, c0 + 1:c1 + 1]).then_inc(signal, 1)

        HIGH_PARTS, LOW_PARTS = 5, 8

        def next_head(it, t):
            return has(it, t) and not (isinstance(it, int) and 2 * it + t // NQ + 1 >= HEADS)

        with nc.Block() as block:

            @block.sync
            def _(sp):
                def load(h):
                    rows = bass.ds(64 * h, 64)
                    for raw, src in ((k_raw, D["KT"]), (q_raw, D["QT"])):
                        for half in range(2):
                            sp.dma_start(raw[64 * half:64 * half + 64, :], src[rows, :]).then_inc(loaded, 16)
                    sp.dma_start(v_raw[:, :, :].unsqueeze(2), v_src[:, :, bass.ds(h, 1), :]).then_inc(loaded, 16)

                def store(h, quad):
                    n = 4 * h + quad + 1
                    wait_apart(sp, oT_done, n if isinstance(n, int) else sp.snap(n))
                    sp.dma_start(D["MIXT"][bass.ds(64 * h, 64), quad * BANK:(quad + 1) * BANK], oT[quad % 2][:, :])\
                        .then_inc(oT_stored[quad % 2], 16)

                load(0)
                sp.wait_ge(head_low, 2)
                load(1)
                with sp.Fori(0, HEADS - 2) as h:
                    store(h, 0)
                    store(h, 1)
                    wait_apart(sp, head_low, sp.snap(2 * h + 4))
                    load(h + 2)
                    store(h, 2)
                    store(h, 3)
                for h in (HEADS - 2, HEADS - 1):
                    for quad in range(4):
                        store(h, quad)
                sp.wait_ge(oT_stored[0], 16 * 16)
                sp.wait_ge(oT_stored[1], 16 * 16)
                sp.wait_ge(rs_done, 4)
                sp.dma_start(D["RSB"][:, 0:2048], beta[0][:, :]).then_inc(rs_stored, 16)
                sp.wait_ge(rs_stored, 16)

            @block.gpsimd
            def _(pool):
                nc.gpsimd.memset(far[:, :], 0.0).then_inc(made, 1)
                nc.gpsimd.memset(fold[:, :], 0.0).then_inc(made, 1)
                nc.gpsimd.memset(ssum[:, :], 0.0).then_inc(made, 1)
                pool.wait_ge(made, 3)
                nc.gpsimd.affine_select(out=far[:, :], in_=far[:, :], pattern=[[-1, P]], compare_op=ALU.is_gt,
                                        fill=-float(2 ** 100), base=0, channel_multiplier=1).then_inc(made, 1)
                pool.wait_ge(made, 4)
                nc.gpsimd.affine_select(out=fold[0:64, :], in_=fold[0:64, :], pattern=[[-1, 64]], compare_op=ALU.not_equal,
                                        fill=1.0, base=0, channel_multiplier=1).then_inc(made, 1)
                pool.wait_ge(made, 5)
                nc.gpsimd.affine_select(out=fold[64:P, :], in_=fold[64:P, :], pattern=[[-1, 64]], compare_op=ALU.not_equal,
                                        fill=1.0, base=0, channel_multiplier=1).then_inc(made, 1)
                pool.wait_ge(made, 6)

                def weights(it, s):
                    n = P * (s % NQ + 1)
                    pool.wait_ge(product_done, PER * it + s + 1)
                    nc.gpsimd.tensor_tensor(rest[s % 4][:, 0:n], rest[s % 4][:, 0:n], beta[s % 4][:, 0:n], ALU.mult).then_inc(a_done, 1)

                def low_operand(h, slot, part):
                    if part == 0:
                        pool.wait_ge(head_high, 4 * h + 2)
                        pool.wait_ge(k_high, h + 1)
                        done = nc.gpsimd.tensor_tensor(k_lo[slot][:, :], k_raw[:, :], f32(k_hi[slot][:, :]), ALU.subtract)
                    else:
                        pool.wait_ge(head_high, 4 * h + 4)
                        done = nc.gpsimd.tensor_tensor(v2[slot][:, :, 64:P], v_raw[:, :, :], f32(v2[slot][:, :, 0:64]), ALU.subtract)
                    done.then_inc(head_low, 1)

                def tick(it, t):
                    if has(it, t - 3):
                        weights(it, t - 3)
                    part = t % NQ - LOW_PARTS
                    if 0 <= part < 2 and next_head(it, t):
                        low_operand(2 * it + t // NQ + 1, 1 - t // NQ, part)

                for part in range(2):
                    low_operand(0, 0, part)
                iterations(pool, tick)

            @block.tensor
            def _(pe):
                def logits(it, s, g):
                    i, hs = s % NQ, s // NQ
                    n = P * (i + 1)
                    if i == 0:
                        pe.wait_ge(head_high, 8 * it + 4 * hs + 4)
                        pe.wait_ge(head_low, 4 * it + 2 * hs + 2)
                    at = NG * it + before(granules, NG, s) + g
                    z = ps_z[(before(granules, NG, s) + g) % 2]
                    pe.wait_ge(b_done, at + 1)
                    width = min(n - 1024 * g, 1024)
                    for c in range(0, width, BANK):
                        w = max(min(BANK, width - c), 2 * P)
                        k0 = 1024 * g + c
                        diagonal = k0 <= n - P < k0 + w
                        q = q2[hs][:, i * P:(i + 1) * P]
                        nc.tensor.matmul(z[:, c:c + w], q, k_hi[hs][:, k0:k0 + w], start=True, stop=False)
                        last = nc.tensor.matmul(z[:, c:c + w], q, k_lo[hs][:, k0:k0 + w], start=False, stop=not diagonal)
                        if diagonal:
                            d = n - P - 1024 * g
                            last = nc.tensor.matmul(z[:, d:d + P], ident_r[:, :], far_r[:, :], start=False, stop=True)
                    last.then_inc(z_ready, 1)

                def turn(it, s, r):
                    at = NR * it + before(groups, NR, s) + r
                    slot = before(groups, NR, s) + r
                    pe.wait_ge(alo_done, at + 1)
                    for kt in range(4 * r, min(4 * r + 4, s % NQ + 1)):
                        last = nc.tensor.transpose(ps_t[slot % 2][:, kt % 4 * P:kt % 4 * P + P], rest[s % 4][:, kt * P:(kt + 1) * P],
                                                   keep["ident"][:, :])
                    last.then_inc(a_turned, 1)

                def weigh(it, s, r):
                    at = NR * it + before(groups, NR, s) + r
                    slot = before(groups, NR, s) + r
                    pe.wait_ge(alo_done, at + 3)
                    if r == 0:
                        pe.wait_ge(o_read, PER * it + s + 1)
                    i, hs = s % NQ, s // NQ % 2
                    for kt in range(4 * r, min(4 * r + 4, i + 1)):
                        last = nc.tensor.matmul(ps_o[:, 0:2 * P], v2[hs][:, kt, :], aT[slot % 4][:, kt % 4, :],
                                                start=kt == 0, stop=kt == i)
                    if r == groups[s % PER] - 1:
                        last.then_inc(o_ready, 1)

                def add_halves(it, s):
                    quad = s // 4
                    pe.wait_ge(o_read, PER * it + s + 2)
                    pe.wait_ge(osq_done, 8 * it + quad + 1)
                    nc.tensor.matmul(ps_f[0:64, :], fold[:, :], o2[quad % 2][:, :], start=True, stop=True).then_inc(folded, 1)

                def tick(it, t):
                    s = t - LAG
                    n_s = groups[s] if has(it, s) else 0
                    if n_s:
                        pe.wait_ge(a_done, PER * it + s + 1)
                        turn(it, s, 0)
                    if has(it, t):
                        logits(it, t, 0)
                    if has(it, s - 1):
                        weigh(it, s - 1, groups[(s - 1) % PER] - 1)
                    for r in range(1, min(n_s, 3)):
                        turn(it, s, r)
                    if has(it, t) and granules[t] == 2:
                        logits(it, t, 1)
                    for r in range(0, min(n_s - 1, 2)):
                        weigh(it, s, r)
                    if n_s == 4:
                        turn(it, s, 3)
                    if has(it, s - 1) and (s - 1) % 4 == 3:
                        add_halves(it, s - 1)
                    if n_s == 4:
                        weigh(it, s, 2)

                pe.sem_inc(o_read, 1)
                pe.wait_ge(cast, 2)
                iterations(pe, tick)
                for c in range(4):
                    if c == 0:
                        pe.wait_ge(sum_done, 33)
                    if c >= 2:
                        pe.wait_ge(rms_done, c - 1)
                    nc.tensor.matmul(ps_t[c % 2][:, :], keep["mean512"][0:64, :], ssum[:, c * BANK:(c + 1) * BANK], start=True, stop=True)\
                        .then_inc(mean_ready, 1)

            @block.scalar
            def _(act):
                def high_part(it, s, r):
                    at = NR * it + before(groups, NR, s) + r
                    slot = before(groups, NR, s) + r
                    w = min(4, s % NQ + 1 - 4 * r)
                    act.wait_ge(a_turned, at + 1)
                    nc.scalar.activation(aT[slot % 4][:, 0:w, 0:P], ps_t[slot % 2][:, 0:w * P].rearrange("p (k t) -> p k t", k=w),
                                         ACT.Copy).then_inc(ahi_done, 1)

                def sigmoid(it, t, g):
                    n = P * (t % NQ + 1)
                    at = before(granules, NG, t) + g
                    w = min(n - 1024 * g, 1024)
                    act.wait_ge(z_ready, NG * it + at + 1)
                    nc.scalar.activation(beta[t % 4][:, 1024 * g:1024 * g + w], ps_z[at % 2][:, 0:w], ACT.Sigmoid,
                                         bias=bias[t // NQ][:, :]).then_inc(b_done, 1)

                def keys_high(h, slot):
                    act.wait_ge(loaded, 80 * h + 80)
                    nc.scalar.activation(k_hi[slot][:, :], k_raw[:, :], ACT.Copy).then_inc(k_high, 1)

                def rest_op(out, in_):
                    return nc.scalar.activation(out, in_, ACT.Identity, scale=-1.0, bias=1.0)

                def tick(it, t):
                    s = t - LAG
                    n_s = groups[s] if has(it, s) else 0
                    if n_s:
                        high_part(it, s, 0)
                    if has(it, t):
                        sigmoid(it, t, 0)
                    if has(it, s - 1):
                        low_product(it, s - 1)
                    if n_s > 1:
                        high_part(it, s, 1)
                    if has(it, t - 1) and granules[(t - 1) % PER] == 2:
                        one_less(act, rest_op, rest_by_act, it, t - 1, 1)
                    if has(it, t) and granules[t] == 2:
                        sigmoid(it, t, 1)
                    if n_s > 2:
                        high_part(it, s, 2)
                    if has(it, s - 2) and (s - 2) % 4 == 3:
                        fold_out(it, (s - 2) // 4)
                    if n_s > 3:
                        high_part(it, s, 3)
                    if t % NQ == HIGH_PARTS and next_head(it, t):
                        keys_high(2 * it + t // NQ + 1, 1 - t // NQ)

                def low_product(it, s):
                    act.wait_ge(o_ready, PER * it + s + 1)
                    act.wait_ge(o_read, PER * it + s + 1)
                    nc.scalar.activation(o_part[:, :], ps_o[:, P:2 * P], ACT.Copy).then_inc(o_part_done, 1)

                def fold_out(it, quad):
                    act.wait_ge(folded, 8 * it + quad + 1)
                    act.wait_ge(oT_stored[quad % 2], 64 * it + 16 * (quad // 2) + 16)
                    nc.scalar.activation(oT[quad % 2][:, :], ps_f[0:64, :], ACT.Copy).then_inc(oT_done, 1)
                    act.wait_ge(sum_done, 8 * it + quad + 1)
                    nc.scalar.activation(sq[:, :], ps_f[0:64, :], ACT.Square).then_inc(osq_done, 1)

                act.sem_inc(b_done, 2)
                act.sem_inc(oT_stored[0], 16)
                act.sem_inc(oT_stored[1], 16)
                act.sem_inc(osq_done, 1)
                keys_high(0, 0)
                act.wait_ge(rest_zeroed, 4)
                iterations(act, tick)
                for c in range(4):
                    act.wait_ge(mean_ready, c + 1)
                    nc.scalar.activation(beta[0][:, c * BANK:(c + 1) * BANK], ps_t[c % 2][:, :], ACT.Sqrt, bias=keep["eps"][:, :])\
                        .then_inc(rms_done, 1)

            @block.vector
            def _(dve):
                def high_operand(h, slot, part):
                    if part == 0:
                        dve.wait_ge(loaded, 80 * h + 80)
                        done = nc.vector.tensor_copy(q2[slot][:, :], q_raw[:, :])
                    elif part == 1:
                        done = nc.vector.tensor_copy(v2[slot][:, :, 0:64], v_raw[:, :, :])
                    elif part == 2:
                        dve.wait_ge(head_high, 4 * h + 1)
                        done = nc.vector.tensor_tensor(q2[slot][64:P, :], q_raw[64:P, :], f32(q2[slot][64:P, :]), ALU.subtract)
                    else:
                        done = nc.vector.tensor_scalar(bias[slot][:, :], keep["sb_bias"][:, bass.ds(h, 1)], 1.0, None, ALU.mult)
                    done.then_inc(head_high, 1)

                def low_part(it, s, r):
                    at = NR * it + before(groups, NR, s) + r
                    slot = before(groups, NR, s) + r
                    w = min(4, s % NQ + 1 - 4 * r)
                    dve.wait_ge(ahi_done, at + 1)
                    nc.vector.tensor_tensor(aT[slot % 4][:, 0:w, P:2 * P], ps_t[slot % 2][:, 0:w * P].rearrange("p (k t) -> p k t", k=w),
                                            f32(aT[slot % 4][:, 0:w, 0:P]), ALU.subtract).then_inc(alo_done, 1)

                def product(it, s):
                    n = P * (s % NQ + 1)
                    r = rest[s % 4][:, 0:n - 1][:, ::-1]
                    dve.wait_ge(rest_by_dve, PER * it + s + 1)
                    if doubles[s % PER]:
                        dve.wait_ge(rest_by_act, N2 * it + before(doubles, N2, s) + 1)
                    nc.vector.tensor_tensor_scan(r, r, r, 1.0, ALU.mult, ALU.min).then_inc(product_done, 1)

                def take_output(it, s):
                    quad = s // 4
                    dve.wait_ge(o_part_done, PER * it + s + 1)
                    nc.vector.tensor_tensor(o2[quad % 2][:, s % 4 * P:(s % 4 + 1) * P], ps_o[:, 0:P], o_part[:, :], ALU.add).then_inc(o_read, 1)

                def rest_op(out, in_):
                    return nc.vector.tensor_scalar(out, in_, -1.0, 1.0, ALU.mult, ALU.add)

                def tick(it, t):
                    s = t - LAG
                    n_s = groups[s] if has(it, s) else 0
                    if n_s:
                        low_part(it, s, 0)
                    if has(it, s - 1):
                        take_output(it, s - 1)
                    if has(it, s - 3) and (s - 3) % 4 == 3:
                        add_square(it, (s - 3) // 4)
                    if n_s > 1:
                        low_part(it, s, 1)
                    if has(it, t - 2):
                        product(it, t - 2)
                    for r in range(2, n_s):
                        low_part(it, s, r)
                    part = t % NQ - HIGH_PARTS
                    if 0 <= part < 4 and next_head(it, t):
                        high_operand(2 * it + t // NQ + 1, 1 - t // NQ, part)
                    if has(it, t - 1):
                        one_less(dve, rest_op, rest_by_dve, it, t - 1, 0)

                def add_square(it, quad):
                    dve.wait_ge(osq_done, 8 * it + quad + 2)
                    cols = slice(quad % 4 * BANK, (quad % 4 + 1) * BANK)
                    nc.vector.tensor_tensor(ssum[:, cols], ssum[:, cols], sq[:, :], ALU.add).then_inc(sum_done, 1)

                dve.sem_inc(alo_done, 2)
                dve.sem_inc(sum_done, 1)
                for n in range(4):
                    nc.vector.memset(rest[n][:, :], 0.0).then_inc(rest_zeroed, 1)
                for part in range(4):
                    high_operand(0, 0, part)
                dve.wait_ge(made, 6)
                nc.vector.tensor_copy(far_r[:, :], far[:, :]).then_inc(cast, 1)
                nc.vector.tensor_copy(ident_r[:, :], keep["ident"][:, :]).then_inc(cast, 1)
                iterations(dve, tick)
                for c in range(4):
                    dve.wait_ge(rms_done, c + 1)
                    nc.vector.reciprocal(beta[0][:, c * BANK:(c + 1) * BANK], beta[0][:, c * BANK:(c + 1) * BANK]).then_inc(rs_done, 1)


def attend_sample(nc, keep, T, D):
    GROUPS, PB, STEPS, RING = 2, 4, 16, 8
    KEYS = 2048
    with ExitStack() as ctx:
        m = Alloc(nc, ctx, "as")
        pages = [m.sb(f"pages{s}", [P, 4, BANK]) for s in range(RING)]
        kT4 = [m.sb(f"kT4{s}", [P, 4, BANK]) for s in range(2)]
        q_block = m.sb("q_block", [P, 4, PB, 32])
        k_new = m.sb("k_new", [P, 4, 4 * PB])
        v_new = m.sb("v_new", [4, PB, BANK])
        beta, rest = m.sb("beta", [P, KEYS + 4]), m.sb("rest", [P, KEYS + 4])
        aT = m.sb("aT", [P, 16, P])
        aT_new = m.sb("aT_new", [4, P])
        own = m.sb("own", [P, BANK])
        row_head, row_bias, biases = m.sb("row_head", [P, 8]), m.sb("row_bias", [P, 1]), m.sb("biases", [P, 8])
        row_query, before = m.sb("row_query", [P, 4]), m.sb("before", [P, 4])
        merge = m.sb("merge", [P, 4 * PB])
        mixT, sq = m.sb("mixT", [P, 4, 32]), m.sb("sq", [P, 4, 32])
        rms = m.sb("rms", [P, 32])
        ps_z = [m.bank(f"ps_z{j}") for j in range(4)]
        ps_t = [m.bank(f"ps_t{s}") for s in range(2)]
        ps_new, ps_o = m.bank("ps_new"), m.bank("ps_o")

        masks, blocks, v_loaded, turned, kT_even, kT_odd, z_done, new_done, b_done, b_new_done, new_masked, rest_done = (
            m.sem(n) for n in ("masks", "blocks", "v_loaded", "turned", "kT_even", "kT_odd", "z_done", "new_done", "b_done",
                               "b_new_done", "new_masked", "rest_done"))
        product_done, a_done, a_turned, aT_even, aT_odd, page_used, o_ready, own_done, mix_ready, mix_done = (
            m.sem(n) for n in ("product_done", "a_done", "a_turned", "aT_even", "aT_odd", "page_used", "o_ready", "own_done",
                               "mix_ready", "mix_done"))
        sq_done, mean_ready, rms_done, rs_done, stored = (m.sem(n) for n in ("sq_done", "mean_ready", "rms_done", "rs_done", "stored"))
        page_loaded = [m.sem(f"page_loaded{s}") for s in range(RING)]
        N_MASKS = 10

        caches = [T[n][0].rearrange("n p h d -> p n (h d)") for n in ("cache_k", "cache_v")]
        v_src = T["v_sample"][0].rearrange("b t h d -> t b (h d)")

        def load_pages(eng, g, part, odd):
            with eng.Fori(0, STEPS // RING) as turn:
                for slot in range(odd, RING, 2):
                    wait_apart(eng, page_used, eng.snap(2 * STEPS * g + STEPS * part + RING * turn + slot + 1))
                    for p in range(4):
                        at = 16 * PB * g + 4 * (RING // PB) * turn + 16 * (slot % PB) + 4 * (slot // PB) + p
                        page = eng.value_load(keep["page_table"][0:1, bass.ds(at, 1)], min_val=0, max_val=159)
                        eng.dma_start(pages[slot][:, p:p + 1, :], caches[part][:, bass.ds(page, 1), :])\
                            .then_inc(page_loaded[slot], 16)

        with nc.Block() as block:

            @block.sync
            def _(sp):
                with sp.Fori(0, GROUPS) as g:
                    for part in range(2):
                        if part == 1:
                            wait_apart(sp, o_ready, sp.snap(g + 1))
                            sp.dma_start(v_new[:, :, :], v_src[:, bass.ds(PB * g, PB), :]).then_inc(v_loaded, 16)
                        load_pages(sp, g, part, 0)
                sp.wait_ge(mix_done, GROUPS + 1)
                sp.dma_start(D["MIXT"][0:512, 2048:2080].rearrange("(k p) t -> p k t", p=P), mixT[:, :, :]).then_inc(stored, 16)
                sp.wait_ge(rs_done, 1)
                sp.dma_start(D["RSB"][:, 2048:2080], rms[:, :]).then_inc(stored, 16)
                sp.wait_ge(stored, 32)

            @block.tensor
            def _(pe):
                def logits(g, k):
                    j, bi = k // PB, k % PB
                    pe.wait_ge(kT_even, 2 * STEPS * g + 2 * k + 3)
                    pe.wait_ge(kT_odd, 2 * STEPS * g + 2 * k + 3)
                    for hp in range(4):
                        last = nc.tensor.matmul(ps_z[j][32 * bi:32 * bi + 32, :], q_block[:, hp, bi, :], kT4[k % 2][:, hp, :],
                                                start=hp == 0, stop=hp == 3, tile_position=(0, 32 * bi))
                    last.then_inc(z_done, 1)

                pe.sem_inc(page_used, RING)
                pe.sem_inc(o_ready, 1)
                pe.sem_inc(z_done, 2)
                pe.wait_ge(masks, N_MASKS)
                with pe.Fori(0, GROUPS) as g:
                    pe.wait_ge(blocks, 9 * g + 9)
                    for k in range(STEPS):
                        pe.wait_ge(page_loaded[k % RING], 256 * g + 64 * (k // RING) + 64)
                        for p in range(4):
                            pe.wait_ge((kT_even, kT_odd)[p % 2], 2 * STEPS * g + 2 * k + p // 2 + 1)
                            for hp in range(4):
                                last = nc.tensor.transpose(ps_t[p % 2][:, hp * P:(hp + 1) * P], pages[k % RING][:, p, hp * P:(hp + 1) * P],
                                                           keep["ident"][:, :])
                            last.then_inc(turned, 1)
                        pe.wait_ge(turned, 4 * STEPS * g + 4 * k + 4)
                        pe.sem_inc(page_used, 1)
                        if k:
                            logits(g, k - 1)
                    logits(g, STEPS - 1)
                    pe.wait_ge(mix_done, g + 1)
                    for bi in range(PB):
                        for hp in range(4):
                            last = nc.tensor.matmul(ps_new[32 * bi:32 * bi + 32, 0:4], q_block[:, hp, bi, :], k_new[:, hp, 4 * bi:4 * bi + 4],
                                                    start=hp == 0, stop=hp == 3, tile_position=(0, 32 * bi))
                    last.then_inc(new_done, 1)
                    pe.wait_ge(a_done, g + 1)
                    for r in range(4):
                        if r >= 2:
                            pe.wait_ge((aT_even, aT_odd)[r % 2], (3, 2)[r % 2] * g + 1)
                        for kt in range(4):
                            last = nc.tensor.transpose(ps_t[r % 2][:, kt * P:(kt + 1) * P], beta[:, (4 * r + kt) * P:(4 * r + kt + 1) * P],
                                                       keep["ident"][:, :])
                        last.then_inc(a_turned, 1)
                    pe.wait_ge(aT_even, 3 * g + 2)
                    nc.tensor.transpose(ps_t[0][0:4, 0:P], beta[:, KEYS:KEYS + 4], keep["ident"][:, :]).then_inc(a_turned, 1)
                    for k in range(STEPS):
                        j, bi = k // PB, k % PB
                        if k == 3 * PB:
                            pe.wait_ge(v_loaded, 16 * g + 16)
                            pe.wait_ge(aT_even, 3 * g + 3)
                        if bi == 0:
                            pe.wait_ge((aT_even, aT_odd)[j % 2], (3, 2)[j % 2] * g + j // 2 + 1)
                        pe.wait_ge(page_loaded[k % RING], 256 * g + 128 + 64 * (k // RING) + 64)
                        for p in range(4):
                            last = nc.tensor.matmul(ps_o[32 * bi:32 * bi + 32, :], aT[:, 4 * j + p, 32 * bi:32 * bi + 32], pages[k % RING][:, p, :],
                                                    start=k < PB and p == 0, stop=False, tile_position=(0, 32 * bi))
                        last.then_inc(page_used, 1)
                    for bi in range(PB):
                        last = nc.tensor.matmul(ps_o[32 * bi:32 * bi + 32, :], aT_new[:, 32 * bi:32 * bi + 32], v_new[:, bi, :],
                                                start=False, stop=True, tile_position=(0, 32 * bi))
                    last.then_inc(o_ready, 1)
                    pe.wait_ge(own_done, g + 1)
                    for c in range(4):
                        last = nc.tensor.matmul(ps_new[:, 64 + 16 * c:80 + 16 * c], own[:, c * P:(c + 1) * P], merge[:, :], start=True, stop=True)
                    last.then_inc(mix_ready, 1)
                pe.wait_ge(sq_done, 1)
                for c in range(4):
                    last = nc.tensor.matmul(ps_new[:, 0:32], keep["mean512"][:, :], sq[:, c, :], start=c == 0, stop=c == 3)
                last.then_inc(mean_ready, 1)

            @block.scalar
            def _(act):
                def sigmoid(g, j):
                    cols = slice(j * BANK, (j + 1) * BANK)
                    act.wait_ge(z_done, STEPS * g + PB * (j + 1) + 2)
                    nc.scalar.activation(beta[:, cols], ps_z[j][:, :], ACT.Sigmoid, bias=row_bias[:, :]).then_inc(b_done, 1)
                    act.wait_ge(b_done, 4 * g + j + 1)
                    if j < 3:
                        nc.scalar.activation(rest[:, cols], beta[:, cols], ACT.Identity, scale=-1.0, bias=1.0).then_inc(rest_done, 1)

                act.sem_inc(kT_odd, 1)
                act.wait_ge(masks, N_MASKS)
                with act.Fori(0, GROUPS) as g:
                    for k in range(STEPS):
                        for p in (1, 3):
                            act.wait_ge(turned, 4 * STEPS * g + 4 * k + p + 1)
                            if p == 1:
                                act.wait_ge(z_done, STEPS * g + k + 1)
                            nc.scalar.activation(kT4[k % 2][:, :, p * P:(p + 1) * P], ps_t[1][:, :].rearrange("p (h t) -> p h t", h=4),
                                                 ACT.Copy).then_inc(kT_odd, 1)
                        if k % PB == 0 and k:
                            sigmoid(g, k // PB - 1)
                    sigmoid(g, 3)
                    act.wait_ge(new_done, g + 1)
                    nc.scalar.activation(beta[:, KEYS:KEYS + 4], ps_new[:, 0:4], ACT.Sigmoid, bias=row_bias[:, :]).then_inc(b_new_done, 1)
                    act.wait_ge(new_masked, g + 1)
                    nc.scalar.activation(rest[:, 1536:KEYS + 4], beta[:, 1536:KEYS + 4], ACT.Identity, scale=-1.0, bias=1.0).then_inc(rest_done, 1)
                    for r in (1, 3):
                        act.wait_ge(a_turned, 5 * g + r + 1)
                        nc.scalar.activation(aT[:, 4 * r:4 * r + 4, :], ps_t[1][:, :].rearrange("p (k t) -> p k t", k=4), ACT.Copy)\
                            .then_inc(aT_odd, 1)
                act.wait_ge(mean_ready, 1)
                nc.scalar.activation(rms[:, :], ps_new[:, 0:32], ACT.Sqrt, bias=keep["eps"][:, :]).then_inc(rms_done, 1)

            @block.gpsimd
            def _(pool):
                nc.gpsimd.memset(q_block[:, :, :, :], 0.0).then_inc(masks, 1)
                with pool.Fori(0, GROUPS) as g:
                    for part in range(2):
                        load_pages(pool, g, part, 1)

            @block.vector
            def _(dve):
                ident = keep["ident"]
                nc.vector.tensor_reduce(row_head[:, :], ident[:, :].rearrange("p (b h q) -> p h b q", b=PB, h=8), AX.XY, ALU.add).then_inc(masks, 1)
                nc.vector.tensor_reduce(row_query[:, :], ident[:, :].rearrange("p (b h q) -> p q b h", b=PB, h=8), AX.XY, ALU.add).then_inc(masks, 1)
                nc.vector.tensor_reduce(merge[:, :].rearrange("p (b q) -> p b q", b=PB), ident[:, :].rearrange("p (b h q) -> p b q h", b=PB, h=8),
                                        AX.X, ALU.add).then_inc(masks, 1)
                nc.vector.memset(before[:, :], 0.0).then_inc(masks, 1)
                dve.wait_ge(masks, 5)
                for t in range(3):
                    nc.vector.tensor_reduce(before[:, t:t + 1], row_query[:, t + 1:4], AX.X, ALU.add).then_inc(masks, 1)
                nc.vector.tensor_tensor(biases[:, :], row_head[:, :], keep["sb_bias"][:, :], ALU.mult).then_inc(masks, 1)
                dve.wait_ge(masks, 9)
                nc.vector.tensor_reduce(row_bias[:, :], biases[:, :], AX.X, ALU.add).then_inc(masks, 1)
                dve.sem_inc(kT_even, 1)
                dve.sem_inc(mix_done, 1)
                dve.wait_ge(masks, N_MASKS)
                with dve.Fori(0, GROUPS) as g:
                    cols = bass.ds(4 * PB * g, 4 * PB)
                    for h in range(8):
                        rows, hp = slice(64 * (h % 2), 64 * (h % 2) + 64), h // 2
                        nc.vector.tensor_scalar(q_block[rows, hp, :, 4 * h:4 * h + 4], keep["qT_s"][rows, hp, cols].rearrange("p (b q) -> p b q", b=PB),
                                                1.0, None, ALU.mult).then_inc(blocks, 1)
                    nc.vector.tensor_scalar(k_new[:, :, :], keep["kT_s"][:, :, cols], 1.0, None, ALU.mult).then_inc(blocks, 1)
                    for k in range(STEPS):
                        for p in (0, 2):
                            dve.wait_ge(turned, 4 * STEPS * g + 4 * k + p + 1)
                            if p == 0:
                                dve.wait_ge(z_done, STEPS * g + k + 1)
                            nc.vector.tensor_copy(kT4[k % 2][:, :, p * P:(p + 1) * P], ps_t[0][:, :].rearrange("p (h t) -> p h t", h=4))\
                                .then_inc(kT_even, 1)
                    dve.wait_ge(b_new_done, g + 1)
                    nc.vector.tensor_tensor(beta[:, KEYS:KEYS + 4], beta[:, KEYS:KEYS + 4], before[:, :], ALU.mult).then_inc(new_masked, 1)
                    dve.wait_ge(rest_done, 4 * g + 4)
                    r = rest[:, :][:, ::-1]
                    nc.vector.tensor_tensor_scan(r, r, r, 1.0, ALU.mult, ALU.min).then_inc(product_done, 1)
                    dve.wait_ge(product_done, g + 1)
                    nc.vector.tensor_tensor(beta[:, 0:KEYS + 3], beta[:, 0:KEYS + 3], rest[:, 1:KEYS + 4], ALU.mult).then_inc(a_done, 1)
                    for r in (0, 2):
                        dve.wait_ge(a_turned, 5 * g + r + 1)
                        nc.vector.tensor_copy(aT[:, 4 * r:4 * r + 4, :], ps_t[0][:, :].rearrange("p (k t) -> p k t", k=4)).then_inc(aT_even, 1)
                    dve.wait_ge(a_turned, 5 * g + 5)
                    nc.vector.tensor_copy(aT_new[:, :], ps_t[0][0:4, 0:P]).then_inc(aT_even, 1)
                    dve.wait_ge(o_ready, g + 2)
                    nc.vector.tensor_tensor(own[:, :].rearrange("p (h d) -> p h d", h=8), ps_o[:, :].rearrange("p (h d) -> p h d", h=8),
                                            row_head[:, :].unsqueeze(2).to_broadcast([P, 8, 64]), ALU.mult).then_inc(own_done, 1)
                    dve.wait_ge(mix_ready, g + 1)
                    nc.vector.tensor_scalar(mixT[:, :, cols], ps_new[:, 64:128].rearrange("p (c t) -> p c t", c=4), 1.0, None, ALU.mult)\
                        .then_inc(mix_done, 1)
                dve.wait_ge(mix_done, GROUPS + 1)
                nc.vector.tensor_tensor(sq[:, :, :], mixT[:, :, :], mixT[:, :, :], ALU.mult).then_inc(sq_done, 1)
                dve.wait_ge(rms_done, 1)
                nc.vector.reciprocal(rms[:, :], rms[:, :]).then_inc(rs_done, 1)


def finish_tokens(nc, keep, T, D):
    NB, TB, NJ = 5, 416, 22
    SLABS, UNITS = 88, 76
    O_AT, U_AT, D_AT, P_AT = 0, 8, 52, 76
    OU, UU, DU, PU = 0, 8, 52, 60
    MIX_ORDER = (4, 5, 6, 7, 0, 1, 2, 3)
    MIX_AT = 2
    with ExitStack() as ctx:
        m = Alloc(nc, ctx, "pf")
        h = m.sb("h", [P, 8, TB])
        mix = m.sb("mix", [P, 8, TB])
        x_hi, x_lo = (m.sb(n, [P, 8, TB], F32R) for n in ("x_hi", "x_lo"))
        f_hi, f_lo = (m.sb(n, [P, NJ, TB], F32R) for n in ("f_hi", "f_lo"))
        raw = [m.sb(f"raw{n}", [P, 1024]) for n in range(4)]
        w_hi = [m.sb(f"w_hi{n}", [P, 1024], F32R) for n in range(4)]
        w_lo = [m.sb(f"w_lo{n}", [P, 1024], F32R) for n in range(4)]
        p_raw = m.sb("p_raw", [P, 2, TB])
        rs_sb = m.sb("rs_sb", [P, TB])
        ssum, sq, rs = (m.sb(n, [P, TB]) for n in ("ssum", "sq", "rs"))
        gate = m.sb("gate", [P, TB + 2])
        gate_s = m.sb("gate_s", [P, 8, 6])
        c = [m.sb(f"c{n}", [P, BANK]) for n in range(2)]
        u = [m.sb(f"u{n}", [P, BANK]) for n in range(2)]
        carry = m.sb("carry", [P, NJ, 2])
        state = m.sb("state", [P, NJ, 16])
        last_rows = m.sb("last_rows", [P, NJ, 18])
        acc = [m.bank(f"acc{n}") for n in range(4)]
        ps_sum = m.bank("ps_sum")
        ps_t = [m.bank(f"ps_t{n}") for n in range(2)]
        state_raw = h[0:16, :, :].rearrange("p k t -> p (k t)")[:, 0:NJ * P]
        out_rows = mix[0:18, :, :].rearrange("p k t -> p (k t)")[:, 0:NJ * P]
        y = [c[0], c[1], u[0], u[1]]

        raw_loaded = [m.sem(f"raw_loaded{n}") for n in range(4)]
        hi_split, lo_split, slab_done, acc_free = (m.sem(n) for n in ("hi_split", "lo_split", "slab_done", "acc_free"))
        h_loaded, mix_loaded, p_loaded, rs_loaded, st_loaded, st_turned, st_ready, carry_zero = (
            m.sem(n) for n in ("h_loaded", "mix_loaded", "p_loaded", "rs_loaded", "st_loaded", "st_turned", "st_ready", "carry_zero"))
        mix_scaled, mix_hi, mix_lo = (m.sem(n) for n in ("mix_scaled", "mix_hi", "mix_lo"))
        sq_done, s_added, xhi_done, xlo_done, sum_ready, rms_done, rs_done = (
            m.sem(n) for n in ("sq_done", "s_added", "xhi_done", "xlo_done", "sum_ready", "rms_done", "rs_done"))
        conv_step, gelu_done, f_ready, fhi_done, flo_done = (
            m.sem(n) for n in ("conv_step", "gelu_done", "f_ready", "fhi_done", "flo_done"))
        p_hi, p_lo, sig_done, h_ready, y_ready, y_turned, y_copied = (
            m.sem(n) for n in ("p_hi", "p_lo", "sig_done", "h_ready", "y_ready", "y_turned", "y_copied"))
        y_stored = [m.sem(f"y_stored{n}") for n in range(4)]
        rows_turned, rows_copied, rows_stored = m.sem("rows_turned"), m.sem("rows_copied"), m.sem("rows_stored")

        w_out, w_up, w_down, w_gate, w_proj = (
            T[n][0].rearrange("(k p) n -> p k n", p=P) for n in ("w_out", "w_up", "w_down", "w_ple_gate", "w_ple_proj"))
        XT, PT, MIXT = (D[n].rearrange("(k p) t -> p k t", p=P) for n in ("XT", "PT", "MIXT"))

        def col(n, count=1):
            return keep["cols"][:, bass.ds(n, count)]

        STEPS, STEPS_LAST = 5, 11

        with nc.Block() as block:

            @block.sync
            def _(sp):
                def slab(q4, k, src, shape=None):
                    g = 4 * q4 + k + 1
                    if not isinstance(g, int):
                        g = sp.snap(g)
                    wait_apart(sp, lo_split, g)
                    n = src.shape[1] * src.shape[2]
                    sp.dma_start(raw[k % 4][:, 0:n].rearrange("p (k n) -> p k n", k=src.shape[1]), src)\
                        .then_inc(raw_loaded[k % 4], 16)

                def out_loads(b):
                    q4 = b * (SLABS // 4)
                    for k in range(8):
                        slab(q4, O_AT + k, w_out[:, :, k * P:(k + 1) * P])

                def other_loads(b):
                    q4 = b * (SLABS // 4)
                    with sp.Fori(0, NJ // 2) as jj:
                        for e in range(2):
                            for part in range(2):
                                n = sp.snap(part * NJ * P + (2 * jj + e) * P)
                                slab(q4 + jj, U_AT + 2 * e + part, w_up[:, :, bass.ds(n, P)])
                    for mt in range(8):
                        for r in range(3):
                            kt = (8 * r, min(8 * r + 8, NJ))
                            slab(q4, D_AT + 3 * mt + r, w_down[:, kt[0]:kt[1], mt * P:(mt + 1) * P])
                    for q in range(4):
                        for e in range(2):
                            slab(q4, P_AT + 3 * q + e, w_gate[:, :, (2 * q + e) * P:(2 * q + e + 1) * P])
                        slab(q4, P_AT + 3 * q + 2, w_proj[:, :, 2 * q * P:2 * (q + 1) * P])

                sp.dma_start(state_raw, T["state_conv"][0].rearrange("b w f -> (b w) f")).then_inc(st_loaded, 16)
                out_loads(0)
                with sp.Fori(0, NB - 1) as b:
                    other_loads(b)
                    out_loads(b + 1)
                other_loads(NB - 1)
                sp.wait_ge(rows_copied, 6)
                sp.dma_start(T["conv_prompt"][0, 0], out_rows[0:2, :]).then_inc(rows_stored, 16)
                sp.dma_start(T["conv_sample"][0].rearrange("b w f -> (b w) f"), out_rows[2:18, :]).then_inc(rows_stored, 16)
                sp.wait_ge(rows_stored, 32)

            @block.gpsimd
            def _(pool):
                pool.sem_inc(lo_split, 4)
                nc.gpsimd.memset(carry[:, :, :], 0.0).then_inc(carry_zero, 1)
                with pool.Fori(0, NB * SLABS // 4) as q4:
                    for k in range(4):
                        pool.wait_ge(hi_split, 4 * q4 + k + 1)
                        nc.gpsimd.tensor_tensor(w_lo[k][:, :], raw[k][:, :], f32(w_hi[k][:, :]), ALU.subtract).then_inc(lo_split, 1)

            @block.tensor
            def _(pe):
                def tile_of(w, k, width=P):
                    return w[:, k * width:(k + 1) * width]

                def take(q4, k, units):
                    pe.wait_ge(lo_split, 4 * q4 + k + 5)
                    pe.wait_ge(acc_free, units)

                def mean_square(value):
                    pe.wait_ge(s_added, value)
                    nc.tensor.matmul(ps_sum[:, 0:TB], ones[0][:, :], ssum[:, :], start=True, stop=True).then_inc(sum_ready, 1)

                ones = [keep["mean1024"]]

                def product(q4, k, unit, mov_hi, mov_lo, order=range(8), ready=None):
                    for i, kt in enumerate(order):
                        if ready:
                            pe.wait_ge(ready[0], ready[1] + i + 1)
                        last = split_product(nc, acc[unit % 4][:, 0:TB], tile_of(w_hi[k % 4], kt), tile_of(w_lo[k % 4], kt),
                                             mov_hi[:, kt, :], mov_lo[:, kt, :], i == 0, i == 7)
                    last.then_inc(slab_done, 1)

                def out_products(b, behind):
                    q4, u0 = b * (SLABS // 4), b * UNITS
                    for mt in range(8):
                        if mt == 4 and behind:
                            turn_out(b - 1)
                        take(q4, O_AT + mt, u0 + OU + mt + 1)
                        product(q4, O_AT + mt, OU + mt, f_hi[:, MIX_AT:MIX_AT + 8, :], f_lo[:, MIX_AT:MIX_AT + 8, :], MIX_ORDER,
                                (mix_lo, 8 * b) if mt == 0 else None)
                        if mt == 0 and behind:
                            mean_square(21 * b)

                def turn_out(b):
                    for tt in range(4):
                        w = P if tt < 3 else 32
                        for half in range(2):
                            n = 2 * tt + half
                            pe.wait_ge(y_ready, 8 * b + 4 * half + 4)
                            pe.wait_ge(y_copied, 8 * b + n + 1)
                            for k in range(4):
                                done = nc.tensor.transpose(ps_t[half][0:w, k * P:(k + 1) * P],
                                                           h[:, 4 * half + k, tt * P:tt * P + w], keep["ident"][:, :])
                            done.then_inc(y_turned, 1)

                def other_products(b):
                    q4, u0 = b * (SLABS // 4), b * UNITS

                    def up_pair(q4, u, first=False):
                        for n in range(4):
                            take(q4, U_AT + n, u + UU + n + 1)
                            product(q4, U_AT + n, UU + n, x_hi, x_lo, ready=(xlo_done, 16 * b) if first and n == 0 else None)
                            if first and n == 0:
                                mean_square(21 * b + 7)

                    up_pair(q4, u0, True)
                    with pe.Fori(1, NJ // 2) as jj:
                        up_pair(q4 + jj, u0 + 4 * jj)
                    for mt in range(8):
                        for r in range(3):
                            if r == 0:
                                take(q4, D_AT + 3 * mt, u0 + DU + mt + 1)
                            else:
                                pe.wait_ge(lo_split, 4 * q4 + D_AT + 3 * mt + r + 5)
                            if mt == 0:
                                pe.wait_ge(flo_done, NJ * b + (NJ - 1 if r < 2 else NJ))
                            for kt in range(8 * r, min(8 * r + 8, NJ)):
                                k = (D_AT + 3 * mt + r) % 4
                                done = split_product(nc, acc[(DU + mt) % 4][:, 0:TB], tile_of(w_hi[k], kt % 8), tile_of(w_lo[k], kt % 8),
                                                     f_hi[:, kt, :], f_lo[:, kt, :], kt == 0, kt == NJ - 1)
                            done.then_inc(slab_done, 1)
                    for q in range(4):
                        for e in range(2):
                            take(q4, P_AT + 3 * q + e, u0 + PU + 4 * q + e + 1)
                            product(q4, P_AT + 3 * q + e, PU + 4 * q + e, x_hi, x_lo, ready=(xlo_done, 16 * b + 8) if q + e == 0 else None)
                            if q + e == 0:
                                mean_square(21 * b + 14)
                        take(q4, P_AT + 3 * q + 2, u0 + PU + 4 * q + 4)
                        if q == 0:
                            pe.wait_ge(p_lo, b + 1)
                        k = (P_AT + 3 * q + 2) % 4
                        for e in range(2):
                            for kt in range(2):
                                at = kt * 2 * P + e * P
                                done = split_product(nc, acc[(PU + 4 * q + 2 + e) % 4][:, 0:TB], w_hi[k][:, at:at + P], w_lo[k][:, at:at + P],
                                                     f_hi[:, kt, :], f_lo[:, kt, :], kt == 0, kt == 1)
                        done.then_inc(slab_done, 1)

                pe.sem_inc(slab_done, 2)
                pe.sem_inc(y_turned, 1)
                pe.wait_ge(st_loaded, 16)
                for j in range(NJ):
                    done = nc.tensor.transpose(ps_t[0][:, 16 * j:16 * j + 16], state_raw[:, j * P:(j + 1) * P], keep["ident"][0:16, 0:16])
                done.then_inc(st_turned, 1)
                out_products(0, False)
                with pe.Fori(0, NB - 1) as b:
                    other_products(b)
                    out_products(b + 1, True)
                other_products(NB - 1)
                mean_square(21 * NB)
                turn_out(NB - 1)
                for n in range(6):
                    if n < 2:
                        pe.wait_ge(y_copied, 8 * NB + n + 1)
                    else:
                        pe.wait_ge(rows_copied, n - 1)
                    for j in range(4 * n, min(4 * n + 4, NJ)):
                        done = nc.tensor.transpose(ps_t[n % 2][0:18, (j % 4) * P:(j % 4 + 1) * P], last_rows[:, j, :], keep["ident"][:, :])
                    done.then_inc(rows_turned, 1)

            @block.scalar
            def _(act):
                def square(b, norm, mt, ready, value):
                    act.wait_ge(ready, value)
                    if mt >= 2:
                        act.wait_ge(s_added, 21 * b + 7 * norm + mt - 1)
                    nc.scalar.activation((ssum if mt == 0 else sq)[:, :], h[:, mt, :], ACT.Square).then_inc(sq_done, 1)

                def root(b, norm):
                    act.wait_ge(sum_ready, 3 * b + norm + 1)
                    nc.scalar.activation(rs[:, :], ps_sum[:, 0:TB], ACT.Sqrt, bias=keep["eps"][:, :]).then_inc(rms_done, 1)

                def residual(b, norm, mt, unit, gain):
                    square(b, norm, mt, acc_free, UNITS * b + unit + mt + 5)
                    nc.scalar.activation(x_hi[:, mt, :], h[:, mt, :], ACT.Copy, scale=col(gain + mt)).then_inc(xhi_done, 1)

                def mix_high(b, i):
                    kt = MIX_ORDER[i]
                    if i == 0:
                        act.wait_ge(mix_loaded, 16 * b + 16)
                    if kt < 4:
                        act.wait_ge(mix_scaled, 4 * b + kt + 1)
                        nc.scalar.activation(f_hi[:, MIX_AT + kt, :], mix[:, kt, :], ACT.Copy).then_inc(mix_hi, 1)
                    else:
                        nc.scalar.activation(f_hi[:, MIX_AT + kt, :], mix[:, kt, :], ACT.Copy, scale=col(G_OUT + kt)).then_inc(mix_hi, 1)

                def load_mix(at):
                    act.dma_start(mix[:, :, :], MIXT[:, :, bass.ds(at, TB)]).then_inc(mix_loaded, 16)
                    act.dma_start(rs_sb[:, :], D["RSB"][:, bass.ds(at, TB)]).then_inc(rs_loaded, 16)

                def load_x(b, at):
                    wait_apart(act, mix_lo, 8 * b + 8)
                    act.dma_start(mix[:, :, :], XT[:, :, bass.ds(at, TB)]).then_inc(h_loaded, 16)
                    act.dma_start(p_raw[:, :, :], PT[:, :, bass.ds(at, TB)]).then_inc(p_loaded, 16)

                def way_out(b, at, last):
                    for tt in range(4):
                        w = P if tt < 3 else 32
                        for half in range(2):
                            n = 2 * tt + half
                            act.wait_ge(y_turned, 8 * b + n + 2)
                            act.wait_ge(y_stored[n % 4], 32 * b + 16 * (n // 4) + 16)
                            nc.scalar.activation(y[n % 4][0:w, :], ps_t[half][0:w, :], ACT.Copy).then_inc(y_copied, 1)
                            act.wait_ge(y_copied, 8 * b + n + 3)
                            cols = slice(half * BANK, (half + 1) * BANK)
                            dst = (T["y_sample"].rearrange("b t d -> (b t) d")[:, cols] if last and tt == 3 else
                                   T["y_prompt"][0][bass.ds(at + tt * P, w), cols])
                            act.dma_start(dst, y[n % 4][0:w, :]).then_inc(y_stored[n % 4], 16)

                def out_acts(b, behind_at):
                    if behind_at is not None:
                        root(b - 1, 2)
                        way_out(b - 1, behind_at, False)
                    for mt in range(8):
                        residual(b, 0, mt, OU, G_FFN)

                def other_acts(b, last):
                    if not last:
                        nxt = act.snap(b * TB + TB)
                        load_mix(nxt)
                    root(b, 0)
                    steps = (STEPS * (NB - 1) * NJ) if last else STEPS * NJ * b
                    per = STEPS_LAST if last else STEPS

                    with act.Fori(0, NJ // 2) as jj:
                        for e in range(2):
                            j = 2 * jj + e
                            wait_apart(act, conv_step, steps + per * (j + 1))
                            nc.scalar.activation(c[e][:, 0:TB], c[e][:, 0:TB], ACT.Gelu_apprx_tanh, bias=col(CONV_B0 + j)).then_inc(gelu_done, 1)
                            wait_apart(act, f_ready, NJ * b + j + 1)
                            nc.scalar.activation(f_hi[:, bass.ds(j, 1), :], u[e][:, 0:TB].unsqueeze(1), ACT.Copy).then_inc(fhi_done, 1)
                    for mt in range(8):
                        residual(b, 1, mt, DU, G_PLE)
                    root(b, 1)
                    for q in range(4):
                        for e in range(2):
                            if q < 2 and not last:
                                mix_high(b + 1, 4 * q + 2 * e)
                                mix_high(b + 1, 4 * q + 2 * e + 1)
                            act.wait_ge(acc_free, UNITS * b + PU + 4 * q + e + 5)
                            nc.scalar.activation(c[e][:, 0:TB], c[e][:, 0:TB], ACT.Sigmoid).then_inc(sig_done, 1)
                        if q == 2 and not last:
                            load_x(b + 1, nxt)
                        for e in range(2):
                            square(b, 2, 2 * q + e, h_ready, 8 * b + 2 * q + e + 1)

                for n in range(4):
                    act.sem_inc(y_stored[n], 16)
                act.sem_inc(y_copied, 2)
                load_mix(0)
                for i in range(8):
                    mix_high(0, i)
                load_x(0, 0)
                out_acts(0, None)
                with act.Fori(0, NB - 1) as b:
                    at = act.snap(b * TB)
                    other_acts(b, False)
                    out_acts(b + 1, at)
                other_acts(NB - 1, True)
                root(NB - 1, 2)
                way_out(NB - 1, (NB - 1) * TB, True)
                for n in range(6):
                    w = min(4, NJ - 4 * n) * P
                    act.wait_ge(rows_turned, n + 1)
                    nc.scalar.activation(out_rows[:, n * BANK:n * BANK + w], ps_t[n % 2][0:18, 0:w], ACT.Copy).then_inc(rows_copied, 1)
                for n in range(4):
                    act.wait_ge(y_stored[n], 32 * NB + 16)

            @block.vector
            def _(dve):
                def split(q4, k, start=False):
                    dve.wait_ge(raw_loaded[k % 4], 16 * (q4 + k // 4 + 1))
                    if not start:
                        dve.wait_ge(slab_done, 4 * q4 + k - 1)
                    nc.vector.tensor_copy(w_hi[k % 4][:, :], raw[k % 4][:, :]).then_inc(hi_split, 1)

                def done(q4, k):
                    dve.wait_ge(slab_done, 4 * q4 + k + 3)

                def mult(out, a, b):
                    return nc.vector.tensor_tensor(out, a, b, ALU.mult)

                def copy(out, a):
                    return nc.vector.tensor_scalar(out, a, 1.0, None, ALU.mult)

                def add_square(b, norm, mt):
                    if mt:
                        dve.wait_ge(sq_done, 24 * b + 8 * norm + mt + 1)
                        if mt >= 2:
                            dve.wait_ge(s_added, 21 * b + 7 * norm + mt - 1)
                        nc.vector.tensor_tensor(ssum[:, :], ssum[:, :], sq[:, :], ALU.add).then_inc(s_added, 1)

                def residual(b, norm, mt, unit, gain):
                    if norm == 0 and mt == 0:
                        dve.wait_ge(y_turned, 8 * b + 1)
                    nc.vector.tensor_tensor(h[:, mt, :], acc[(unit + mt) % 4][:, 0:TB], (h if norm else mix)[:, mt, :], ALU.add)\
                        .then_inc(acc_free, 1)
                    dve.wait_ge(xhi_done, 16 * b + 8 * norm + mt + 1)
                    nc.vector.scalar_tensor_tensor(x_lo[:, mt, :], h[:, mt, :], col(gain + mt), f32(x_hi[:, mt, :]),
                                                   ALU.mult, ALU.subtract).then_inc(xlo_done, 1)
                    add_square(b, norm, mt)

                def inverse(b, norm):
                    dve.wait_ge(rms_done, 3 * b + norm + 1)
                    nc.vector.reciprocal(rs[:, :], rs[:, :]).then_inc(rs_done, 1)
                    dve.wait_ge(rs_done, 3 * b + norm + 1)

                def mix_parts(b, i):
                    if i == 0:
                        dve.wait_ge(mix_loaded, 16 * b + 16)
                        dve.wait_ge(rs_loaded, 16 * b + 16)
                    kt = i % 4
                    if i < 4:
                        nc.vector.scalar_tensor_tensor(mix[:, kt, :], mix[:, kt, :], col(G_OUT + kt), rs_sb[:, :],
                                                       ALU.mult, ALU.mult).then_inc(mix_scaled, 1)
                        dve.wait_ge(mix_hi, 8 * b + kt + 1)
                        nc.vector.scalar_tensor_tensor(f_lo[:, MIX_AT + 4 + kt, :], mix[:, 4 + kt, :], col(G_OUT + 4 + kt),
                                                       f32(f_hi[:, MIX_AT + 4 + kt, :]), ALU.mult, ALU.subtract).then_inc(mix_lo, 1)
                    else:
                        dve.wait_ge(mix_hi, 8 * b + kt + 5)
                        nc.vector.tensor_tensor(f_lo[:, MIX_AT + kt, :], mix[:, kt, :], f32(f_hi[:, MIX_AT + kt, :]), ALU.subtract)\
                            .then_inc(mix_lo, 1)

                def normalise(b, mt):
                    nc.vector.scalar_tensor_tensor(h[:, mt, :], h[:, mt, :], col(G_FIN + mt), rs[:, :], ALU.mult, ALU.mult)\
                        .then_inc(y_ready, 1)

                def out_steps(b, behind):
                    q4 = b * (SLABS // 4)
                    if behind:
                        split(q4, O_AT + 2)
                        split(q4, O_AT + 3)
                        inverse(b - 1, 2)
                        for mt in range(8):
                            normalise(b - 1, mt)
                            if mt % 4 == 3:
                                split(q4, O_AT + 4 + mt // 4)
                    for mt in range(8):
                        if mt == 0:
                            dve.wait_ge(h_loaded, 16 * b + 16)
                        if not behind:
                            split(q4, O_AT + mt + 2)
                        done(q4, O_AT + mt)
                        residual(b, 0, mt, OU, G_FFN)
                        if behind and mt < 4:
                            split(q4, O_AT + mt + 6)

                def other_steps(b, last):
                    q4 = b * (SLABS // 4)
                    steps = (STEPS * (NB - 1) * NJ) if last else STEPS * NJ * b
                    per = STEPS_LAST if last else STEPS

                    def conv(out, src, width, base, start):
                        win = (lambda n: src[:, n:n + width]) if width != 4 else (lambda n: src[:, :, n:n + 4])
                        dve.wait_ge(conv_step, base + start)
                        nc.vector.tensor_scalar(out, win(0), col(CONV_W0 + jcol[0]), None, ALU.mult).then_inc(conv_step, 1)
                        for tap in (1, 2):
                            dve.wait_ge(conv_step, base + start + tap)
                            nc.vector.scalar_tensor_tensor(out, win(tap), col(CONV_W0 + NJ * tap + jcol[0]), out,
                                                           ALU.mult, ALU.add).then_inc(conv_step, 1)

                    jcol = [None]

                    def up_pair(q4, jj, first=False):
                        for e in range(2):
                            j = 2 * jj + e
                            jcol[0] = j
                            base = steps + per * j
                            split(q4, U_AT + 2 * e + 2)
                            if first and e == 0:
                                inverse(b, 0)
                                for n in range(4):
                                    dve.wait_ge(y_stored[n], 32 * b + 16)
                            done(q4, U_AT + 2 * e)
                            copy(gate[:, 0:2], carry[:, bass.ds(j, 1), :].rearrange("p a t -> p (a t)")).then_inc(conv_step, 1)
                            g_acc = acc[(UU + 2 * e) % 4]
                            if not last:
                                mult(gate[:, 2:TB + 2], g_acc[:, 0:TB], rs[:, :]).then_inc(acc_free, 1)
                                dve.wait_ge(acc_free, UNITS * b + UU + 2 * j + 5)
                                copy(carry[:, bass.ds(j, 1), :].rearrange("p a t -> p (a t)"), gate[:, TB:TB + 2])\
                                    .then_inc(conv_step, 1)
                                conv(c[e][:, 0:TB], gate, TB, base, 2)
                            else:
                                tp = TB - 32
                                copy(gate_s[:, :, 0:2], state[:, bass.ds(j, 1), :].rearrange("p a (b w) -> p (a b) w", w=2))\
                                    .then_inc(conv_step, 1)
                                mult(gate[:, 2:tp + 2], g_acc[:, 0:tp], rs[:, 0:tp]).then_inc(conv_step, 1)
                                mult(gate_s[:, :, 2:6], g_acc[:, tp:TB].rearrange("p (b t) -> p b t", b=8),
                                     rs[:, tp:TB].rearrange("p (b t) -> p b t", b=8)).then_inc(acc_free, 1)
                                dve.wait_ge(conv_step, base + 3)
                                dve.wait_ge(acc_free, UNITS * b + UU + 2 * j + 5)
                                copy(last_rows[:, bass.ds(j, 1), 0:2].rearrange("p a t -> p (a t)"), gate[:, tp:tp + 2])\
                                    .then_inc(conv_step, 1)
                                copy(last_rows[:, bass.ds(j, 1), 2:18].rearrange("p a (b w) -> p (a b) w", w=2),
                                                      gate_s[:, :, 4:6]).then_inc(conv_step, 1)
                                conv(c[e][:, 0:tp], gate, tp, base, 5)
                                conv(c[e][:, tp:TB].rearrange("p (b t) -> p b t", b=8), gate_s, 4, base, 8)
                            split(q4, U_AT + 2 * e + 3)
                            done(q4, U_AT + 2 * e + 1)
                            mult(u[e][:, 0:TB], acc[(UU + 2 * e + 1) % 4][:, 0:TB], rs[:, :]).then_inc(acc_free, 1)
                            dve.wait_ge(acc_free, UNITS * b + UU + 2 * j + 6)
                            dve.wait_ge(gelu_done, NJ * b + j + 1)
                            mult(u[e][:, 0:TB], u[e][:, 0:TB], c[e][:, 0:TB]).then_inc(f_ready, 1)
                            dve.wait_ge(fhi_done, NJ * b + j + 1)
                            nc.vector.tensor_tensor(f_lo[:, bass.ds(j, 1), :], u[e][:, 0:TB].unsqueeze(1), f32(f_hi[:, bass.ds(j, 1), :]),
                                                    ALU.subtract).then_inc(flo_done, 1)

                    up_pair(q4, 0, True)
                    with dve.Fori(1, NJ // 2) as jj:
                        up_pair(q4 + jj, jj)
                    for mt in range(8):
                        for r in range(3):
                            split(q4, D_AT + 3 * mt + r + 2)
                        done(q4, D_AT + 3 * mt + 2)
                        residual(b, 1, mt, DU, G_PLE)
                        if mt == 7:
                            dve.wait_ge(p_loaded, 16 * b + 16)
                            nc.vector.tensor_copy(f_hi[:, 0:2, :], p_raw[:, :, :]).then_inc(p_hi, 1)
                            dve.wait_ge(p_hi, b + 1)
                            nc.vector.tensor_tensor(f_lo[:, 0:2, :], p_raw[:, :, :], f32(f_hi[:, 0:2, :]), ALU.subtract).then_inc(p_lo, 1)
                    for q in range(4):
                        for e in range(2):
                            if not (last and 3 * q + e + 2 >= 12):
                                split(q4, P_AT + 3 * q + e + 2)
                            if q + e == 0:
                                inverse(b, 1)
                            done(q4, P_AT + 3 * q + e)
                            mult(c[e][:, 0:TB], acc[(PU + 4 * q + e) % 4][:, 0:TB], rs[:, :]).then_inc(acc_free, 1)
                            if q < 2 and not last:
                                mix_parts(b + 1, 4 * q + 2 * e)
                                mix_parts(b + 1, 4 * q + 2 * e + 1)
                        if not (last and 3 * q + 4 >= 12):
                            split(q4, P_AT + 3 * q + 4)
                        done(q4, P_AT + 3 * q + 2)
                        for e in range(2):
                            mt = 2 * q + e
                            dve.wait_ge(sig_done, 8 * b + mt + 1)
                            mult(u[e][:, 0:TB], c[e][:, 0:TB], acc[(PU + 4 * q + 2 + e) % 4][:, 0:TB]).then_inc(acc_free, 1)
                            dve.wait_ge(acc_free, UNITS * b + PU + 4 * q + 2 + e + 5)
                            nc.vector.tensor_tensor(h[:, mt, :], h[:, mt, :], u[e][:, 0:TB], ALU.add).then_inc(h_ready, 1)
                            add_square(b, 2, mt)

                dve.sem_inc(acc_free, 4)
                dve.wait_ge(carry_zero, 1)
                dve.wait_ge(st_turned, 1)
                nc.vector.tensor_copy(state[:, :, :].rearrange("p j t -> p (j t)"), ps_t[0][:, 0:16 * NJ]).then_inc(st_ready, 1)
                for k in range(2):
                    split(0, k, True)
                for i in range(8):
                    mix_parts(0, i)
                out_steps(0, False)
                with dve.Fori(0, NB - 1) as b:
                    other_steps(b, False)
                    out_steps(b + 1, True)
                other_steps(NB - 1, True)
                inverse(NB - 1, 2)
                for mt in range(8):
                    normalise(NB - 1, mt)


def program(nc, T):
    D = {n: nc.dram_tensor(n, s, F32, kind="Internal").ap() for n, s in
         (("XT", (1024, 2080)), ("PT", (256, 2080)), ("MIXT", (1024, 2080)), ("QT", (512, 2048)), ("KT", (512, 2048)),
          ("RSB", (P, 2080)))}
    with ExitStack() as ctx:
        m = Alloc(nc, ctx, "keep")
        keep = {
            "ident": m.sb("ident", [P, P]), "mean1024": m.sb("mean1024", [P, P]), "mean512": m.sb("mean512", [P, P]),
            "eps": m.sb("eps", [P, 1]), "cols": m.sb("cols", [P, P]), "rs": m.sb("rs", [P, 17]),
            "page_table": m.sb("page_table", [1, P], I32), "sb_bias": m.sb("sb_bias", [P, 8]),
            "qT_s": m.sb("qT_s", [P, 4, 32]), "kT_s": m.sb("kT_s", [P, 4, 32]),
        }
        constants(nc, keep, T)
        project_mlp(nc, keep, T, D)
        project_qk(nc, keep, T, D)
        attend_prompt(nc, keep, T, D)
        attend_sample(nc, keep, T, D)
        finish_tokens(nc, keep, T, D)


_OUTS = (
    ("y_prompt", (1, 2048, 1024)), ("y_sample", (8, 4, 1024)),
    ("k_prompt", (1, 1, 2048, 8, 64)), ("v_prompt", (1, 1, 2048, 8, 64)),
    ("k_sample", (1, 8, 4, 8, 64)), ("v_sample", (1, 8, 4, 8, 64)),
    ("conv_prompt", (1, 1, 2, 2816)), ("conv_sample", (1, 8, 2, 2816)), ("mlp_v_sample", (1, 8, 4, 512)),
)


def kernel(**inputs):
    import numpy as np
    import concourse.bacc as bacc
    from concourse.bass_utils import run_bass_kernel_spmd

    nc = bacc.Bacc("TRN2", target_bir_lowering=False, num_devices=1)
    arrays, T = {}, {}
    for name, value in inputs.items():
        a = np.ascontiguousarray(value)
        arrays[f"in_{name}_dram"] = a
        T[name] = nc.dram_tensor(f"in_{name}_dram", a.shape, mybir.dt.from_np(a.dtype), kind="ExternalInput").ap()
    for name, shape in _OUTS:
        T[name] = nc.dram_tensor(f"out_{name}_dram", shape, F32, kind="ExternalOutput").ap()
    program(nc, T)
    got = run_bass_kernel_spmd(nc, [arrays], core_ids=[0]).results[0]
    return tuple(got[f"out_{name}_dram"] for name, _ in _OUTS)
```
